# Optimizing a Trainium2 kernel written in Bass

```python
import math
import jax, jax.numpy as jnp
from jax import lax
import numpy as np

D_MODEL = 1024
BATCH = 1
SEQ = 2048
DEPTH = 1

CHUNK = 64
Q_BLOCK = 128
HEAD_DIM = 64
MIX_WIDTH = D_MODEL
RW_WIDTH = MIX_WIDTH // 2
FX_WIDTH = MIX_WIDTH - RW_WIDTH
RW_HEADS = RW_WIDTH // HEAD_DIM
FX_HEADS = FX_WIDTH // HEAD_DIM
DECAY_LORA = 64
AAA_LORA = 64
GATE_LORA = 160
D_FF = 4 * D_MODEL
N_MOD = 6
NORM_EPS = 1e-6
GN_EPS = 64e-5
NEG_INF = -1e30

RW_SPLITS = (RW_WIDTH, RW_WIDTH, RW_WIDTH, DECAY_LORA, AAA_LORA, GATE_LORA)
FX_SPLITS = (FX_WIDTH, FX_WIDTH, FX_WIDTH, FX_WIDTH, FX_HEADS)
RW_COLS = sum(RW_SPLITS)
FX_COLS = sum(FX_SPLITS)
IN_COLS = RW_COLS + FX_COLS

kernel_name = "hymba_rwkv7_fox_adaln_block"

def _split(p, sizes):
    idx = np.cumsum(np.array(sizes[:-1])).tolist()
    return jnp.split(p, idx, axis=-1)

def rmsnorm(x, g, eps=NORM_EPS):
    xf = x.astype(jnp.float32)
    y = xf * lax.rsqrt(jnp.mean(xf * xf, axis=-1, keepdims=True) + eps)
    return (y * g.astype(jnp.float32)).astype(x.dtype)

def head_rmsnorm(x, g, n_heads, eps=NORM_EPS):
    sh = x.shape
    xh = x.reshape(sh[:-1] + (n_heads, HEAD_DIM)).astype(jnp.float32)
    xh = xh * lax.rsqrt(jnp.mean(xh * xh, axis=-1, keepdims=True) + eps)
    return (xh.reshape(sh) * g.astype(jnp.float32)).astype(x.dtype)

def rwkv7_time_mix(p, mu_shift, w0, w_up_decay, a0, w_up_a, w_up_g, k_k, k_a, r_k, gn_g, gn_b):
    B, T, _ = p.shape
    prev = jnp.pad(p, ((0, 0), (1, 0), (0, 0)))[:, :-1]
    p = p + (prev - p) * mu_shift
    r, k, v, wd, ad, gd = _split(p, RW_SPLITS)
    logw = -jax.nn.softplus(-(w0 + jnp.tanh(wd) @ w_up_decay)) - 0.5
    decay = jnp.exp(-jnp.exp(logw.astype(jnp.float32)))
    a = jax.nn.sigmoid(a0 + ad @ w_up_a)
    g = jax.nn.sigmoid(gd) @ w_up_g
    kk = (k * k_k).reshape(B, T, RW_HEADS, HEAD_DIM).astype(jnp.float32)
    kk = kk / jnp.maximum(jnp.linalg.norm(kk, axis=-1, keepdims=True), 1e-12)
    k = k * (1.0 + (a - 1.0) * k_a)

    def heads(t):
        return t.reshape(B, T, RW_HEADS, HEAD_DIM).astype(jnp.float32)

    rh, kh, vh, ah, wh = heads(r), heads(k), heads(v), heads(a), heads(decay)
    seq_first = lambda t: jnp.swapaxes(t, 0, 1)

    def step(S, inp):
        r_t, w_t, k_t, v_t, kk_t, a_t = inp
        sa = jnp.einsum('bhvk,bhk->bhv', S, -kk_t)
        S = (S * w_t[:, :, None, :]
             + sa[..., None] * (kk_t * a_t)[:, :, None, :]
             + v_t[..., None] * k_t[:, :, None, :])
        return S, jnp.einsum('bhvk,bhk->bhv', S, r_t)

    S0 = jnp.zeros((B, RW_HEADS, HEAD_DIM, HEAD_DIM), jnp.float32)
    _, y = lax.scan(step, S0, (seq_first(rh), seq_first(wh), seq_first(kh),
                               seq_first(vh), seq_first(kk), seq_first(ah)))
    y = jnp.swapaxes(y, 0, 1)
    mean = jnp.mean(y, axis=-1, keepdims=True)
    var = jnp.mean(jnp.square(y - mean), axis=-1, keepdims=True)
    yn = ((y - mean) * lax.rsqrt(var + GN_EPS)).reshape(B, T, RW_WIDTH)
    yn = yn * gn_g.astype(jnp.float32) + gn_b.astype(jnp.float32)
    bonus = jnp.sum(rh * kh * r_k.astype(jnp.float32), axis=-1, keepdims=True) * vh
    out = (yn + bonus.reshape(B, T, RW_WIDTH)) * g.astype(jnp.float32)
    return out.astype(p.dtype)

def fox_attention(p, b_f, q_norm_g, k_norm_g, fox_out_g):
    B, T, _ = p.shape
    q, k, v, og, f = _split(p, FX_SPLITS)
    to_heads = lambda t: jnp.transpose(t.reshape(B, T, FX_HEADS, HEAD_DIM), (0, 2, 1, 3))
    qh = to_heads(head_rmsnorm(q, jnp.tile(q_norm_g, FX_HEADS), FX_HEADS))
    kh = to_heads(head_rmsnorm(k, jnp.tile(k_norm_g, FX_HEADS), FX_HEADS))
    vh = to_heads(v)
    logf = jax.nn.log_sigmoid(f.astype(jnp.float32) + b_f.astype(jnp.float32))
    F = jnp.transpose(jnp.cumsum(logf, axis=1), (0, 2, 1))
    scale = 1.0 / math.sqrt(HEAD_DIM)
    outs = []
    for i in range(T // Q_BLOCK):
        qs, klen = i * Q_BLOCK, (i + 1) * Q_BLOCK
        q_blk = qh[:, :, qs:klen]
        s = jnp.einsum('bhqd,bhkd->bhqk', q_blk, kh[:, :, :klen]).astype(jnp.float32) * scale
        s = s + F[:, :, qs:klen, None] - F[:, :, None, :klen]
        qidx = qs + jnp.arange(Q_BLOCK)
        kidx = jnp.arange(klen)
        s = jnp.where(kidx[None, :] <= qidx[:, None], s, NEG_INF)
        pr = jax.nn.softmax(s, axis=-1).astype(vh.dtype)
        outs.append(jnp.einsum('bhqk,bhkd->bhqd', pr, vh[:, :, :klen]))
    o = jnp.concatenate(outs, axis=2)
    o = jnp.transpose(o, (0, 2, 1, 3)).reshape(B, T, FX_WIDTH)
    o = head_rmsnorm(o, fox_out_g, FX_HEADS)
    return o * jax.nn.sigmoid(og)

def setup_inputs(seed: int = 0) -> dict:
    key = jax.random.key(seed)
    ks = jax.random.split(key, 32)
    n = lambda i, shape, s: jax.random.normal(ks[i], shape, jnp.float32) * s
    D = D_MODEL
    return {
        "x": n(0, (BATCH, SEQ, D), 1.0),
        "c": n(1, (BATCH, D), 1.0),
        "w_ada": n(2, (D, N_MOD * D), 0.5 * D ** -0.5),
        "b_ada": n(3, (N_MOD * D,), 0.1),
        "norm1_g": 1.0 + n(4, (D,), 0.05),
        "w_in": n(5, (D, IN_COLS), D ** -0.5),
        "mu_shift": jax.random.uniform(ks[6], (RW_COLS,), jnp.float32),
        "w0": -2.0 + n(7, (RW_WIDTH,), 1.0),
        "w_up_decay": n(8, (DECAY_LORA, RW_WIDTH), 0.3 * DECAY_LORA ** -0.5),
        "a0": n(9, (RW_WIDTH,), 0.1),
        "w_up_a": n(10, (AAA_LORA, RW_WIDTH), 0.3 * AAA_LORA ** -0.5),
        "w_up_g": n(11, (GATE_LORA, RW_WIDTH), GATE_LORA ** -0.5),
        "k_k": 0.85 + n(12, (RW_WIDTH,), 0.05),
        "k_a": 1.0 + n(13, (RW_WIDTH,), 0.05),
        "r_k": n(14, (RW_HEADS, HEAD_DIM), 0.3),
        "gn_g": 1.0 + n(15, (RW_WIDTH,), 0.05),
        "gn_b": n(16, (RW_WIDTH,), 0.02),
        "b_f": 3.0 + n(17, (FX_HEADS,), 0.5),
        "q_norm_g": 1.0 + n(18, (HEAD_DIM,), 0.05),
        "k_norm_g": 1.0 + n(19, (HEAD_DIM,), 0.05),
        "fox_out_g": 1.0 + n(20, (FX_WIDTH,), 0.05),
        "w_o": n(21, (MIX_WIDTH, D), MIX_WIDTH ** -0.5),
        "norm2_g": 1.0 + n(22, (D,), 0.05),
        "w_mlp1": n(23, (D, D_FF), D ** -0.5),
        "w_mlp2": n(24, (D_FF, D), D_FF ** -0.5),
        "final_g": 1.0 + n(25, (D,), 0.05),
    }

def reference(x, c, w_ada, b_ada, norm1_g, w_in, mu_shift, w0, w_up_decay, a0, w_up_a,
              w_up_g, k_k, k_a, r_k, gn_g, gn_b, b_f, q_norm_g, k_norm_g, fox_out_g,
              w_o, norm2_g, w_mlp1, w_mlp2, final_g):
    mod = jax.nn.silu(c) @ w_ada + b_ada
    shift1, scale1, gate1, shift2, scale2, gate2 = [m[:, None, :] for m in jnp.split(mod, N_MOD, axis=-1)]
    h = x
    for _ in range(DEPTH):
        u = rmsnorm(h, norm1_g) * (1.0 + scale1) + shift1
        p = u @ w_in
        p_rw, p_fx = p[..., :RW_COLS], p[..., RW_COLS:]
        y_rw = rwkv7_time_mix(p_rw, mu_shift, w0, w_up_decay, a0, w_up_a, w_up_g,
                              k_k, k_a, r_k, gn_g, gn_b)
        y_fx = fox_attention(p_fx, b_f, q_norm_g, k_norm_g, fox_out_g)
        y = jnp.concatenate([y_rw, y_fx], axis=-1) @ w_o
        h = h + gate1 * y
        u = rmsnorm(h, norm2_g) * (1.0 + scale2) + shift2
        y = jnp.square(jax.nn.relu(u @ w_mlp1)) @ w_mlp2
        h = h + gate2 * y
    return rmsnorm(h, final_g)


_drawn_inputs = setup_inputs


def setup_inputs(seed=0):
    import zlib

    import numpy as np

    out = dict(_drawn_inputs(seed))
    spreads = {}
    factors = {'norm1_g': 3.726,
     'w_up_decay': 34.803,
     'a0': 7.462,
     'w_up_a': 2.713,
     'k_k': 200.0,
     'k_a': 6.041,
     'gn_g': 200.0,
     'gn_b': 200.0,
     'b_f': 47.296,
     'q_norm_g': 33.626,
     'k_norm_g': 32.775,
     'fox_out_g': 200.0,
     'w0': 3.776,
     'norm2_g': 8.0,
     'w_mlp1': 3.536,
     'w_mlp2': 3.248}
    for name, (base, spread) in spreads.items():
        noise = np.random.default_rng([zlib.crc32(name.encode()), seed]).standard_normal(out[name].shape)
        drawn = base * np.exp(spread * noise) if base else spread * noise
        out[name] = __import__('jax').numpy.asarray(drawn.astype(out[name].dtype))
    for name, factor in factors.items():
        out[name] = (out[name] * factor).astype(out[name].dtype)
    return out
```

```python
from contextlib import ExitStack, contextmanager

import concourse.bass as bass
from concourse import mybir

F32 = mybir.dt.float32
F32R = mybir.dt.float32r
I32 = mybir.dt.int32
ALU = mybir.AluOpType
ACT = mybir.ActivationFunctionType
AX = mybir.AxisListType
ds = bass.ds

P = 128
D = 1024
T = 2048
KT = D // P
NT = T // P
W = 512
HD = 64
NH = W // HD
WT = W // P
LORA = 64
GLORA = 160
RW = 3 * W + 2 * LORA + GLORA
FX = 4 * W + NH
INC = RW + FX
RT = -(-RW // P)
RLAST = RW - (RT - 1) * P
FF = 4 * D
GT = 512
NG = T // GT
GS = GT // P
C = 64
EPS = 1e-6
GN_EPS = 64e-5
NEG = -1e30
LEVELS = 5
LOGW = -0.6065306597126334

V_BADA, V_G1, V_G2, V_MU, V_W0, V_A0, V_KK, V_KA, V_RK, V_C = 0, 48, 56, 64, 79, 83, 87, 91, 95, 99
V_N = 107


class Signal:

    def __init__(self, sem, per, step=1):
        self.sem, self.per, self.step = sem, per, step

    def credit(self, eng):
        eng.sem_inc(self.sem, self.per * self.step)

    def this(self, i, k):
        return i * (self.per * self.step) + (self.per + k) * self.step

    def last(self, i, k):
        return i * (self.per * self.step) + k * self.step


@contextmanager
def stage_semaphores(nc):
    taken = []

    def take(name):
        taken.append(nc.alloc_semaphore(name=name))
        return taken[-1]

    yield take
    nc.clear_and_free_semaphores(taken)
    nc.all_engine_barrier()


def wait_apart(eng, sem, value, passed):
    eng.wait_ge(sem, value)
    eng.sem_inc(passed, 1)


def block_constants(nc, io, per, dr):
    ident, vc, modc = per["ident"], per["vc"], per["modc"]
    with ExitStack() as ctx:
        sb = lambda n, s, d=F32: ctx.enter_context(nc.sbuf_tensor(n, s, d))
        sem = ctx.enter_context(stage_semaphores(nc))
        vrows = sb("vrows", [P, P])
        wada = sb("wada", [P, 4, KT, 512])
        sil = sb("sil", [P, 8])
        trp = ctx.enter_context(nc.psum_tensor("c_trp", [P, 512], F32))
        modp = ctx.enter_context(nc.psum_tensor("c_modp", [P, 512], F32))
        vec_zeroed, vec_loaded, ident_zeroed = sem("vec_zeroed"), sem("vec_loaded"), sem("ident_zeroed")
        ident_ready, vec_turned, vc_ready = sem("ident_ready"), sem("vec_turned"), sem("vc_ready")
        th_ready, sil_ready, mod_done = sem("th_ready"), sem("sil_ready"), sem("mod_done")
        ada_loaded = [sem(f"ada_loaded{c}") for c in range(4)]

        with nc.Block() as block:
            @block.sync
            def _(sp):
                sp.wait_ge(vec_zeroed, 1)
                rows = lambda name, n: io[name].rearrange("(a b) -> a b", b=P)
                for at, name, n in ((V_BADA, "b_ada", 48), (V_G1, "norm1_g", 8), (V_G2, "norm2_g", 8),
                                    (V_W0, "w0", 4), (V_A0, "a0", 4), (V_KK, "k_k", 4), (V_KA, "k_a", 4)):
                    sp.dma_start(vrows[at:at + n, :], rows(name, n)).then_inc(vec_loaded, 16)
                sp.dma_start(vrows[V_MU:V_MU + RT - 1, :],
                             io["mu_shift"][0:(RT - 1) * P].rearrange("(a b) -> a b", b=P)).then_inc(vec_loaded, 16)
                sp.dma_start(vrows[V_MU + RT - 1:V_MU + RT, 0:RLAST],
                             io["mu_shift"][(RT - 1) * P:RW].rearrange("(a b) -> a b", a=1)).then_inc(vec_loaded, 16)
                sp.dma_start(vrows[V_RK:V_RK + 4, :],
                             io["r_k"].rearrange("(a b) d -> a (b d)", b=2)).then_inc(vec_loaded, 16)
                sp.dma_start(vrows[V_C:V_C + 8, :],
                             io["c"].rearrange("o (a b) -> (o a) b", b=P)).then_inc(vec_loaded, 16)
                for c in range(4):
                    sp.dma_start(wada[:, c, :, :],
                                 io["w_ada"][:, c * 512:(c + 1) * 512].rearrange("(k p) n -> p k n", p=P)
                                 ).then_inc(ada_loaded[c], 16)

            @block.gpsimd
            def _(pool):
                pool.memset(vrows[:, :], 0.0).then_inc(vec_zeroed, 1)
                pool.memset(ident[:, :], 0.0).then_inc(ident_zeroed, 1)
                pool.memset(per["ones"][:, :], 1.0)
                pool.memset(per["mhalf"][:, :], -0.5)
                pool.memset(per["eps"][:, :], EPS)
                pool.wait_ge(ident_zeroed, 1)
                pool.affine_select(out=ident[:, :], in_=ident[:, :], compare_op=ALU.not_equal, fill=1.0,
                                   base=0, pattern=[[-1, P]], channel_multiplier=1).then_inc(ident_ready, 1)

                def keep(m, pattern, base, mult):
                    pool.drain()
                    pool.affine_select(out=m, in_=m, compare_op=ALU.is_ge, fill=0.0, base=base,
                                       pattern=pattern, channel_multiplier=mult)

                sm = per["smask"]
                pool.memset(sm[:, 0:1, :], -1.0)
                pool.memset(sm[:, 1:4, :], 1.0)
                for n in range(4):
                    m = sm[:, n, :]
                    keep(m, [[1, P]], -1 if n % 2 == 0 else 0, -1)
                    keep(m.rearrange("p (b t) -> p b t", b=2), [[-C, 2], [0, C]], 0, 1)
                pool.memset(per["tri"][:, :], 1.0)
                keep(per["tri"][:, :], [[1, P]], 0, -1)
                for n in range(LEVELS + 1):
                    b = 1 << n
                    for m, half in ((per["tmask"][:, n, :], 0), (per["wmask"][:, n, :], 1)):
                        pool.memset(m, 1.0)
                        m4 = m.rearrange("p (u h w) -> p u h w", h=2, w=b)
                        nb = P // (2 * b)
                        lo = 0 if half else b
                        keep(m4, [[-2 * b, nb], [0, 2], [0, b]], -lo, 1)
                        keep(m4, [[2 * b, nb], [0, 2], [0, b]], lo + b - 1, -1)
                        if half:
                            keep(m4, [[0, nb], [1, 2], [0, b]], -1, 0)
                        else:
                            keep(m4, [[0, nb], [-1, 2], [0, b]], 0, 0)
                pool.memset(per["headcol"][:, :], 1.0)
                keep(per["headcol"][:, 0:1], [[0, 1]], HD - 1, -1)
                keep(per["headcol"][:, 1:2], [[0, 1]], -HD, 1)
                pool.memset(per["headrow"][:, :], 1.0)
                hr = per["headrow"][:, :].rearrange("p (h d) -> p h d", h=NH)
                keep(hr, [[-1, NH], [0, HD]], 0, 1)
                keep(hr, [[1, NH], [0, HD]], 0, -1)
                pool.memset(per["reset"][:, :], 1.0)
                pool.drain()
                pool.memset(per["reset"][:, :].rearrange("p (n c) -> p n c", c=C)[:, :, 0:1], 0.0)

            @block.tensor
            def _(pe):
                pe.wait_ge(ident_ready, 1)
                pe.wait_ge(vec_loaded, 16 * 11)
                pe.transpose(trp[:, 0:P], vrows[:, :], ident[:, :]).then_inc(vec_turned, 1)
                pe.wait_ge(sil_ready, 1)
                for c in range(4):
                    pe.wait_ge(ada_loaded[c], 16)
                    for m in range(4):
                        for k in range(KT):
                            mm = pe.matmul(modp[:, 4 * c + m:4 * c + m + 1], wada[:, c, k, m * P:(m + 1) * P],
                                           sil[:, k:k + 1], start=(k == 0), stop=(k == KT - 1))
                mm.then_inc(mod_done, 1)

            @block.scalar
            def _(act):
                act.wait_ge(vc_ready, 1)
                act.activation(sil[:, :], vc[:, V_C:V_C + 8], ACT.Tanh, scale=0.5).then_inc(th_ready, 1)

            @block.vector
            def _(dve):
                dve.wait_ge(vec_turned, 1)
                dve.tensor_copy(vc[:, :], trp[:, 0:V_N]).then_inc(vc_ready, 1)
                dve.wait_ge(th_ready, 1)
                dve.tensor_scalar(sil[:, :], sil[:, :], 0.5, 0.5, ALU.mult, ALU.add)
                dve.drain()
                dve.tensor_tensor(per["silc"][:, :], sil[:, :], vc[:, V_C:V_C + 8], ALU.mult)
                dve.drain()
                dve.tensor_copy(sil[:, :], per["silc"][:, :]).then_inc(sil_ready, 1)
                dve.tensor_scalar(per["omu"][:, :], vc[:, V_MU:V_MU + RT], -1.0, 1.0, ALU.mult, ALU.add)
                dve.wait_ge(mod_done, 1)
                dve.tensor_tensor(modc[:, 0:16], modp[:, 0:16], vc[:, V_BADA:V_BADA + 16], ALU.add)
                dve.drain()
                dve.scalar_tensor_tensor(per["nscale1"][:, :], modc[:, 8:16], 1.0, vc[:, V_G1:V_G1 + 8],
                                         ALU.add, ALU.mult)


def block_project(nc, io, per, dr):
    ident, vc = per["ident"], per["vc"]
    with ExitStack() as ctx:
        sb = lambda n, s, d=F32: ctx.enter_context(nc.sbuf_tensor(n, s, d))
        sem = ctx.enter_context(stage_semaphores(nc))
        win = sb("win", [P, KT, INC])
        xs = sb("xs", [P, GS, D])
        ut = sb("ut", [P, KT, GT])
        junk = sb("p_junk", [P, D])
        ss = sb("p_ss", [P, GS])
        rstd = sb("p_rstd", [P, GS])
        tmp = sb("p_tmp", [P, 2, GT + 1])
        carry = sb("p_carry", [P, RT])
        stage = sb("p_stage", [P, 4, GT])
        qk = sb("p_qk", [P, 2, W])
        sqb = sb("p_sqb", [P, 2, W])
        ssq = sb("p_ssq", [P, 2, NH])
        rsq = sb("p_rsq", [P, 2, NH])
        qkh, qkl = sb("p_qkh", [P, 2, W], F32R), sb("p_qkl", [P, 2, W], F32R)
        vhl = sb("p_vhl", [P, NH, 2, HD], F32R)
        ogs = sb("p_ogs", [P, W])
        gqk = sb("p_gqk", [P, 2, HD])
        bf = sb("p_bf", [P, NH])
        banks = [ctx.enter_context(nc.psum_tensor(f"p_b{i}", [P, 512], F32)) for i in range(8)]
        xtb, mmb, qtb = banks[0:2], banks[3:8], [banks[2], banks[1]]

        wloaded = [sem(f"win_loaded{c}") for c in range(8)]
        sp_passed = sem("p_sp_passed")
        small_loaded, carry_zeroed = sem("p_small_loaded"), sem("carry_zeroed")
        x_loaded = Signal(sem("x_loaded"), 1, 16)
        sq_done, rstd_done, xn_ready = (Signal(sem(n), GS) for n in ("sq_done", "rstd_done", "xn_ready"))
        xt_done = Signal(sem("xt_done"), GS)
        ut_act, ut_dve = Signal(sem("ut_act"), GS), Signal(sem("ut_dve"), GS)
        uses = ["rw"] * RT + ["q", "k", "v", "og", "f"] * GS
        mm_done = Signal(sem("p_mm_done"), len(uses))
        free_act = Signal(sem("free_act"), 2 * GS)
        free_dve = Signal(sem("free_dve"), RT + 3 * GS)
        tmp_ready = Signal(sem("tmp_ready"), RT)
        st_done = [Signal(sem(f"st_done{r}"), 4, 16) for r in range(4)]
        sqk_done, rqk_done, qk_ready = (Signal(sem(n), 2 * GS) for n in ("sqk_done", "rqk_done", "qk_ready"))
        ssqk_done = Signal(sem("ssqk_done"), 2 * GS)
        qt_done = Signal(sem("qt_done"), 2 * GS)
        qkh_ready, qkl_ready = Signal(sem("qkh_ready"), 2 * GS), Signal(sem("qkl_ready"), 2 * GS)
        qt_stored = [Signal(sem(f"qt_stored{r}"), 2 * GS, 16) for r in range(2)]
        vog_ready = Signal(sem("vog_ready"), 2 * GS)
        vog_stored = [Signal(sem(f"vog_stored{r}"), GS, 16) for r in range(2)]

        def freed(n):
            a = sum(u in "qk" for u in uses[:n + 1])
            return (free_act, a) if uses[n] in "qk" else (free_dve, n + 1 - a)

        def wait_bank(pe, g, n):
            if n >= 5:
                s, k = freed(n - 5)
                pe.wait_ge(s.sem, s.this(g, k))
            else:
                s, k = freed(n - 5 + len(uses))
                pe.wait_ge(s.sem, s.last(g, k))

        with nc.Block() as block:
            @block.sync
            def _(sp):
                for s in (x_loaded, *st_done, *qt_stored, *vog_stored):
                    s.credit(sp)
                sp.dma_start(bf[:, :], io["b_f"].partition_broadcast(P)).then_inc(small_loaded, 16)
                sp.dma_start(gqk[:, 0, :], io["q_norm_g"].partition_broadcast(P)).then_inc(small_loaded, 16)
                sp.dma_start(gqk[:, 1, :], io["k_norm_g"].partition_broadcast(P)).then_inc(small_loaded, 16)
                x_of = lambda t0: io["x"][0, ds(t0, GT), :].rearrange("(s p) n -> p s n", p=P)
                with sp.Fori(0, NG) as g:
                    t0 = sp.snap(g * GT)
                    ts = [sp.snap(t0 + s * P) for s in range(GS)]
                    sp.wait_ge(xt_done.sem, xt_done.last(g, GS))
                    sp.dma_start(xs[:, :, :], x_of(t0)).then_inc(x_loaded.sem, 16)
                    for m in range(RT):
                        rows = P if m < RT - 1 else RLAST
                        wait_apart(sp, free_dve.sem, free_dve.this(g, m + 1), sp_passed)
                        sp.dma_start(dr["prw"][m * P:m * P + rows, ds(t0, GT)],
                                     stage[0:rows, m % 4, :]).then_inc(st_done[m % 4].sem, 16)
                    sp.sem_inc(st_done[3].sem, 16)
                    for s in range(GS):
                        sp.wait_ge(vog_ready.sem, vog_ready.this(g, 2 * s + 1))
                        sp.dma_start(dr["v"][ds(ts[s], P), :], vhl[:, :, :, :].rearrange("p h c d -> p (h c d)").bitcast(F32)
                                     ).then_inc(vog_stored[0].sem, 16)
                        sp.wait_ge(vog_ready.sem, vog_ready.this(g, 2 * s + 2))
                        sp.dma_start(dr["og"][ds(ts[s], P), :], ogs[:, :]).then_inc(vog_stored[1].sem, 16)
                        for r in range(2):
                            for part, src, name in ((qkh_ready, qkh, "qk"[r] + "h"), (qkl_ready, qkl, "qk"[r] + "l")):
                                wait_apart(sp, part.sem, part.this(g, 2 * s + r + 1), sp_passed)
                                sp.dma_start(dr[name][:, ds(ts[s], P)].rearrange("(j p) n -> p j n", p=P),
                                             src[:, r, :].rearrange("p (j n) -> p j n", j=WT).bitcast(F32)
                                             ).then_inc(qt_stored[r].sem, 16)
                for s in (*st_done, *qt_stored, *vog_stored):
                    sp.wait_ge(s.sem, s.this(NG - 1, s.per))

            @block.gpsimd
            def _(pool):
                rstd_done.credit(pool)
                rqk_done.credit(pool)
                pool.memset(carry[:, :], 0.0).then_inc(carry_zeroed, 1)
                for c in range(8):
                    lo, hi = c * 512, min(c * 512 + 512, INC)
                    pool.dma_start(win[:, :, lo:hi],
                                   io["w_in"][:, lo:hi].rearrange("(k p) n -> p k n", p=P)).then_inc(wloaded[c], 16)
                with pool.Fori(0, NG) as g:
                    for s in range(GS):
                        pool.wait_ge(sq_done.sem, sq_done.this(g, s + 1))
                        pool.tensor_tensor(rstd[:, s:s + 1], ss[:, s:s + 1], per["eps"][:, 0:1], ALU.add)
                        pool.drain()
                        pool.tensor_tensor(rstd[:, s:s + 1], rstd[:, s:s + 1], per["mhalf"][:, 0:1],
                                           ALU.pow).then_inc(rstd_done.sem, 1)
                    for n in range(2 * GS):
                        pool.wait_ge(ssqk_done.sem, ssqk_done.this(g, n + 1))
                        pool.tensor_tensor(rsq[:, n % 2, :], ssq[:, n % 2, :], per["eps"][:, :], ALU.add)
                        pool.drain()
                        pool.tensor_tensor(rsq[:, n % 2, :], rsq[:, n % 2, :], per["mhalf"][:, :],
                                           ALU.pow).then_inc(rqk_done.sem, 1)

            @block.tensor
            def _(pe):
                for s in (xt_done, mm_done, qt_done):
                    s.credit(pe)
                with pe.Fori(0, NG) as g:
                    for s in range(GS):
                        pe.wait_ge(xn_ready.sem, xn_ready.this(g, s + 1))
                        for ev in (ut_act, ut_dve):
                            pe.wait_ge(ev.sem, ev.this(g, s) if s else ev.last(g, GS))
                        if s == 0:
                            pe.wait_ge(qkl_ready.sem, qkl_ready.last(g, 2 * GS))
                        for k in range(KT):
                            mm = pe.transpose(xtb[k // 4][:, (k % 4) * P:(k % 4 + 1) * P],
                                              xs[:, s, k * P:(k + 1) * P], ident[:, :])
                        mm.then_inc(xt_done.sem, 1)
                    for ev in (ut_act, ut_dve):
                        pe.wait_ge(ev.sem, ev.this(g, GS))
                    n = 0
                    for m in range(RT):
                        cols = P if m < RT - 1 else RLAST
                        wait_bank(pe, g, n)
                        pe.wait_ge(wloaded[m * P // 512], 16)
                        for k in range(KT):
                            mm = pe.matmul(mmb[n % 5][0:cols, :], win[:, k, m * P:m * P + cols], ut[:, k, :],
                                           start=(k == 0), stop=(k == KT - 1))
                        mm.then_inc(mm_done.sem, 1)
                        n += 1
                    for s in range(GS):
                        for f in range(5):
                            lo, hi = RW + f * W, min(RW + f * W + W, INC)
                            wait_bank(pe, g, n)
                            for c in range(lo // 512, (hi - 1) // 512 + 1):
                                pe.wait_ge(wloaded[c], 16)
                            for k in range(KT):
                                mm = pe.matmul(mmb[n % 5][:, 0:hi - lo], ut[:, k, s * P:(s + 1) * P],
                                               win[:, k, lo:hi], start=(k == 0), stop=(k == KT - 1))
                            mm.then_inc(mm_done.sem, 1)
                            n += 1
                        for r in range(2):
                            pe.wait_ge(qk_ready.sem, qk_ready.this(g, 2 * s + r + 1))
                            k = 2 * (s - 1) + r + 1
                            pe.wait_ge(qkl_ready.sem, qkl_ready.this(g, k) if k > 0 else qkl_ready.last(g, 2 * GS + k))
                            for j in range(WT):
                                mm = pe.transpose(qtb[r][:, j * P:(j + 1) * P], qk[:, r, j * P:(j + 1) * P],
                                                  ident[:, :])
                            mm.then_inc(qt_done.sem, 1)

            @block.scalar
            def _(act):
                for s in (sq_done, ut_act, free_act, tmp_ready, sqk_done, qkh_ready):
                    s.credit(act)
                act.wait_ge(carry_zeroed, 1)
                with act.Fori(0, NG) as g:
                    for s in range(GS):
                        act.drain()
                        act.wait_ge(x_loaded.sem, x_loaded.this(g, 1))
                        if s == 0:
                            act.wait_ge(rstd_done.sem, rstd_done.last(g, GS))
                        act.activation(junk[:, :], xs[:, s, :], ACT.Square, scale=D ** -0.5,
                                       accum_out=ss[:, s:s + 1]).then_inc(sq_done.sem, 1)
                    act.wait_ge(mm_done.sem, mm_done.last(g, len(uses)))
                    for s in range(GS):
                        act.wait_ge(xt_done.sem, xt_done.this(g, s + 1))
                        for k in range(KT // 2):
                            ev = act.activation(ut[:, k, s * P:(s + 1) * P], xtb[0][:, k * P:(k + 1) * P], ACT.Identity,
                                                bias=per["modc"][:, k:k + 1], scale=per["nscale1"][:, k:k + 1])
                        ev.then_inc(ut_act.sem, 1)
                    for m in range(RT):
                        rows = P if m < RT - 1 else RLAST
                        act.wait_ge(mm_done.sem, mm_done.this(g, m + 1))
                        act.wait_ge(free_dve.sem, free_dve.this(g, m - 1) if m >= 2
                                    else free_dve.last(g, RT + m - 1))
                        act.copy(tmp[0:rows, m % 2, 0:1], carry[0:rows, m:m + 1])
                        act.activation(tmp[0:rows, m % 2, 1:GT + 1], mmb[m % 5][0:rows, :], ACT.Identity,
                                       scale=vc[0:rows, V_MU + m:V_MU + m + 1])
                        act.drain()
                        act.copy(carry[0:rows, m:m + 1], tmp[0:rows, m % 2, GT:GT + 1]).then_inc(tmp_ready.sem, 1)
                    for s in range(GS):
                        for r in range(2):
                            n = RT + 5 * s + r
                            act.wait_ge(mm_done.sem, mm_done.this(g, n + 1))
                            k = 2 * s + r - 1
                            act.wait_ge(qt_done.sem, qt_done.this(g, k) if k > 0 else qt_done.last(g, 2 * GS + k))
                            act.wait_ge(ssqk_done.sem, ssqk_done.this(g, k) if k > 0
                                        else ssqk_done.last(g, 2 * GS + k))
                            act.activation(sqb[:, r, :], mmb[n % 5][:, :], ACT.Square,
                                           scale=HD ** -0.5).then_inc(sqk_done.sem, 1)
                            act.copy(qk[:, r, :], mmb[n % 5][:, :]).then_inc(free_act.sem, 1)
                        for r in range(2):
                            act.wait_ge(qt_done.sem, qt_done.this(g, 2 * s + r + 1))
                            st = qt_stored[r]
                            act.wait_ge(st.sem, st.this(g, 2 * s) if s else st.last(g, 2 * GS))
                            act.copy(qkh[:, r, :], qtb[r][:, :]).then_inc(qkh_ready.sem, 1)

            @block.vector
            def _(dve):
                for s in (xn_ready, ut_dve, free_dve, ssqk_done, qk_ready, qkl_ready, vog_ready):
                    s.credit(dve)
                dve.wait_ge(small_loaded, 48)
                dve.tensor_scalar(gqk[:, 0, :], gqk[:, 0, :], HD ** -0.5, None, ALU.mult)
                with dve.Fori(0, NG) as g:
                    for s in range(GS):
                        dve.wait_ge(rstd_done.sem, rstd_done.this(g, s + 1))
                        dve.tensor_scalar(xs[:, s, :], xs[:, s, :], rstd[:, s:s + 1], None,
                                          ALU.mult).then_inc(xn_ready.sem, 1)
                    dve.wait_ge(mm_done.sem, mm_done.last(g, len(uses)))
                    for s in range(GS):
                        dve.wait_ge(xt_done.sem, xt_done.this(g, s + 1))
                        for k in range(KT // 2, KT):
                            ev = dve.tensor_scalar(ut[:, k, s * P:(s + 1) * P], xtb[1][:, (k - 4) * P:(k - 3) * P],
                                                   per["nscale1"][:, k:k + 1], per["modc"][:, k:k + 1],
                                                   ALU.mult, ALU.add)
                        ev.then_inc(ut_dve.sem, 1)
                    for m in range(RT):
                        rows = P if m < RT - 1 else RLAST
                        dve.wait_ge(tmp_ready.sem, tmp_ready.this(g, m + 1))
                        s = st_done[m % 4]
                        dve.wait_ge(s.sem, s.this(g, m // 4) if m >= 4 else s.last(g, 4))
                        dve.scalar_tensor_tensor(stage[0:rows, m % 4, :], mmb[m % 5][0:rows, :],
                                                 per["omu"][0:rows, m:m + 1], tmp[0:rows, m % 2, 0:GT],
                                                 ALU.mult, ALU.add).then_inc(free_dve.sem, 1)
                    for s in range(GS):
                        for r in range(2):
                            dve.wait_ge(sqk_done.sem, sqk_done.this(g, 2 * s + r + 1))
                            k = 2 * s + r - 1
                            dve.wait_ge(rqk_done.sem, rqk_done.this(g, k) if k > 0 else rqk_done.last(g, 2 * GS + k))
                            dve.tensor_reduce(ssq[:, r, :], sqb[:, r, :].rearrange("p (h d) -> p h d", h=NH),
                                              AX.X, ALU.add).then_inc(ssqk_done.sem, 1)
                            dve.wait_ge(rqk_done.sem, rqk_done.this(g, 2 * s + r + 1))
                            dve.wait_ge(free_act.sem, free_act.this(g, 2 * s + r + 1))
                            q3 = qk[:, r, :].rearrange("p (h d) -> p h d", h=NH)
                            dve.tensor_tensor(q3, q3, rsq[:, r, :].unsqueeze(2).to_broadcast([P, NH, HD]), ALU.mult)
                            dve.drain()
                            dve.tensor_tensor(q3, q3, gqk[:, r, :].unsqueeze(1).to_broadcast([P, NH, HD]),
                                              ALU.mult).then_inc(qk_ready.sem, 1)
                        for r in range(2):
                            n = RT + 5 * s + 2 + r
                            dve.wait_ge(mm_done.sem, mm_done.this(g, n + 1))
                            st = vog_stored[r]
                            dve.wait_ge(st.sem, st.this(g, s) if s else st.last(g, GS))
                            if r == 0:
                                vb = mmb[n % 5][:, :].rearrange("p (h d) -> p h d", h=NH)
                                dve.tensor_copy(vhl[:, :, 0, :], vb)
                                dve.drain()
                                dve.tensor_tensor(vhl[:, :, 1, :], vb, vhl[:, :, 0, :].bitcast(F32),
                                                  ALU.subtract).then_inc(free_dve.sem, 1)
                            else:
                                dve.tensor_copy(ogs[:, :], mmb[n % 5][:, :]).then_inc(free_dve.sem, 1)
                            dve.drain()
                            dve.sem_inc(vog_ready.sem, 1)
                        n = RT + 5 * s + 4
                        dve.wait_ge(mm_done.sem, mm_done.this(g, n + 1))
                        dve.tensor_tensor(per["fraw"][:, ds(g * GS + s, 1), :],
                                          mmb[n % 5][:, 0:NH].unsqueeze(1), bf[:, :].unsqueeze(1),
                                          ALU.add).then_inc(free_dve.sem, 1)
                        for r in range(2):
                            dve.wait_ge(qkh_ready.sem, qkh_ready.this(g, 2 * s + r + 1))
                            dve.tensor_tensor(qkl[:, r, :], qtb[r][:, :], qkh[:, r, :].bitcast(F32),
                                              ALU.subtract).then_inc(qkl_ready.sem, 1)


def block_rwkv(nc, io, per, dr):
    ident, vc = per["ident"], per["vc"]
    with ExitStack() as ctx:
        sb = lambda n, s, d=F32: ctx.enter_context(nc.sbuf_tensor(n, s, d))
        sem = ctx.enter_context(stage_semaphores(nc))
        sig = lambda n, per_turn=1, step=1: Signal(sem(n), per_turn, step)
        wud, wua = sb("wud", [LORA, W]), sb("wua", [P, W])
        wug0, wug1 = sb("wug0", [P, W]), sb("wug1", [GLORA - P, W])
        gnw = sb("gnw", [P, 2, W])
        hw0, ha0 = sb("hw0", [P, WT]), sb("ha0", [P, WT])
        pt = sb("r_pt", [P, RT, P])
        adas = sb("r_adas", [P, KT, 2 * P])
        th = sb("r_th", [LORA, P])
        sg = sb("r_sg", [P, 2, P])
        names = ["tw", "ta", "nlw", "lc", "lx", "e1", "e2", "e1x", "kkr", "sq", "t1", "kp", "pr", "kk", "bt", "zt"]
        f = {n: sb("r_" + n, [P, WT, P]) for n in names}
        kr = sb("r_kr", [P, WT, 2, P])
        ssm, rn, bon = sb("r_ssm", [P, NH]), sb("r_rn", [P, NH]), sb("r_bon", [P, NH])
        rnt = sb("r_rnt", [NH, P])
        v_t, b_t, z_t = sb("r_v", [P, W]), sb("r_b", [P, W]), sb("r_z", [P, W])
        sc = sb("r_sc", [P, NH, 4, P])
        tm, wm, gt = sb("r_tm", [P, NH, P]), sb("r_wm", [P, NH, P]), sb("r_gt", [P, NH, P])
        akv, xn, u = sb("r_akv", [P, W]), sb("r_xn", [P, W]), sb("r_u", [P, W])
        st = sb("r_state", [P, 2, WT, HD])
        y, yq = sb("r_y", [P, W]), sb("r_yq", [P, W])
        gs, gr = sb("r_gs", [P, 2, NH]), sb("r_gr", [P, NH])
        yo = sb("r_yo", [P, W])
        bk = [ctx.enter_context(nc.psum_tensor(f"r_b{i}", [P, 512], F32)) for i in range(8)]

        once_loaded, init_done = sem("r_once_loaded"), sem("r_init_done")
        pe_passed, sp_passed, dve_passed = sem("pe_passed"), sem("sp_passed"), sem("dve_passed")
        p_loaded, ada_loaded, y_stored = sig("p_loaded", 2, 16), sig("r_ada_loaded", 1, 16), sig("y_stored", 1, 16)
        th_ready, sgt_ready, sg_ready = sig("th_ready_"), sig("sgt_ready"), sig("sg_ready")
        zw_done, za_done, g_done = sig("zw_done"), sig("za_done"), sig("g_done")
        tw_ready, ta_ready, kkr_ready, sq_ready = sig("tw_ready"), sig("ta_ready"), sig("kkr_ready"), sig("sq_ready")
        l_ready, e_ready, pr_ready = sig("l_ready"), sig("e_ready"), sig("pr_ready")
        ss_done, ssm_ready, rn_ready = sig("ss_done"), sig("ssm_ready"), sig("rn_ready")
        rnt_done, rnt_ready, rnbc_done = sig("rnt_done"), sig("rnt_ready"), sig("rnbc_done")
        kk_ready, feats_ready = sig("kk_ready"), sig("feats_ready")
        bonus_done, bon_ready = sig("bonus_done"), sig("bon_ready")
        tr_done, tr_ready = sig("tr_done", 3), sig("tr_ready", 3)
        score_done, score_ready = sig("score_done", NH), sig("score_ready", NH)
        w2_ready, t2_done, t2_ready = sig("w2_ready"), sig("t2_done", 2), sig("t2_ready", 2)
        gt_done, gt_ready = sig("gt_done", 2 * LEVELS), sig("gt_ready", 2 * LEVELS)
        tgt_done, tw_upd = sig("tgt_done", 2 * LEVELS), sig("tw_upd", 2 * LEVELS)
        akv_done, akv_ready = sig("akv_done"), sig("akv_ready")
        x_done, x_ready, u_done, u_ready = sig("x_done", 2), sig("x_ready", 2), sig("u_done", 2), sig("u_ready", 2)
        dst_done, st_ready = sig("dst_done", 2), sig("st_ready", 2)
        y_done, y_ready, yc_ready, yq_ready = sig("y_done"), sig("y_ready"), sig("yc_ready"), sig("yq_ready")
        var_ready, gr_ready, yo_ready = sig("var_ready"), sig("gr_ready"), sig("yo_ready")
        ada_done, ada_ready = sig("r_ada_done"), sig("r_ada_ready")
        h3 = lambda ap: ap.rearrange("p (h d) -> p h d", h=NH)
        r_, k_, v_ = (pt[:, n * WT:(n + 1) * WT, :] for n in range(3))
        col = lambda base: vc[:, base:base + WT].unsqueeze(2).to_broadcast([P, WT, P])

        with nc.Block() as block:
            @block.sync
            def _(sp):
                for s in (p_loaded, ada_loaded, y_stored):
                    s.credit(sp)
                sp.dma_start(wud[:, :], io["w_up_decay"]).then_inc(once_loaded, 16)
                sp.dma_start(wua[LORA:P, :], io["w_up_a"]).then_inc(once_loaded, 16)
                sp.dma_start(wug0[:, :], io["w_up_g"][0:P, :]).then_inc(once_loaded, 16)
                sp.dma_start(wug1[:, :], io["w_up_g"][P:GLORA, :]).then_inc(once_loaded, 16)
                sp.dma_start(gnw[:, 0, :], io["gn_g"].partition_broadcast(P)).then_inc(once_loaded, 16)
                sp.dma_start(gnw[:, 1, :], io["gn_b"].partition_broadcast(P)).then_inc(once_loaded, 16)
                with sp.Fori(0, NT) as i:
                    t0 = sp.snap(i * P)
                    c0 = sp.snap(i * (2 * P))
                    wait_apart(sp, tr_done.sem, tr_done.last(i, 3), sp_passed)
                    sp.wait_ge(feats_ready.sem, feats_ready.last(i, 1))
                    sp.dma_start(pt[:, 0:RT - 1, :],
                                 dr["prw"][0:(RT - 1) * P, ds(t0, P)].rearrange("(m p) n -> p m n", p=P)
                                 ).then_inc(p_loaded.sem, 16)
                    sp.dma_start(pt[0:RLAST, RT - 1, :], dr["prw"][(RT - 1) * P:RW, ds(t0, P)]
                                 ).then_inc(p_loaded.sem, 16)
                    sp.wait_ge(ada_done.sem, ada_done.last(i, 1))
                    sp.dma_start(adas[:, :, :],
                                 io["w_ada"][:, ds(c0 + 2 * D, 2 * P)].rearrange("(k p) n -> p k n", p=P)
                                 ).then_inc(ada_loaded.sem, 16)
                    sp.wait_ge(yo_ready.sem, yo_ready.this(i, 1))
                    sp.dma_start(dr["yrw"][ds(t0, P), :], yo[:, :]).then_inc(y_stored.sem, 16)
                sp.wait_ge(y_stored.sem, y_stored.this(NT - 1, 1))

            @block.gpsimd
            def _(pool):
                rn_ready.credit(pool)
                gr_ready.credit(pool)
                pool.memset(xn[:, :], 0.0)
                pool.drain()
                pool.memset(st[:, :, :, :], 0.0).then_inc(init_done, 1)
                with pool.Fori(0, NT) as i:
                    pool.wait_ge(ssm_ready.sem, ssm_ready.this(i, 1))
                    pool.wait_ge(rnt_done.sem, rnt_done.last(i, 1))
                    pool.tensor_tensor(rn[:, :], ssm[:, :], per["mhalf"][:, :], ALU.pow).then_inc(rn_ready.sem, 1)
                    pool.wait_ge(var_ready.sem, var_ready.this(i, 1))
                    pool.tensor_tensor(gr[:, :], gs[:, 1, :], per["mhalf"][:, :], ALU.pow).then_inc(gr_ready.sem, 1)

            @block.tensor
            def _(pe):
                for s in (zw_done, za_done, g_done, ss_done, rnt_done, rnbc_done, bonus_done, tr_done, score_done,
                          t2_done, gt_done, tgt_done, akv_done, x_done, u_done, dst_done, y_done, ada_done):
                    s.credit(pe)
                pe.wait_ge(once_loaded, 16 * 6)
                with pe.Fori(0, NT) as i:
                    pe.wait_ge(th_ready.sem, th_ready.this(i, 1))
                    pe.wait_ge(y_ready.sem, y_ready.last(i, 1))
                    for j in range(WT):
                        mm = pe.matmul(bk[0][:, j * P:(j + 1) * P], wud[:, j * P:(j + 1) * P], th[:, :],
                                       start=True, stop=True)
                    mm.then_inc(zw_done.sem, 1)
                    for j in range(WT):
                        mm = pe.matmul(bk[1][:, j * P:(j + 1) * P], wua[LORA:P, j * P:(j + 1) * P],
                                       pt[LORA:P, RT - 3, :], start=True, stop=True)
                    mm.then_inc(za_done.sem, 1)
                    pe.wait_ge(sq_ready.sem, sq_ready.this(i, 1))
                    pe.wait_ge(ada_ready.sem, ada_ready.last(i, 1))
                    for j in range(WT):
                        mm = pe.matmul(bk[2][:, 2 * j:2 * j + 2], f["sq"][:, j, :], per["headcol"][:, :],
                                       start=True, stop=True)
                    mm.then_inc(ss_done.sem, 1)
                    pe.wait_ge(sg_ready.sem, sg_ready.this(i, 1))
                    pe.wait_ge(yo_ready.sem, yo_ready.last(i, 1))
                    pe.matmul(bk[3][:, :], sg[:, 0, :], wug0[:, :], start=True, stop=False)
                    pe.matmul(bk[3][:, :], sg[0:GLORA - P, 1, :], wug1[:, :], start=False,
                              stop=True).then_inc(g_done.sem, 1)
                    pe.wait_ge(ta_ready.sem, ta_ready.this(i, 1))
                    for j in range(WT):
                        mm = pe.transpose(bk[1][:, j * P:(j + 1) * P], v_[:, j, :], ident[:, :])
                    mm.then_inc(tr_done.sem, 1)
                    pe.wait_ge(pr_ready.sem, pr_ready.this(i, 1))
                    for j in range(WT):
                        mm = pe.matmul(bk[2][:, 16 + 2 * j:18 + 2 * j], f["pr"][:, j, :], per["headcol"][:, :],
                                       start=True, stop=True)
                    mm.then_inc(bonus_done.sem, 1)
                    pe.wait_ge(rn_ready.sem, rn_ready.this(i, 1))
                    pe.transpose(bk[2][0:NH, P:2 * P], rn[:, :], ident[:, :]).then_inc(rnt_done.sem, 1)
                    pe.wait_ge(rnt_ready.sem, rnt_ready.this(i, 1))
                    pe.wait_ge(tw_ready.sem, tw_ready.this(i, 1))
                    for j in range(WT):
                        mm = pe.matmul(bk[0][:, j * P:(j + 1) * P], per["headrow"][0:NH, j * P:(j + 1) * P],
                                       rnt[:, :], start=True, stop=True)
                    mm.then_inc(rnbc_done.sem, 1)
                    pe.wait_ge(feats_ready.sem, feats_ready.this(i, 1))
                    for n, name in ((0, "bt"), (1, "zt")):
                        if n == 1:
                            pe.wait_ge(tr_ready.sem, tr_ready.this(i, 1))
                        for j in range(WT):
                            mm = pe.transpose(bk[n][:, j * P:(j + 1) * P], f[name][:, j, :], ident[:, :])
                        mm.then_inc(tr_done.sem, 1)
                    for h in range(NH):
                        q, j = h % 2, h // 2
                        pe.wait_ge(score_ready.sem, score_ready.this(i, h - 1) if h >= 2 else
                                   score_ready.last(i, NH + h - 1))
                        if h < 2:
                            pe.wait_ge(x_ready.sem, x_ready.last(i, 2))
                        feat = slice(HD * q, HD * q + HD)
                        for n, name in ((0, "bt"), (1, "zt")):
                            mm = pe.matmul(bk[4 + q][:, n * 2 * P:(n + 1) * 2 * P], f[name][feat, j, :],
                                           kr[feat, j, :, :], start=True, stop=True)
                        mm.then_inc(score_done.sem, 1)
                    pe.wait_ge(w2_ready.sem, w2_ready.this(i, 1))
                    for a in range(2):
                        pe.wait_ge(u_ready.sem, u_ready.last(i, 2))
                        pe.wait_ge(st_ready.sem, st_ready.last(i, 2))
                        for h in range(4):
                            mm = pe.transpose(bk[6 + a][:, h * P:(h + 1) * P], wm[:, 4 * a + h, :], ident[:, :])
                        mm.then_inc(t2_done.sem, 1)
                    for lv in range(LEVELS):
                        for a in range(2):
                            n = 2 * lv + a
                            if lv == 0:
                                pe.wait_ge(t2_ready.sem, t2_ready.this(i, a + 1))
                                pe.wait_ge(score_ready.sem, score_ready.this(i, NH))
                            else:
                                pe.wait_ge(tw_upd.sem, tw_upd.this(i, n - 1))
                            for h in range(4 * a, 4 * a + 4):
                                mm = pe.matmul(bk[4 + a][:, (h % 4) * P:(h % 4 + 1) * P], sc[:, h, 0, :],
                                               tm[:, h, :], start=True, stop=True)
                            mm.then_inc(gt_done.sem, 1)
                        for a in range(2):
                            n = 2 * lv + a
                            tb, wb = (bk[6], bk[7]) if a == 0 else (bk[0], bk[1])
                            pe.wait_ge(gt_ready.sem, gt_ready.this(i, n + 1))
                            if lv == 0:
                                pe.wait_ge(t2_ready.sem, t2_ready.this(i, 2))
                                pe.wait_ge(tr_ready.sem, tr_ready.this(i, 3))
                            for h in range(4 * a, 4 * a + 4):
                                out = slice((h % 4) * P, (h % 4 + 1) * P)
                                if lv < LEVELS - 1:
                                    pe.matmul(tb[:, out], wm[:, h, :], gt[:, h, :], start=True, stop=True)
                                mm = pe.matmul(wb[:, out], gt[:, h, :], wm[:, h, :], start=True, stop=True)
                            mm.then_inc(tgt_done.sem, 1)
                    pe.wait_ge(bon_ready.sem, bon_ready.this(i, 1))
                    pe.wait_ge(rnt_ready.sem, rnt_ready.this(i, 1))
                    for h in range(NH):
                        mm = pe.matmul(bk[2][:, h * HD:(h + 1) * HD], sc[:, h, 2, :], v_t[:, h * HD:(h + 1) * HD],
                                       start=True, stop=True)
                    mm.then_inc(akv_done.sem, 1)
                    for c in range(2):
                        rows = slice(C * c, C * c + C)
                        pe.wait_ge(gt_ready.sem, gt_ready.this(i, 2 * LEVELS))
                        if c:
                            pe.wait_ge(x_ready.sem, x_ready.this(i, 1))
                        wait_apart(pe, st_ready.sem, st_ready.this(i, 1) if c else st_ready.last(i, 2), pe_passed)
                        for h in range(NH):
                            q, j = h % 2, h // 2
                            feat = slice(HD * q, HD * q + HD)
                            mm = pe.matmul(bk[4 + q][rows, j * HD:(j + 1) * HD], kr[feat, j, 0, rows],
                                           st[feat, c, j, :], start=True, stop=True)
                        mm.then_inc(x_done.sem, 1)
                        wait_apart(pe, tw_upd.sem, tw_upd.this(i, 2 * LEVELS), pe_passed)
                        for h in range(NH):
                            q, j = h % 2, h // 2
                            feat = slice(HD * q, HD * q + HD)
                            pe.matmul(bk[q][rows, j * HD:(j + 1) * HD], kr[feat, j, 1, rows], st[feat, c, j, :],
                                      start=(j == 0), stop=False, skip_group_check=True)
                        pe.wait_ge(x_ready.sem, x_ready.this(i, c + 1))
                        if c:
                            pe.wait_ge(u_ready.sem, u_ready.this(i, 1))
                        for h in range(NH):
                            mm = pe.matmul(bk[6][rows, h * HD:(h + 1) * HD], wm[:, h, rows],
                                           xn[:, h * HD:(h + 1) * HD], start=True, stop=True)
                        mm.then_inc(u_done.sem, 1)
                        if c:
                            pe.wait_ge(st_ready.sem, st_ready.this(i, 1))
                        wait_apart(pe, u_ready.sem, u_ready.this(i, c + 1), pe_passed)
                        for h in range(NH):
                            q, j = h % 2, h // 2
                            hs = slice(h * HD, (h + 1) * HD)
                            out = bk[7][HD * q:HD * q + HD, j * HD:(j + 1) * HD]
                            pe.matmul(out, b_t[rows, hs], u[rows, hs], start=True, stop=False)
                            mm = pe.matmul(out, z_t[rows, hs], v_t[rows, hs], start=False, stop=True)
                        mm.then_inc(dst_done.sem, 1)
                    for h in range(NH):
                        q, j = h % 2, h // 2
                        hs = slice(h * HD, (h + 1) * HD)
                        out = bk[q][:, j * HD:(j + 1) * HD]
                        pe.matmul(out, sc[:, h, 1, :], u[:, hs], start=False, stop=False, skip_group_check=True)
                        mm = pe.matmul(out, sc[:, h, 3, :], v_t[:, hs], start=False, stop=(j == WT - 1),
                                       skip_group_check=True)
                    mm.then_inc(y_done.sem, 1)
                    pe.wait_ge(ada_loaded.sem, ada_loaded.this(i, 1))
                    pe.wait_ge(akv_ready.sem, akv_ready.this(i, 1))
                    for m in range(2):
                        for k in range(KT):
                            mm = pe.matmul(bk[2][:, m:m + 1], adas[:, k, m * P:(m + 1) * P],
                                           per["silc"][:, k:k + 1], start=(k == 0), stop=(k == KT - 1))
                    mm.then_inc(ada_done.sem, 1)

            @block.scalar
            def _(act):
                for s in (th_ready, sgt_ready, tw_ready, ta_ready, sq_ready, e_ready, rnt_ready, tr_ready, t2_ready,
                          gt_ready, akv_ready, u_ready, y_ready, yq_ready):
                    s.credit(act)
                act.activation(hw0[:, :], vc[:, V_W0:V_W0 + WT], ACT.Copy, scale=0.5)
                act.activation(ha0[:, :], vc[:, V_A0:V_A0 + WT], ACT.Copy, scale=0.5)
                act.wait_ge(init_done, 1)
                with act.Fori(0, NT) as i:
                    act.wait_ge(p_loaded.sem, p_loaded.this(i, 2))
                    act.wait_ge(zw_done.sem, zw_done.last(i, 1))
                    act.activation(th[:, :], pt[0:LORA, RT - 3, :], ACT.Tanh).then_inc(th_ready.sem, 1)
                    act.wait_ge(g_done.sem, g_done.last(i, 1))
                    act.activation(sg[:, 0, :], pt[:, RT - 2, :], ACT.Tanh, scale=0.5)
                    act.activation(sg[0:GLORA - P, 1, :], pt[0:GLORA - P, RT - 1, :], ACT.Tanh,
                                   scale=0.5).then_inc(sgt_ready.sem, 1)
                    act.wait_ge(zw_done.sem, zw_done.this(i, 1))
                    act.wait_ge(l_ready.sem, l_ready.last(i, 1))
                    for j in range(WT):
                        ev = act.activation(f["tw"][:, j, :], bk[0][:, j * P:(j + 1) * P], ACT.Tanh, scale=0.5,
                                            bias=hw0[:, j:j + 1])
                    ev.then_inc(tw_ready.sem, 1)
                    act.wait_ge(za_done.sem, za_done.this(i, 1))
                    act.wait_ge(feats_ready.sem, feats_ready.last(i, 1))
                    for j in range(WT):
                        ev = act.activation(f["ta"][:, j, :], bk[1][:, j * P:(j + 1) * P], ACT.Tanh, scale=0.5,
                                            bias=ha0[:, j:j + 1])
                    ev.then_inc(ta_ready.sem, 1)
                    act.wait_ge(kkr_ready.sem, kkr_ready.this(i, 1))
                    act.wait_ge(ss_done.sem, ss_done.last(i, 1))
                    act.activation(f["sq"][:, :, :], f["kkr"][:, :, :], ACT.Square).then_inc(sq_ready.sem, 1)
                    act.wait_ge(l_ready.sem, l_ready.this(i, 1))
                    act.wait_ge(feats_ready.sem, feats_ready.last(i, 1))
                    act.wait_ge(st_ready.sem, st_ready.last(i, 2))
                    act.activation(f["e1"][:, :, :], f["lc"][:, :, :], ACT.Exp)
                    act.activation(f["e2"][:, :, :], f["lc"][:, :, :], ACT.Exp, scale=-1.0)
                    act.activation(f["e1x"][:, :, :], f["lx"][:, :, :], ACT.Exp).then_inc(e_ready.sem, 1)
                    act.wait_ge(tr_done.sem, tr_done.this(i, 1))
                    act.wait_ge(yo_ready.sem, yo_ready.last(i, 1))
                    act.copy(v_t[:, :], bk[1][:, :]).then_inc(tr_ready.sem, 1)
                    act.wait_ge(rnt_done.sem, rnt_done.this(i, 1))
                    act.wait_ge(rnbc_done.sem, rnbc_done.last(i, 1))
                    act.copy(rnt[:, :], bk[2][0:NH, P:2 * P]).then_inc(rnt_ready.sem, 1)
                    act.wait_ge(dst_done.sem, dst_done.last(i, 2))
                    for n, dst in ((0, b_t), (1, z_t)):
                        act.wait_ge(tr_done.sem, tr_done.this(i, n + 2))
                        act.copy(dst[:, :], bk[n][:, :]).then_inc(tr_ready.sem, 1)
                    for a in range(2):
                        act.wait_ge(t2_done.sem, t2_done.this(i, a + 1))
                        act.copy(tm[:, 4 * a:4 * a + 4, :], bk[6 + a][:, :].rearrange("p (h n) -> p h n", h=4)
                                 ).then_inc(t2_ready.sem, 1)
                    for n in range(2 * LEVELS):
                        a = n % 2
                        act.wait_ge(gt_done.sem, gt_done.this(i, n + 1))
                        act.wait_ge(tgt_done.sem, tgt_done.this(i, n - 1) if n >= 2
                                    else tgt_done.last(i, 2 * LEVELS + n - 1))
                        act.copy(gt[:, 4 * a:4 * a + 4, :], bk[4 + a][:, :].rearrange("p (h n) -> p h n", h=4)
                                 ).then_inc(gt_ready.sem, 1)
                    act.wait_ge(akv_done.sem, akv_done.this(i, 1))
                    act.wait_ge(x_ready.sem, x_ready.last(i, 2))
                    act.copy(akv[:, :], bk[2][:, :]).then_inc(akv_ready.sem, 1)
                    for c in range(2):
                        rows = slice(C * c, C * c + C)
                        act.wait_ge(u_done.sem, u_done.this(i, c + 1))
                        act.wait_ge(y_done.sem, y_done.last(i, 1))
                        act.copy(u[rows, :], bk[6][rows, :]).then_inc(u_ready.sem, 1)
                    act.wait_ge(y_done.sem, y_done.this(i, 1))
                    act.wait_ge(yo_ready.sem, yo_ready.last(i, 1))
                    for q in range(2):
                        ev = act.copy(y[:, :].rearrange("p (j q d) -> p j q d", q=2, d=HD)[:, :, q, :],
                                      bk[q][:, 0:WT * HD].rearrange("p (j d) -> p j d", d=HD))
                    ev.then_inc(y_ready.sem, 1)
                    act.wait_ge(yc_ready.sem, yc_ready.this(i, 1))
                    act.activation(yq[:, :], y[:, :], ACT.Square, scale=HD ** -0.5).then_inc(yq_ready.sem, 1)

            @block.vector
            def _(dve):
                for s in (sg_ready, kkr_ready, l_ready, pr_ready, ssm_ready, kk_ready, feats_ready, bon_ready,
                          score_ready, w2_ready, tw_upd, x_ready, st_ready, yc_ready, var_ready, yo_ready, ada_ready):
                    s.credit(dve)
                dve.wait_ge(once_loaded, 16 * 6)
                dve.wait_ge(init_done, 1)
                tt = dve.tensor_tensor
                with dve.Fori(0, NT) as i:
                    i2 = dve.snap(i * 2)
                    dve.wait_ge(p_loaded.sem, p_loaded.this(i, 2))
                    dve.wait_ge(sq_ready.sem, sq_ready.last(i, 1))
                    tt(f["kkr"][:, :, :], k_, col(V_KK), ALU.mult).then_inc(kkr_ready.sem, 1)
                    dve.wait_ge(sgt_ready.sem, sgt_ready.this(i, 1))
                    dve.tensor_scalar(sg[:, 0, :], sg[:, 0, :], 0.5, 0.5, ALU.mult, ALU.add)
                    dve.tensor_scalar(sg[0:GLORA - P, 1, :], sg[0:GLORA - P, 1, :], 0.5, 0.5, ALU.mult,
                                      ALU.add).then_inc(sg_ready.sem, 1)
                    dve.wait_ge(tw_ready.sem, tw_ready.this(i, 1))
                    dve.wait_ge(e_ready.sem, e_ready.last(i, 1))
                    dve.tensor_scalar(f["nlw"][:, :, :], f["tw"][:, :, :], 0.5 * LOGW, 0.5 * LOGW, ALU.mult, ALU.add)
                    dve.drain()
                    flat = lambda a: a[:, :, :].rearrange("p j n -> p (j n)")
                    dve.tensor_tensor_scan(flat(f["lc"]), per["reset"][:, :], flat(f["nlw"]), 0.0, ALU.mult, ALU.add)
                    dve.drain()
                    tt(f["lx"][:, :, :], f["lc"][:, :, :], f["nlw"][:, :, :], ALU.subtract).then_inc(l_ready.sem, 1)
                    dve.wait_ge(ta_ready.sem, ta_ready.this(i, 1))
                    dve.tensor_scalar(f["ta"][:, :, :], f["ta"][:, :, :], 0.5, 0.5, ALU.mult, ALU.add)
                    dve.drain()
                    dve.scalar_tensor_tensor(f["t1"][:, :, :], f["ta"][:, :, :], -1.0, col(V_KA), ALU.add, ALU.mult)
                    dve.drain()
                    dve.scalar_tensor_tensor(f["kp"][:, :, :], f["t1"][:, :, :], 1.0, k_, ALU.add, ALU.mult)
                    dve.wait_ge(ss_done.sem, ss_done.this(i, 1))
                    dve.wait_ge(rn_ready.sem, rn_ready.last(i, 1))
                    dve.tensor_scalar(ssm[:, :], bk[2][:, 0:NH], 1e-24, None, ALU.max).then_inc(ssm_ready.sem, 1)
                    dve.drain()
                    tt(f["t1"][:, :, :], f["kp"][:, :, :], col(V_RK), ALU.mult)
                    dve.drain()
                    dve.wait_ge(bonus_done.sem, bonus_done.last(i, 1))
                    tt(f["pr"][:, :, :], f["t1"][:, :, :], r_, ALU.mult).then_inc(pr_ready.sem, 1)
                    dve.wait_ge(e_ready.sem, e_ready.this(i, 1))
                    dve.wait_ge(y_done.sem, y_done.last(i, 1))
                    tt(kr[:, :, 1, :], r_, f["e1"][:, :, :], ALU.mult)
                    tt(f["zt"][:, :, :], f["kp"][:, :, :], f["e2"][:, :, :], ALU.mult)
                    dve.wait_ge(rnbc_done.sem, rnbc_done.this(i, 1))
                    tt(f["kk"][:, :, :], f["kkr"][:, :, :], bk[0][:, :].rearrange("p (j n) -> p j n", j=WT), ALU.mult)
                    dve.drain()
                    tt(kr[:, :, 0, :], f["kk"][:, :, :], f["e1x"][:, :, :], ALU.mult)
                    tt(f["bt"][:, :, :], f["kk"][:, :, :], f["ta"][:, :, :], ALU.mult)
                    dve.drain()
                    tt(f["bt"][:, :, :], f["bt"][:, :, :], f["e2"][:, :, :], ALU.mult).then_inc(feats_ready.sem, 1)
                    dve.wait_ge(bonus_done.sem, bonus_done.this(i, 1))
                    dve.tensor_copy(bon[:, :], bk[2][:, 16:16 + NH]).then_inc(bon_ready.sem, 1)
                    for h in range(NH):
                        dve.wait_ge(score_done.sem, score_done.this(i, h + 1))
                        tt(sc[:, h, :, :], bk[4 + h % 2][:, :].rearrange("p (n t) -> p n t", n=4),
                           per["smask"][:, :, :], ALU.mult).then_inc(score_ready.sem, 1)
                    dve.drain()
                    lvl = lambda m, n, heads: per[m][:, n, :].unsqueeze(1).to_broadcast([P, heads, P])
                    tt(wm[:, :, :], sc[:, :, 0, :], lvl("wmask", 0, NH), ALU.mult)
                    dve.drain()
                    tt(wm[:, :, :], wm[:, :, :], ident[:, :].unsqueeze(1).to_broadcast([P, NH, P]),
                       ALU.add).then_inc(w2_ready.sem, 1)
                    for lv in range(LEVELS):
                        for a in range(2):
                            n = 2 * lv + a
                            tb, wb = (bk[6], bk[7]) if a == 0 else (bk[0], bk[1])
                            hs = slice(4 * a, 4 * a + 4)
                            b3 = lambda b: b[:, :].rearrange("p (h n) -> p h n", h=4)
                            wait_apart(dve, tgt_done.sem, tgt_done.this(i, n + 1), dve_passed)
                            if lv < LEVELS - 1:
                                dve.copy_predicated(tm[:, hs, :], lvl("tmask", lv + 1, 4).bitcast(I32), b3(tb))
                            dve.copy_predicated(wm[:, hs, :], lvl("wmask", lv + 1, 4).bitcast(I32),
                                                b3(wb)).then_inc(tw_upd.sem, 1)
                    for c in range(2):
                        rows = slice(C * c, C * c + C)
                        dve.wait_ge(x_done.sem, x_done.this(i, c + 1))
                        dve.wait_ge(akv_ready.sem, akv_ready.this(i, 1))
                        jq = lambda ap: ap.rearrange("p (j q d) -> p j q d", q=2, d=HD)
                        for q in range(2):
                            ev = dve.scalar_tensor_tensor(
                                jq(xn[rows, :])[:, :, q, :], bk[4 + q][rows, 0:WT * HD].rearrange(
                                    "p (j d) -> p j d", d=HD), -1.0, jq(akv[rows, :])[:, :, q, :],
                                ALU.mult, ALU.subtract)
                        ev.then_inc(x_ready.sem, 1)
                        dve.wait_ge(dst_done.sem, dst_done.this(i, c + 1))
                        tt(st[:, 1 - c, :, :], st[:, c, :, :],
                           bk[7][:, 0:WT * HD].rearrange("p (j d) -> p j d", d=HD), ALU.add)
                        dve.drain()
                        end = f["e1"][:, :, C * c + C - 1:C * c + C].to_broadcast([P, WT, HD])
                        tt(st[:, 1 - c, :, :], st[:, 1 - c, :, :], end, ALU.mult).then_inc(st_ready.sem, 1)
                    dve.wait_ge(y_ready.sem, y_ready.this(i, 1))
                    dve.tensor_reduce(gs[:, 0, :], h3(y[:, :]), AX.X, ALU.add)
                    dve.drain()
                    dve.tensor_scalar(gs[:, 0, :], gs[:, 0, :], 1.0 / HD, None, ALU.mult)
                    dve.drain()
                    bc = lambda ap: ap.unsqueeze(2).to_broadcast([P, NH, HD])
                    tt(h3(y[:, :]), h3(y[:, :]), bc(gs[:, 0, :]), ALU.subtract).then_inc(yc_ready.sem, 1)
                    dve.wait_ge(yq_ready.sem, yq_ready.this(i, 1))
                    dve.wait_ge(gr_ready.sem, gr_ready.last(i, 1))
                    dve.tensor_reduce(gs[:, 1, :], h3(yq[:, :]), AX.X, ALU.add)
                    dve.drain()
                    dve.tensor_scalar(gs[:, 1, :], gs[:, 1, :], GN_EPS, None, ALU.add).then_inc(var_ready.sem, 1)
                    dve.wait_ge(gr_ready.sem, gr_ready.this(i, 1))
                    tt(h3(y[:, :]), h3(y[:, :]), bc(gr[:, :]), ALU.mult)
                    dve.drain()
                    tt(y[:, :], y[:, :], gnw[:, 0, :], ALU.mult)
                    tt(h3(yq[:, :]), h3(v_t[:, :]), bc(bon[:, :]), ALU.mult)
                    dve.drain()
                    tt(y[:, :], y[:, :], gnw[:, 1, :], ALU.add)
                    dve.drain()
                    tt(y[:, :], y[:, :], yq[:, :], ALU.add)
                    dve.drain()
                    dve.wait_ge(g_done.sem, g_done.this(i, 1))
                    dve.wait_ge(y_stored.sem, y_stored.last(i, 1))
                    tt(yo[:, :], y[:, :], bk[3][:, :], ALU.mult).then_inc(yo_ready.sem, 1)
                    dve.wait_ge(ada_done.sem, ada_done.this(i, 1))
                    dve.tensor_tensor(per["mod2"][:, ds(i2, 2)], bk[2][:, 0:2], vc[:, ds(i2 + 16, 2)],
                                      ALU.add).then_inc(ada_ready.sem, 1)


def block_fox(nc, io, per, dr):
    ident, oall = per["ident"], per["tiles"]
    KB = 512
    GQ = KB // P
    nb = [t // GQ + 1 for t in range(NT)]
    NSB, NB = 5, sum(nb)
    assert NB % NSB == 0
    first = [sum(nb[:t]) for t in range(NT + 1)]
    tile_of = [t for t in range(NT) for _ in range(nb[t])]
    blocks = [(G, j) for G in range(NG) for j in range(GQ * (G + 1))]
    NBL = len(blocks)
    gfirst = [blocks.index((G, 0)) for G in range(NG)] + [NBL]
    order, behind = [("scores", n) for n in range(first[GQ])], []
    for G in range(NG):
        ns = range(first[GQ * (G + 1)], first[min(GQ * (G + 2), NT)])
        bs = list(range(gfirst[G], gfirst[G + 1]))
        while ns or bs:
            if ns:
                order.append(("scores", ns[0]))
                ns = ns[1:]
            if bs and len(bs) * max(GQ * (G + 2), 1) > len(ns) * GQ * (G + 1):
                B = bs.pop(0)
                order.append(("turn", B))
                if B:
                    order.append(("values", B - 1))
                    if B - 1 in gfirst[1:-1]:
                        order.append(("out", blocks[B - 1][0] - 1))
    order += [("values", NBL - 1), ("out", NG - 1)]
    uses = [(w, i) for w, i in order if w in ("turn", "out")]
    NU = len(uses)
    use = {wi: n for n, wi in enumerate(uses)}
    assert NU % 2 == 0 and NBL % 2 == 0
    with ExitStack() as ctx:
        sb = lambda n, s, d=F32: ctx.enter_context(nc.sbuf_tensor(n, s, d))
        sem = ctx.enter_context(stage_semaphores(nc))
        sig = lambda n, per_turn=1, step=1: Signal(sem(n), per_turn, step)
        k1, k2 = sb("a_k1", [P, 2, T], F32R), sb("a_k2", [P, 2, T], F32R)
        q1, q2 = sb("a_q1", [P, T], F32R), sb("a_q2", [P, T], F32R)
        va = sb("a_v", [P, 2, NT, P], F32R)
        lf = sb("a_lf", [P, NT * NH])
        e1, fneg = sb("a_e1", [P, NT * NH]), sb("a_fneg", [P, NT * NH])
        run = sb("a_run", [P, NT * NH])
        ft = sb("a_ft", [P, 2, P], F32R)
        dmask = sb("a_dmask", [P, P])
        prs = [sb(f"a_pr{i}", [P, GQ, KB * (NG - 1 + i)]) for i in range(2)]
        pr = lambda t, lo, hi: prs[t // GQ % 2][:, t % GQ, lo:hi]
        pth, ptl = sb("a_pth", [P, 2, KB], F32R), sb("a_ptl", [P, 2, KB], F32R)
        ot = sb("a_ot", [P, KB])
        osum = sb("a_osum", [P, GQ, HD])
        mx = sb("a_mx", [P, 4, 4])
        nmx = sb("a_nmx", [P, 2 * GQ])
        rs = sb("a_rs", [P, 2 * GQ, 4])
        rsum, rinv = sb("a_rsum", [P, GQ]), sb("a_rinv", [P, GQ])
        sbk = [ctx.enter_context(nc.psum_tensor(f"a_s{i}", [P, 512], F32)) for i in range(NSB)]
        tbk = [ctx.enter_context(nc.psum_tensor(f"a_t{i}", [P, 512], F32)) for i in range(2)]
        obk = ctx.enter_context(nc.psum_tensor("a_o", [P, 512], F32))

        consts_ready = sem("a_consts_ready")
        lf_abs, lf_exp, lf_ln, lf_ready = sem("lf_abs"), sem("lf_exp"), sem("lf_ln"), sem("lf_ready")
        cum_done, run_ready, fneg_ready, ft_done, fth_ready, ftl_ready = (
            sem(n) for n in ("cum_done", "run_ready", "fneg_ready", "ft_done", "fth_ready", "ftl_ready"))
        f_stored = sem("f_stored")
        kv_loaded = [sig(f"kv_loaded{v}", 6, 16) for v in range(2)]
        q_loaded = [sig(f"q_loaded{G}", 3, 16) for G in range(NG)]
        s_done, max_ready, exp_ready = sig("s_done", NB), sig("max_ready", NT), sig("exp_ready", NB)
        t_done, t_read = sig("t_done", NU), sig("t_read", NU)
        hi_ready, pv_done = sig("hi_ready", NBL), sig("pv_done", NBL)
        ot_ready = sig("ot_ready", NG)

        with nc.Block() as block:
            @block.sync
            def _(sp):
                for s in (*q_loaded, *kv_loaded):
                    s.credit(sp)
                sp.wait_ge(fth_ready, 1)
                sp.wait_ge(ftl_ready, 1)
                sp.dma_start(dr["fneg"].rearrange("c r n -> r c n"), ft[:, :, :].bitcast(F32)).then_inc(f_stored, 16)
                sp.wait_ge(f_stored, 16)
                sp.wait_ge(consts_ready, 4)
                fneg_of = dr["fneg"].rearrange("c (t h) n -> h c t n", h=NH)
                with sp.Fori(0, NH // 2) as u:
                    for v in range(2):
                        h = sp.snap(2 * u + v)
                        row = sp.snap(h * HD)
                        sp.wait_ge(pv_done.sem, pv_done.last(h, 1))
                        for dst, name in ((k1[0:HD, v, :], "kh"), (k1[HD:P, v, :], "kl"), (k2[0:HD, v, :], "kh")):
                            sp.dma_start(dst.bitcast(F32), dr[name][ds(row, HD), :]).then_inc(kv_loaded[v].sem, 16)
                        for c in range(2):
                            sp.dma_start(k2[HD + c:HD + c + 1, v, :].rearrange("o (t n) -> o t n", n=P).bitcast(F32),
                                         fneg_of[ds(h, 1), c, :, :]).then_inc(kv_loaded[v].sem, 16)
                        sp.dma_start(va[:, v, :, :].bitcast(F32), dr["v"][:, ds(row * 2, P)].rearrange("(t p) n -> p t n", p=P)
                                     ).then_inc(kv_loaded[v].sem, 16)
                        for G in range(NG):
                            sp.wait_ge(s_done.sem, s_done.last(h, first[GQ * (G + 1)]))
                            cs = slice(G * KB, (G + 1) * KB)
                            for dst, name in ((q1[0:HD, cs], "qh"), (q1[HD:P, cs], "qh"), (q2[0:HD, cs], "ql")):
                                sp.dma_start(dst.bitcast(F32), dr[name][ds(row, HD), cs]).then_inc(q_loaded[G].sem, 16)

            @block.gpsimd
            def _(pool):
                pool.memset(dmask[:, :], 0.0)
                pool.drain()
                pool.affine_select(out=dmask[:, :], in_=dmask[:, :], compare_op=ALU.is_ge, fill=NEG, base=0,
                                   pattern=[[-1, P]], channel_multiplier=1).then_inc(consts_ready, 1)
                pool.drain()
                pool.memset(k2[HD:P, :, :].bitcast(F32), 0.0).then_inc(consts_ready, 1)
                pool.drain()
                pool.memset(q2[HD:P, :].bitcast(F32), 0.0).then_inc(consts_ready, 1)
                pool.drain()
                pool.memset(q2[HD:HD + 2, :].bitcast(F32), 1.0).then_inc(consts_ready, 1)

            @block.tensor
            def _(pe):
                for s in (s_done, t_done, pv_done):
                    s.credit(pe)
                pe.wait_ge(lf_ready, 1)
                pe.matmul(sbk[0][:, 0:NT * NH], per["tri"][:, :], lf[:, :], start=True, stop=True)
                pe.matmul(sbk[1][:, 0:NT * NH], per["ones"][:, :], lf[:, :], start=True,
                          stop=True).then_inc(cum_done, 1)
                pe.wait_ge(fneg_ready, 1)
                pe.transpose(sbk[2][:, 0:P], fneg[:, :], ident[:, :]).then_inc(ft_done, 1)
                pe.wait_ge(consts_ready, 4)
                pe.wait_ge(ftl_ready, 1)

                def scores(h, v, n):
                    t, b = tile_of[n], n - first[tile_of[n]]
                    if b == 0 and t % GQ == 0:
                        pe.wait_ge(q_loaded[t // GQ].sem, q_loaded[t // GQ].this(h, 3))
                    pe.wait_ge(exp_ready.sem, exp_ready.this(h, n - NSB + 1) if n >= NSB
                               else exp_ready.last(h, NB + n - NSB + 1))
                    width = min(KB, (t + 1) * P - b * KB)
                    out = sbk[n % NSB][:, 0:width]
                    pe.matmul(out, q1[:, t * P:(t + 1) * P], k1[:, v, b * KB:b * KB + width], start=True, stop=False)
                    pe.matmul(out, q2[:, t * P:(t + 1) * P], k2[:, v, b * KB:b * KB + width], start=False,
                              stop=True).then_inc(s_done.sem, 1)

                def bank_read(h, n):
                    pe.wait_ge(t_read.sem, t_read.this(h, n - 1) if n >= 2 else t_read.last(h, NU + n - 1))

                def turn(h, B):
                    G, j = blocks[B]
                    n = use["turn", B]
                    pe.wait_ge(exp_ready.sem, exp_ready.this(h, first[GQ * G + GQ - 1] + j // GQ + 1))
                    bank_read(h, n)
                    for m in range(max(0, j - GQ * G), GQ):
                        mm = pe.transpose(tbk[n % 2][:, m * P:(m + 1) * P],
                                          pr(GQ * G + m, j * P, (j + 1) * P), ident[:, :])
                    mm.then_inc(t_done.sem, 1)

                def values(h, v, B):
                    G, j = blocks[B]
                    lo = max(0, j - GQ * G) * P
                    if j == 0:
                        pe.wait_ge(ot_ready.sem, ot_ready.this(h, G))
                    pe.wait_ge(t_read.sem, t_read.this(h, use["turn", B] + 1))
                    pe.matmul(obk[:, lo:KB], va[:, v, j, :], pth[:, B % 2, lo:KB], start=(j == 0), stop=False,
                              skip_group_check=True)
                    pe.matmul(obk[:, lo:KB], va[:, v, j, :], ptl[:, B % 2, lo:KB], start=False,
                              stop=(B + 1 in gfirst), skip_group_check=True).then_inc(pv_done.sem, 1)

                def out(h, G):
                    n = use["out", G]
                    pe.wait_ge(ot_ready.sem, ot_ready.this(h, G + 1))
                    bank_read(h, n)
                    for m in range(GQ):
                        mm = pe.transpose(tbk[n % 2][:, m * P:(m + 1) * P], ot[:, m * P:(m + 1) * P], ident[:, :])
                    mm.then_inc(t_done.sem, 1)

                with pe.Fori(0, NH // 2) as u:
                    for v in range(2):
                        h = pe.snap(2 * u + v)
                        pe.wait_ge(kv_loaded[v].sem, kv_loaded[v].this(u, 6))
                        for what, n in order:
                            if what == "scores":
                                scores(h, v, n)
                            elif what == "turn":
                                turn(h, n)
                            elif what == "values":
                                values(h, v, n)
                            else:
                                out(h, n)

            @block.scalar
            def _(act):
                for s in (exp_ready, hi_ready, ot_ready):
                    s.credit(act)
                act.wait_ge(lf_abs, 1)
                act.activation(e1[:, :], e1[:, :], ACT.Exp, scale=-1.0).then_inc(lf_exp, 1)
                act.wait_ge(lf_exp, 1)
                act.activation(e1[:, :], e1[:, :], ACT.Ln, bias=per["ones"][:, 0:1]).then_inc(lf_ln, 1)
                act.wait_ge(ft_done, 1)
                act.copy(ft[:, 0, :], sbk[2][:, 0:P]).then_inc(fth_ready, 1)

                def exp(h, n):
                    t, b = tile_of[n], n - first[tile_of[n]]
                    if b == 0:
                        act.wait_ge(max_ready.sem, max_ready.this(h, t + 1))
                        if t % GQ == 0:
                            G = t // GQ
                            act.wait_ge(t_done.sem, t_done.this(h, use["turn", gfirst[G - 1] - 1] + 1) if G >= 2
                                        else t_done.last(h, use["turn", gfirst[G + 3] - 1] + 1))
                            act.wait_ge(t_read.sem, t_read.this(h, use["out", G - 2] + 1) if G >= 2
                                        else t_read.last(h, use["out", G + 2] + 1))
                    width = min(KB, (t + 1) * P - b * KB)
                    s = t % (2 * GQ)
                    act.activation(pr(t, b * KB, b * KB + width), sbk[n % NSB][:, 0:width], ACT.Exp,
                                   bias=nmx[:, s:s + 1], accum_out=rs[:, s, b:b + 1]).then_inc(exp_ready.sem, 1)

                def hi(h, B):
                    G, j = blocks[B]
                    lo = max(0, j - GQ * G) * P
                    n = use["turn", B]
                    act.wait_ge(t_done.sem, t_done.this(h, n + 1))
                    act.wait_ge(pv_done.sem, pv_done.this(h, B - 1) if B >= 2 else pv_done.last(h, NBL + B - 1))
                    act.copy(pth[:, B % 2, lo:KB], tbk[n % 2][:, lo:KB]).then_inc(hi_ready.sem, 1)

                def out_copy(h, G):
                    act.wait_ge(pv_done.sem, pv_done.this(h, gfirst[G + 1]))
                    act.wait_ge(t_done.sem, t_done.this(h, use["out", G - 1] + 1) if G else t_done.last(h, NU))
                    act.copy(ot[:, :], obk[:, :]).then_inc(ot_ready.sem, 1)

                with act.Fori(0, NH) as h:
                    done = seen = 0
                    for what, n in order:
                        if what == "scores":
                            seen = tile_of[n] + (n + 1 == first[tile_of[n] + 1])
                        elif what == "turn":
                            G, j = blocks[n]
                            while done <= first[GQ * G + GQ - 1] + j // GQ:
                                exp(h, done)
                                done += 1
                            hi(h, n)
                        elif what == "values" and n + 1 in gfirst:
                            out_copy(h, blocks[n][0])
                        if what != "values" and done < first[seen]:
                            exp(h, done)
                            done += 1

            @block.vector
            def _(dve):
                for s in (max_ready, t_read):
                    s.credit(dve)
                fr = per["fraw"][:, :, :].rearrange("p t h -> p (t h)")
                dve.tensor_scalar(lf[:, :], fr, -1.0, None, ALU.mult)
                dve.drain()
                dve.tensor_tensor(e1[:, :], lf[:, :], fr, ALU.max).then_inc(lf_abs, 1)
                dve.drain()
                dve.tensor_scalar(lf[:, :], fr, 0.0, None, ALU.min)
                dve.drain()
                dve.wait_ge(lf_ln, 1)
                dve.tensor_tensor(lf[:, :], lf[:, :], e1[:, :], ALU.subtract).then_inc(lf_ready, 1)
                dve.wait_ge(cum_done, 1)
                dve.memset(run[:, 0:NH], 0.0)
                for t in range(1, NT):
                    dve.drain()
                    dve.tensor_tensor(run[:, t * NH:(t + 1) * NH], run[:, (t - 1) * NH:t * NH],
                                      sbk[1][:, (t - 1) * NH:t * NH], ALU.add)
                dve.drain()
                dve.scalar_tensor_tensor(fneg[:, :], sbk[0][:, 0:NT * NH], -1.0, run[:, :], ALU.mult,
                                         ALU.subtract).then_inc(fneg_ready, 1)
                dve.wait_ge(fth_ready, 1)
                dve.tensor_tensor(ft[:, 1, :], sbk[2][:, 0:P], ft[:, 0, :].bitcast(F32), ALU.subtract
                                  ).then_inc(ftl_ready, 1)
                dve.wait_ge(consts_ready, 4)

                def maximum(h, n):
                    t, b = tile_of[n], n - first[tile_of[n]]
                    width = min(KB, (t + 1) * P - b * KB)
                    dve.wait_ge(s_done.sem, s_done.this(h, n + 1))
                    if b == nb[t] - 1:
                        diag = sbk[n % NSB][:, width - P:width]
                        dve.tensor_tensor(diag, diag, dmask[:, :], ALU.add)
                        dve.drain()
                    if b == 0 and nb[t] == 1:
                        dve.drain()
                    dve.tensor_reduce(mx[:, t % 4, b:b + 1], sbk[n % NSB][:, 0:width], AX.X, ALU.max)
                    if b == nb[t] - 1:
                        dve.drain()
                        s = t % (2 * GQ)
                        dve.wait_ge(exp_ready.sem, exp_ready.this(h, first[t - 7]) if t >= 8
                                    else exp_ready.last(h, first[NT + t - 7]))
                        dve.tensor_reduce(nmx[:, s:s + 1], mx[:, t % 4, 0:nb[t]], AX.X, ALU.max,
                                          negate=True).then_inc(max_ready.sem, 1)

                def lo_part(h, B):
                    G, j = blocks[B]
                    lo = max(0, j - GQ * G) * P
                    dve.wait_ge(hi_ready.sem, hi_ready.this(h, B + 1))
                    dve.tensor_tensor(ptl[:, B % 2, lo:KB], tbk[use["turn", B] % 2][:, lo:KB],
                                      pth[:, B % 2, lo:KB].bitcast(F32), ALU.subtract).then_inc(t_read.sem, 1)

                def out(h, G):
                    n = use["out", G]
                    s = GQ * G % (2 * GQ)
                    dve.tensor_reduce(rsum[:, :], rs[:, s:s + GQ, 0:G + 1], AX.X, ALU.add)
                    dve.drain()
                    dve.reciprocal(rinv[:, :], rsum[:, :])
                    dve.wait_ge(t_done.sem, t_done.this(h, n + 1))
                    both = tbk[n % 2][:, :].rearrange("p (t c d) -> p t c d", t=GQ, c=2)
                    dve.tensor_copy(osum[:, :, :], both[:, :, 0, :])
                    dve.drain()
                    dve.tensor_tensor(osum[:, :, :], osum[:, :, :], both[:, :, 1, :], ALU.add)
                    dve.drain()
                    dve.tensor_tensor(oall[:, GQ * G:GQ * (G + 1), ds(h * HD, HD)], osum[:, :, :],
                                      rinv[:, :].unsqueeze(2).to_broadcast([P, GQ, HD]),
                                      ALU.mult).then_inc(t_read.sem, 1)

                with dve.Fori(0, NH) as h:
                    for what, n in order:
                        if what == "scores":
                            maximum(h, n)
                        elif what == "turn":
                            lo_part(h, n)
                        elif what == "out":
                            out(h, n)


def block_out_proj(nc, io, per, dr):
    ident, vc = per["ident"], per["vc"]
    oall = u2 = per["tiles"]
    with ExitStack() as ctx:
        sb = lambda n, s, d=F32: ctx.enter_context(nc.sbuf_tensor(n, s, d))
        sem = ctx.enter_context(stage_semaphores(nc))
        sig = lambda n, per_turn=1, step=1: Signal(sem(n), per_turn, step)
        wo = sb("o_wo", [P, KT, D])
        fg = sb("o_fg", [P, W])
        g1 = sb("o_g1", [P, D])
        gcol = sb("o_gcol", [P, 2, KT, P])
        yc = sb("o_yc", [P, D])
        og = sb("o_og", [P, W])
        sg = sb("o_sg", [P, W])
        xt = sb("o_xt", [P, D])
        fq = sb("o_fq", [P, W])
        fs, fr = sb("o_fs", [P, NH]), sb("o_fr", [P, NH])
        yt = sb("o_yt", [P, KT, P])
        h2 = sb("o_h2", [P, D])
        junk = sb("o_junk", [P, D])
        xn = sb("o_xn", [P, D])
        hs, hr = sb("o_hs", [P, 1]), sb("o_hr", [P, 1])
        bk = [ctx.enter_context(nc.psum_tensor(f"o_b{i}", [P, 512], F32)) for i in range(8)]

        act_passed = sem("o_act_passed")
        wo_loaded, fg_loaded = sem("wo_loaded"), sem("fg_loaded")
        gcol_ready, gbc_done = sem("gcol_ready"), sem("gbc_done")
        yr_loaded, og_loaded, x_loaded = (sig(n, 1, 16) for n in ("o_yr_loaded", "o_og_loaded", "o_x_loaded"))
        h2_stored = sig("h2_stored", 1, 16)
        sg_ready, fq_ready, fs_ready, fr_ready = (sig(n) for n in ("o_sg_ready", "o_fq_ready", "o_fs_ready",
                                                                  "o_fr_ready"))
        yc_ready, yt_done, mm_done, h2_ready = sig("o_yc_ready"), sig("yt_done"), sig("o_mm_done"), sig("h2_ready")
        yt_act, yt_dve = sig("yt_act"), sig("yt_dve")
        hs_ready, hr_ready, xn_ready = sig("o_hs_ready"), sig("o_hr_ready"), sig("o_xn_ready")
        ut_done, ut_act, ut_dve = sig("o_ut_done"), sig("o_ut_act"), sig("o_ut_dve")
        h3 = lambda ap: ap.rearrange("p (h d) -> p h d", h=NH)
        bc = lambda ap: ap.unsqueeze(2).to_broadcast([P, NH, HD])

        with nc.Block() as block:
            @block.sync
            def _(sp):
                for s in (yr_loaded, og_loaded, x_loaded, h2_stored):
                    s.credit(sp)
                sp.dma_start(fg[:, :], io["fox_out_g"].partition_broadcast(P)).then_inc(fg_loaded, 16)
                sp.dma_start(wo[:, :, :], io["w_o"].rearrange("(k p) n -> p k n", p=P)).then_inc(wo_loaded, 16)
                with sp.Fori(0, NT) as t:
                    t0 = sp.snap(t * P)
                    sp.wait_ge(fr_ready.sem, fr_ready.last(t, 1))
                    sp.wait_ge(yc_ready.sem, yc_ready.last(t, 1))
                    sp.dma_start(og[:, :], dr["og"][ds(t0, P), :]).then_inc(og_loaded.sem, 16)
                    sp.wait_ge(yt_done.sem, yt_done.last(t, 1))
                    sp.dma_start(yc[:, 0:W], dr["yrw"][ds(t0, P), :]).then_inc(yr_loaded.sem, 16)
                    sp.wait_ge(h2_ready.sem, h2_ready.last(t, 1))
                    sp.dma_start(xt[:, :], io["x"][0, ds(t0, P), :]).then_inc(x_loaded.sem, 16)
                    sp.wait_ge(h2_ready.sem, h2_ready.this(t, 1))
                    sp.dma_start(dr["h2"][ds(t0, P), :], h2[:, :]).then_inc(h2_stored.sem, 16)
                sp.wait_ge(h2_stored.sem, h2_stored.this(NT - 1, 1))

            @block.gpsimd
            def _(pool):
                fr_ready.credit(pool)
                hr_ready.credit(pool)
                with pool.Fori(0, NT) as t:
                    pool.wait_ge(fs_ready.sem, fs_ready.this(t, 1))
                    pool.tensor_tensor(fr[:, :], fs[:, :], per["eps"][:, :], ALU.add)
                    pool.drain()
                    pool.tensor_tensor(fr[:, :], fr[:, :], per["mhalf"][:, :], ALU.pow).then_inc(fr_ready.sem, 1)
                    pool.wait_ge(hs_ready.sem, hs_ready.this(t, 1))
                    pool.tensor_tensor(hr[:, :], hs[:, :], per["eps"][:, 0:1], ALU.add)
                    pool.drain()
                    pool.tensor_tensor(hr[:, :], hr[:, :], per["mhalf"][:, 0:1], ALU.pow).then_inc(hr_ready.sem, 1)

            @block.tensor
            def _(pe):
                for s in (yt_done, mm_done, ut_done):
                    s.credit(pe)
                pe.wait_ge(gcol_ready, 1)
                for n in range(2):
                    for k in range(KT):
                        mm = pe.matmul(bk[2 * n + k // 4][:, (k % 4) * P:(k % 4 + 1) * P], gcol[:, n, k, :],
                                       ident[:, :], start=True, stop=True)
                mm.then_inc(gbc_done, 1)
                pe.wait_ge(h2_ready.sem, 1)
                pe.wait_ge(wo_loaded, 16)
                with pe.Fori(0, NT) as t:
                    pe.wait_ge(yc_ready.sem, yc_ready.this(t, 1))
                    pe.wait_ge(yt_act.sem, yt_act.last(t, 1))
                    pe.wait_ge(yt_dve.sem, yt_dve.last(t, 1))
                    for k in range(KT):
                        mm = pe.transpose(bk[k // 4][:, (k % 4) * P:(k % 4 + 1) * P], yc[:, k * P:(k + 1) * P],
                                          ident[:, :])
                    mm.then_inc(yt_done.sem, 1)
                    pe.wait_ge(yt_act.sem, yt_act.this(t, 1))
                    pe.wait_ge(yt_dve.sem, yt_dve.this(t, 1))
                    pe.wait_ge(h2_ready.sem, h2_ready.last(t, 1))
                    for n in range(2):
                        for k in range(KT):
                            mm = pe.matmul(bk[2 + n][:, :], yt[:, k, :], wo[:, k, n * 512:(n + 1) * 512],
                                           start=(k == 0), stop=(k == KT - 1))
                    mm.then_inc(mm_done.sem, 1)
                    pe.wait_ge(xn_ready.sem, xn_ready.this(t, 1))
                    pe.wait_ge(ut_act.sem, ut_act.last(t, 1))
                    pe.wait_ge(ut_dve.sem, ut_dve.last(t, 1))
                    for k in range(KT):
                        mm = pe.transpose(bk[4 + k // 4][:, (k % 4) * P:(k % 4 + 1) * P], xn[:, k * P:(k + 1) * P],
                                          ident[:, :])
                    mm.then_inc(ut_done.sem, 1)

            @block.scalar
            def _(act):
                for s in (sg_ready, fq_ready, yt_act, hs_ready, ut_act):
                    s.credit(act)
                with act.Fori(0, NT) as t:
                    wait_apart(act, fs_ready.sem, fs_ready.last(t, 1), act_passed)
                    act.activation(fq[:, :].unsqueeze(1), oall[:, ds(t, 1), 0:W], ACT.Square,
                                   scale=HD ** -0.5).then_inc(fq_ready.sem, 1)
                    act.wait_ge(og_loaded.sem, og_loaded.this(t, 1))
                    act.wait_ge(yc_ready.sem, yc_ready.last(t, 1))
                    act.activation(sg[:, :], og[:, :], ACT.Tanh, scale=0.5).then_inc(sg_ready.sem, 1)
                    act.wait_ge(yt_done.sem, yt_done.this(t, 1))
                    act.wait_ge(mm_done.sem, mm_done.last(t, 1))
                    act.copy(yt[:, 0:4, :], bk[0][:, :].rearrange("p (k n) -> p k n", k=4)).then_inc(yt_act.sem, 1)
                    act.wait_ge(h2_ready.sem, h2_ready.this(t, 1))
                    act.wait_ge(hr_ready.sem, hr_ready.last(t, 1))
                    act.activation(junk[:, :], h2[:, :], ACT.Square, scale=D ** -0.5,
                                   accum_out=hs[:, :]).then_inc(hs_ready.sem, 1)
                    wait_apart(act, ut_done.sem, ut_done.this(t, 1), act_passed)
                    for k in range(4):
                        ev = act.activation(u2[:, ds(t, 1), k * P:(k + 1) * P], bk[4][:, k * P:(k + 1) * P].unsqueeze(1), ACT.Identity,
                                            bias=per["mod2"][:, 8 + k:9 + k], scale=per["nscale2"][:, k:k + 1])
                    ev.then_inc(ut_act.sem, 1)

            @block.vector
            def _(dve):
                for s in (fs_ready, yc_ready, yt_dve, xn_ready, ut_dve):
                    s.credit(dve)
                tt = dve.tensor_tensor
                dve.scalar_tensor_tensor(per["nscale2"][:, :], per["mod2"][:, 16:24], 1.0, vc[:, V_G2:V_G2 + 8],
                                         ALU.add, ALU.mult)
                for n, at in ((0, 0), (1, 24)):
                    ev = dve.tensor_copy(gcol[:, n, :, :], per["mod2"][:, at:at + 8].unsqueeze(2).to_broadcast(
                        [P, KT, P]))
                    dve.drain()
                dve.sem_inc(gcol_ready, 1)
                dve.wait_ge(gbc_done, 1)
                for n, dst in ((0, g1[:, :]), (1, per["g2row"][:, :])):
                    for m in range(2):
                        dve.tensor_copy(dst[:, m * 512:(m + 1) * 512], bk[2 * n + m][:, :])
                dve.drain()
                h2_ready.credit(dve)
                dve.wait_ge(fg_loaded, 16)
                with dve.Fori(0, NT) as t:
                    dve.wait_ge(fq_ready.sem, fq_ready.this(t, 1))
                    dve.wait_ge(fr_ready.sem, fr_ready.last(t, 1))
                    dve.tensor_reduce(fs[:, :], h3(fq[:, :]), AX.X, ALU.add).then_inc(fs_ready.sem, 1)
                    dve.wait_ge(sg_ready.sem, sg_ready.this(t, 1))
                    dve.tensor_scalar(sg[:, :], sg[:, :], 0.5, 0.5, ALU.mult, ALU.add)
                    dve.drain()
                    tt(sg[:, :], sg[:, :], fg[:, :], ALU.mult)
                    dve.wait_ge(fr_ready.sem, fr_ready.this(t, 1))
                    dve.wait_ge(yt_done.sem, yt_done.last(t, 1))
                    tt(h3(yc[:, W:D]), oall[:, ds(t, 1), 0:W].rearrange("p o (h d) -> p (o h) d", h=NH),
                       bc(fr[:, :]), ALU.mult)
                    dve.drain()
                    dve.wait_ge(yr_loaded.sem, yr_loaded.this(t, 1))
                    tt(yc[:, W:D], yc[:, W:D], sg[:, :], ALU.mult).then_inc(yc_ready.sem, 1)
                    dve.wait_ge(yt_done.sem, yt_done.this(t, 1))
                    dve.wait_ge(mm_done.sem, mm_done.last(t, 1))
                    dve.tensor_copy(yt[:, 4:8, :], bk[1][:, :].rearrange("p (k n) -> p k n", k=4)
                                    ).then_inc(yt_dve.sem, 1)
                    dve.wait_ge(mm_done.sem, mm_done.this(t, 1))
                    dve.wait_ge(h2_stored.sem, h2_stored.last(t, 1))
                    dve.wait_ge(hs_ready.sem, hs_ready.last(t, 1))
                    for n in range(2):
                        cs = slice(n * 512, (n + 1) * 512)
                        tt(h2[:, cs], bk[2 + n][:, :], g1[:, cs], ALU.mult)
                    dve.drain()
                    dve.wait_ge(x_loaded.sem, x_loaded.this(t, 1))
                    tt(h2[:, :], h2[:, :], xt[:, :], ALU.add).then_inc(h2_ready.sem, 1)
                    dve.drain()
                    dve.wait_ge(hr_ready.sem, hr_ready.this(t, 1))
                    dve.wait_ge(ut_done.sem, ut_done.last(t, 1))
                    dve.tensor_scalar(xn[:, :], h2[:, :], hr[:, 0:1], None, ALU.mult).then_inc(xn_ready.sem, 1)
                    dve.wait_ge(ut_done.sem, ut_done.this(t, 1))
                    for k in range(4, 8):
                        ev = dve.tensor_scalar(u2[:, ds(t, 1), k * P:(k + 1) * P], bk[5][:, (k - 4) * P:(k - 3) * P].unsqueeze(1),
                                               per["nscale2"][:, k:k + 1], per["mod2"][:, 8 + k:9 + k],
                                               ALU.mult, ALU.add)
                    ev.then_inc(ut_dve.sem, 1)


def block_mlp(nc, io, per, dr):
    u2 = per["tiles"]
    RING, FC = 4, 256
    N1, N2 = FF // FC, FF // 512
    FT = FF // P
    CH = N1 + 2 * N2
    assert CH % RING == 0
    with ExitStack() as ctx:
        sb = lambda n, s, d=F32: ctx.enter_context(nc.sbuf_tensor(n, s, d))
        sem = ctx.enter_context(stage_semaphores(nc))
        sig = lambda n, per_turn=1, step=1: Signal(sem(n), per_turn, step)
        wr = sb("m_wr", [P, RING, KT * FC])
        hid = sb("m_hid", [P, FT, GT])
        rl = sb("m_rl", [P, 2, GT])
        h3 = sb("m_h3", [P, GS, D])
        tmp = sb("m_tmp", [P, 2, 512])
        junk = sb("m_junk", [P, D])
        fgr = sb("m_fgr", [P, D])
        hs, hr = sb("m_hs", [P, GS]), sb("m_hr", [P, GS])
        bk = [ctx.enter_context(nc.psum_tensor(f"m_b{i}", [P, 512], F32)) for i in range(8)]
        fg_loaded = sem("m_fg_loaded")
        w_loaded = [sig(f"w_loaded{r}", CH // RING, 16) for r in range(RING)]
        w_used = sig("w_used", CH)
        h2_loaded, out_stored = sig("m_h2_loaded", 1, 16), sig("out_stored", GS, 16)
        up_done, rl_ready, hid_ready = sig("up_done", FT), sig("rl_ready", FT), sig("hid_ready", FT)
        down_done, down_ev = sig("down_done", 2), sig("down_ev", 2)
        hs_ready, hr_ready, out_ready = sig("m_hs_ready", GS), sig("m_hr_ready", GS), sig("m_out_ready", GS)

        with nc.Block() as block:
            @block.sync
            def _(sp):
                for s in (*w_loaded, ):
                    s.credit(sp)
                with sp.Fori(0, NG) as g:
                    for n in range(CH):
                        sp.wait_ge(w_used.sem, w_used.this(g, n - RING + 1) if n >= RING
                                   else w_used.last(g, CH + n - RING + 1))
                        slot = wr[:, n % RING, :]
                        if n < N1:
                            sp.dma_start(slot.rearrange("p (k n) -> p k n", k=KT),
                                         io["w_mlp1"][:, n * FC:(n + 1) * FC].rearrange("(k p) n -> p k n", p=P)
                                         ).then_inc(w_loaded[n % RING].sem, 16)
                        else:
                            half, m = divmod(n - N1, N2)
                            sp.dma_start(slot.rearrange("p (f n) -> p f n", f=4),
                                         io["w_mlp2"][m * 512:(m + 1) * 512, half * 512:(half + 1) * 512].rearrange(
                                             "(f p) n -> p f n", p=P)).then_inc(w_loaded[n % RING].sem, 16)

            @block.gpsimd
            def _(pool):
                hr_ready.credit(pool)
                with pool.Fori(0, NG) as g:
                    for s in range(GS):
                        pool.wait_ge(hs_ready.sem, hs_ready.this(g, s + 1))
                        pool.tensor_tensor(hr[:, s:s + 1], hs[:, s:s + 1], per["eps"][:, 0:1], ALU.add)
                        pool.drain()
                        pool.tensor_tensor(hr[:, s:s + 1], hr[:, s:s + 1], per["mhalf"][:, 0:1],
                                           ALU.pow).then_inc(hr_ready.sem, 1)

            @block.tensor
            def _(pe):
                for s in (w_used, up_done, down_done):
                    s.credit(pe)
                with pe.Fori(0, NG) as g:
                    g0 = pe.snap(g * GS)
                    for n in range(N1):
                        pe.wait_ge(w_loaded[n % RING].sem, w_loaded[n % RING].this(g, n // RING + 1))
                        w1 = wr[:, n % RING, :].rearrange("p (k n) -> p k n", k=KT)
                        for m in range(FC // P):
                            f = n * (FC // P) + m
                            pe.wait_ge(rl_ready.sem, rl_ready.this(g, f - 1) if f >= 2 else rl_ready.last(g, FT + f - 1))
                            if f < 2:
                                pe.wait_ge(down_ev.sem, down_ev.last(g, 2))
                            for k in range(KT):
                                mm = pe.matmul(bk[f % 2][:, :].rearrange("p (s n) -> p s n", s=GS), w1[:, k, m * P:(m + 1) * P], u2[:, ds(g0, GS), k * P:(k + 1) * P],
                                               start=(k == 0), stop=(k == KT - 1))
                            mm.then_inc(up_done.sem, 1)
                        pe.drain().then_inc(w_used.sem, 1)
                    for half in range(2):
                        banks = bk[4 * (1 - half):4 * (1 - half) + 4]
                        if half:
                            pe.wait_ge(rl_ready.sem, rl_ready.this(g, FT))
                        for m in range(N2):
                            n = N1 + half * N2 + m
                            pe.wait_ge(w_loaded[n % RING].sem, w_loaded[n % RING].this(g, n // RING + 1))
                            w2 = wr[:, n % RING, :].rearrange("p (f n) -> p f n", f=4)
                            for fi in range(4):
                                f = 4 * m + fi
                                if half == 0:
                                    pe.wait_ge(hid_ready.sem, hid_ready.this(g, f + 1))
                                for s in range(GS):
                                    mm = pe.matmul(banks[s][:, :], hid[:, f, s * P:(s + 1) * P], w2[:, fi, :],
                                                   start=(f == 0), stop=(f == FT - 1))
                            if m == N2 - 1:
                                mm.then_inc(down_done.sem, 1)
                            pe.drain().then_inc(w_used.sem, 1)

            @block.scalar
            def _(act):
                for s in (rl_ready, hs_ready, h2_loaded, out_stored):
                    s.credit(act)
                act.dma_start(fgr[:, :], io["final_g"].partition_broadcast(P)).then_inc(fg_loaded, 16)
                with act.Fori(0, NG) as g:
                    t0 = act.snap(g * GT)
                    ts = [act.snap(t0 + s * P) for s in range(GS)]
                    act.wait_ge(out_stored.sem, out_stored.last(g, GS))
                    act.dma_start(h3[:, :, :], dr["h2"][ds(t0, GT), :].rearrange("(s p) n -> p s n", p=P)
                                  ).then_inc(h2_loaded.sem, 16)
                    for f in range(FT):
                        act.wait_ge(up_done.sem, up_done.this(g, f + 1))
                        act.wait_ge(hid_ready.sem, hid_ready.this(g, f - 1) if f >= 2
                                    else hid_ready.last(g, FT + f - 1))
                        act.activation(rl[:, f % 2, :], bk[f % 2][:, :], ACT.Relu).then_inc(rl_ready.sem, 1)
                    for s in range(GS):
                        act.drain()
                        act.wait_ge(hr_ready.sem, hr_ready.last(g, GS))
                        act.wait_ge(down_ev.sem, down_ev.this(g, 2))
                        act.activation(junk[:, :], h3[:, s, :], ACT.Square, scale=D ** -0.5,
                                       accum_out=hs[:, s:s + 1]).then_inc(hs_ready.sem, 1)
                    for s in range(GS):
                        act.wait_ge(out_ready.sem, out_ready.this(g, s + 1))
                        act.dma_start(io["out"][0, ds(ts[s], P), :], h3[:, s, :]).then_inc(out_stored.sem, 16)
                act.wait_ge(out_stored.sem, out_stored.this(NG - 1, GS))

            @block.vector
            def _(dve):
                for s in (hid_ready, down_ev, out_ready):
                    s.credit(dve)
                tt = dve.tensor_tensor
                dve.wait_ge(fg_loaded, 16)
                with dve.Fori(0, NG) as g:
                    for f in range(FT):
                        if f == 0:
                            dve.wait_ge(down_done.sem, down_done.last(g, 2))
                        dve.wait_ge(rl_ready.sem, rl_ready.this(g, f + 1))
                        tt(hid[:, f, :], rl[:, f % 2, :], rl[:, f % 2, :], ALU.mult).then_inc(hid_ready.sem, 1)
                    dve.wait_ge(h2_loaded.sem, h2_loaded.this(g, 1))
                    for half in range(2):
                        banks = bk[4 * (1 - half):4 * (1 - half) + 4]
                        cs = slice(half * 512, (half + 1) * 512)
                        dve.wait_ge(down_done.sem, down_done.this(g, half + 1))
                        for s in range(GS):
                            tt(tmp[:, s % 2, :], banks[s][:, :], per["g2row"][:, cs], ALU.mult)
                            dve.drain()
                            ev = tt(h3[:, s, cs], h3[:, s, cs], tmp[:, s % 2, :], ALU.add)
                        ev.then_inc(down_ev.sem, 1)
                    for s in range(GS):
                        dve.wait_ge(hr_ready.sem, hr_ready.this(g, s + 1))
                        dve.scalar_tensor_tensor(h3[:, s, :], h3[:, s, :], hr[:, s:s + 1], fgr[:, :], ALU.mult,
                                                 ALU.mult).then_inc(out_ready.sem, 1)


KEPT = {"ident": [P, P], "ones": [P, P], "tri": [P, P], "vc": [P, V_N], "modc": [P, 16], "mod2": [P, 32],
        "nscale1": [P, 8], "nscale2": [P, 8], "silc": [P, 8], "omu": [P, RT], "fraw": [P, NT, NH], "eps": [P, 8],
        "mhalf": [P, 8]}
MASKS = {"smask": [P, 4, P], "tmask": [P, LEVELS + 1, P], "wmask": [P, LEVELS + 1, P], "headcol": [P, 2],
         "headrow": [P, W], "reset": [P, W]}
SCRATCH = {"prw": [RW, T], "og": [T, W], "yrw": [T, W], "h2": [T, D],
           "qh": [W, T], "ql": [W, T], "kh": [W, T], "kl": [W, T], "v": [T, 2 * W], "fneg": [2, P, P]}


_INS = ["x", "c", "w_ada", "b_ada", "norm1_g", "w_in", "mu_shift", "w0", "w_up_decay", "a0", "w_up_a", "w_up_g",
        "k_k", "k_a", "r_k", "gn_g", "gn_b", "b_f", "q_norm_g", "k_norm_g", "fox_out_g", "w_o", "norm2_g",
        "w_mlp1", "w_mlp2", "final_g"]


def build(nc, io):
    dr = {n: nc.dram_tensor(f"scratch_{n}", shape, F32, kind="Internal").ap() for n, shape in SCRATCH.items()}
    keep = lambda ctx, shapes: {n: ctx.enter_context(nc.sbuf_tensor(n, shape, F32)) for n, shape in shapes.items()}
    with ExitStack() as ctx:
        per = keep(ctx, KEPT)
        with ExitStack() as masks_ctx:
            masks = keep(masks_ctx, MASKS)
            block_constants(nc, io, {**per, **masks}, dr)
            block_project(nc, io, per, dr)
            block_rwkv(nc, io, {**per, **masks}, dr)
        per |= keep(ctx, {"tiles": [P, NT, D], "g2row": [P, D]})
        block_fox(nc, io, per, dr)
        block_out_proj(nc, io, per, dr)
        block_mlp(nc, io, per, dr)


def kernel(**inputs):
    import numpy as np
    import concourse.bacc as bacc
    from concourse.bass_utils import run_bass_kernel_spmd

    nc = bacc.Bacc("TRN2", target_bir_lowering=False, num_devices=1)
    arrays, io = {}, {}
    for name in _INS:
        a = np.ascontiguousarray(inputs[name])
        arrays[f"in_{name}"] = a
        io[name] = nc.dram_tensor(f"in_{name}", a.shape, mybir.dt.from_np(a.dtype), kind="ExternalInput").ap()
    io["out"] = nc.dram_tensor("out", [1, T, D], F32, kind="ExternalOutput").ap()
    build(nc, io)
    r = run_bass_kernel_spmd(nc, [arrays], core_ids=[0])
    return r.results[0]["out"]
```

```python
from contextlib import ExitStack, contextmanager

import concourse.bass as bass
from concourse import mybir

F32 = mybir.dt.float32
F32R = mybir.dt.float32r
I32 = mybir.dt.int32
ALU = mybir.AluOpType
ACT = mybir.ActivationFunctionType
AX = mybir.AxisListType
ds = bass.ds

P = 128
D = 1024
T = 2048
KT = D // P
NT = T // P
W = 512
HD = 64
NH = W // HD
WT = W // P
LORA = 64
GLORA = 160
RW = 3 * W + 2 * LORA + GLORA
FX = 4 * W + NH
INC = RW + FX
RT = -(-RW // P)
RLAST = RW - (RT - 1) * P
FF = 4 * D
GT = 512
NG = T // GT
GS = GT // P
C = 64
EPS = 1e-6
GN_EPS = 64e-5
NEG = -1e30
LEVELS = 5
LOGW = -0.6065306597126334

V_BADA, V_G1, V_G2, V_MU, V_W0, V_A0, V_KK, V_KA, V_RK, V_C = 0, 48, 56, 64, 79, 83, 87, 91, 95, 99
V_N = 107


class Signal:

    def __init__(self, sem, per, step=1):
        self.sem, self.per, self.step = sem, per, step

    def credit(self, eng, ahead=0):
        eng.sem_inc(self.sem, (self.per - ahead) * self.step)

    def this(self, i, k):
        return i * (self.per * self.step) + (self.per + k) * self.step

    def last(self, i, k):
        return i * (self.per * self.step) + k * self.step


@contextmanager
def stage_semaphores(nc):
    taken = []

    def take(name):
        taken.append(nc.alloc_semaphore(name=name))
        return taken[-1]

    yield take
    nc.clear_and_free_semaphores(taken)
    nc.all_engine_barrier()


def wait_apart(eng, sem, value, passed):
    eng.wait_ge(sem, value)
    eng.sem_inc(passed, 1)


def block_constants(nc, io, per, dr):
    ident, vc, modc = per["ident"], per["vc"], per["modc"]
    with ExitStack() as ctx:
        sb = lambda n, s, d=F32: ctx.enter_context(nc.sbuf_tensor(n, s, d))
        sem = ctx.enter_context(stage_semaphores(nc))
        vrows = sb("vrows", [P, P])
        wada = sb("wada", [P, 4, KT, 512])
        sil = sb("sil", [P, 8])
        trp = ctx.enter_context(nc.psum_tensor("c_trp", [P, 512], F32))
        modp = ctx.enter_context(nc.psum_tensor("c_modp", [P, 512], F32))
        vec_zeroed, vec_loaded, ident_zeroed = sem("vec_zeroed"), sem("vec_loaded"), sem("ident_zeroed")
        ident_ready, vec_turned, vc_ready = sem("ident_ready"), sem("vec_turned"), sem("vc_ready")
        th_ready, sil_ready, mod_done = sem("th_ready"), sem("sil_ready"), sem("mod_done")
        ada_loaded = [sem(f"ada_loaded{c}") for c in range(4)]

        with nc.Block() as block:
            @block.sync
            def _(sp):
                sp.wait_ge(vec_zeroed, 1)
                rows = lambda name, n: io[name].rearrange("(a b) -> a b", b=P)
                for at, name, n in ((V_BADA, "b_ada", 48), (V_G1, "norm1_g", 8), (V_G2, "norm2_g", 8),
                                    (V_W0, "w0", 4), (V_A0, "a0", 4), (V_KK, "k_k", 4), (V_KA, "k_a", 4)):
                    sp.dma_start(vrows[at:at + n, :], rows(name, n)).then_inc(vec_loaded, 16)
                sp.dma_start(vrows[V_MU:V_MU + RT - 1, :],
                             io["mu_shift"][0:(RT - 1) * P].rearrange("(a b) -> a b", b=P)).then_inc(vec_loaded, 16)
                sp.dma_start(vrows[V_MU + RT - 1:V_MU + RT, 0:RLAST],
                             io["mu_shift"][(RT - 1) * P:RW].rearrange("(a b) -> a b", a=1)).then_inc(vec_loaded, 16)
                sp.dma_start(vrows[V_RK:V_RK + 4, :],
                             io["r_k"].rearrange("(a b) d -> a (b d)", b=2)).then_inc(vec_loaded, 16)
                sp.dma_start(vrows[V_C:V_C + 8, :],
                             io["c"].rearrange("o (a b) -> (o a) b", b=P)).then_inc(vec_loaded, 16)
                for c in range(4):
                    sp.dma_start(wada[:, c, :, :],
                                 io["w_ada"][:, c * 512:(c + 1) * 512].rearrange("(k p) n -> p k n", p=P)
                                 ).then_inc(ada_loaded[c], 16)

            @block.gpsimd
            def _(pool):
                pool.memset(vrows[:, :], 0.0).then_inc(vec_zeroed, 1)
                pool.memset(ident[:, :], 0.0).then_inc(ident_zeroed, 1)
                pool.memset(per["ones"][:, :], 1.0)
                pool.memset(per["mhalf"][:, :], -0.5)
                pool.memset(per["eps"][:, :], EPS)
                pool.wait_ge(ident_zeroed, 1)
                pool.affine_select(out=ident[:, :], in_=ident[:, :], compare_op=ALU.not_equal, fill=1.0,
                                   base=0, pattern=[[-1, P]], channel_multiplier=1).then_inc(ident_ready, 1)

                def keep(m, pattern, base, mult):
                    pool.drain()
                    pool.affine_select(out=m, in_=m, compare_op=ALU.is_ge, fill=0.0, base=base,
                                       pattern=pattern, channel_multiplier=mult)

                sm = per["smask"]
                pool.memset(sm[:, 0:1, :], -1.0)
                pool.memset(sm[:, 1:4, :], 1.0)
                for n in range(4):
                    m = sm[:, n, :]
                    keep(m, [[1, P]], -1 if n % 2 == 0 else 0, -1)
                    keep(m.rearrange("p (b t) -> p b t", b=2), [[-C, 2], [0, C]], 0, 1)
                pool.memset(per["tri"][:, :], 1.0)
                keep(per["tri"][:, :], [[1, P]], 0, -1)
                for n in range(LEVELS + 1):
                    b = 1 << n
                    for m, half in ((per["tmask"][:, n, :], 0), (per["wmask"][:, n, :], 1)):
                        pool.memset(m, 1.0)
                        m4 = m.rearrange("p (u h w) -> p u h w", h=2, w=b)
                        nb = P // (2 * b)
                        lo = 0 if half else b
                        keep(m4, [[-2 * b, nb], [0, 2], [0, b]], -lo, 1)
                        keep(m4, [[2 * b, nb], [0, 2], [0, b]], lo + b - 1, -1)
                        if half:
                            keep(m4, [[0, nb], [1, 2], [0, b]], -1, 0)
                        else:
                            keep(m4, [[0, nb], [-1, 2], [0, b]], 0, 0)
                pool.memset(per["headcol"][:, :], 1.0)
                keep(per["headcol"][:, 0:1], [[0, 1]], HD - 1, -1)
                keep(per["headcol"][:, 1:2], [[0, 1]], -HD, 1)
                pool.memset(per["headrow"][:, :], 1.0)
                hr = per["headrow"][:, :].rearrange("p (h d) -> p h d", h=NH)
                keep(hr, [[-1, NH], [0, HD]], 0, 1)
                keep(hr, [[1, NH], [0, HD]], 0, -1)
                pool.memset(per["reset"][:, :], 1.0)
                pool.drain()
                pool.memset(per["reset"][:, :].rearrange("p (n c) -> p n c", c=C)[:, :, 0:1], 0.0)

            @block.tensor
            def _(pe):
                pe.wait_ge(ident_ready, 1)
                pe.wait_ge(vec_loaded, 16 * 11)
                pe.transpose(trp[:, 0:P], vrows[:, :], ident[:, :]).then_inc(vec_turned, 1)
                pe.wait_ge(sil_ready, 1)
                for c in range(4):
                    pe.wait_ge(ada_loaded[c], 16)
                    for m in range(4):
                        for k in range(KT):
                            mm = pe.matmul(modp[:, 4 * c + m:4 * c + m + 1], wada[:, c, k, m * P:(m + 1) * P],
                                           sil[:, k:k + 1], start=(k == 0), stop=(k == KT - 1))
                mm.then_inc(mod_done, 1)

            @block.scalar
            def _(act):
                act.wait_ge(vc_ready, 1)
                act.activation(sil[:, :], vc[:, V_C:V_C + 8], ACT.Tanh, scale=0.5).then_inc(th_ready, 1)

            @block.vector
            def _(dve):
                dve.wait_ge(vec_turned, 1)
                dve.tensor_copy(vc[:, :], trp[:, 0:V_N]).then_inc(vc_ready, 1)
                dve.wait_ge(th_ready, 1)
                dve.tensor_scalar(sil[:, :], sil[:, :], 0.5, 0.5, ALU.mult, ALU.add)
                dve.drain()
                dve.tensor_tensor(per["silc"][:, :], sil[:, :], vc[:, V_C:V_C + 8], ALU.mult)
                dve.drain()
                dve.tensor_copy(sil[:, :], per["silc"][:, :]).then_inc(sil_ready, 1)
                dve.tensor_scalar(per["omu"][:, :], vc[:, V_MU:V_MU + RT], -1.0, 1.0, ALU.mult, ALU.add)
                dve.wait_ge(mod_done, 1)
                dve.tensor_tensor(modc[:, 0:16], modp[:, 0:16], vc[:, V_BADA:V_BADA + 16], ALU.add)
                dve.drain()
                dve.scalar_tensor_tensor(per["nscale1"][:, :], modc[:, 8:16], 1.0, vc[:, V_G1:V_G1 + 8],
                                         ALU.add, ALU.mult)


def block_project(nc, io, per, dr):
    ident, vc = per["ident"], per["vc"]
    with ExitStack() as ctx:
        sb = lambda n, s, d=F32: ctx.enter_context(nc.sbuf_tensor(n, s, d))
        sem = ctx.enter_context(stage_semaphores(nc))
        win = sb("win", [P, KT, INC])
        xs = sb("xs", [P, GS, D])
        ut = sb("ut", [P, KT, GT])
        junk = sb("p_junk", [P, D])
        ss = sb("p_ss", [P, GS])
        rstd = sb("p_rstd", [P, GS])
        tmp = sb("p_tmp", [P, 2, GT + 1])
        carry = sb("p_carry", [P, RT])
        stage = sb("p_stage", [P, 4, GT])
        qk = sb("p_qk", [P, 2, W])
        sqb = sb("p_sqb", [P, 2, W])
        ssq = sb("p_ssq", [P, 2, NH])
        rsq = sb("p_rsq", [P, 2, NH])
        qkh, qkl = sb("p_qkh", [P, 2, W], F32R), sb("p_qkl", [P, 2, W], F32R)
        vhl = sb("p_vhl", [P, NH, 2, HD], F32R)
        ogs = sb("p_ogs", [P, W])
        gqk = sb("p_gqk", [P, 2, HD])
        bf = sb("p_bf", [P, NH])
        banks = [ctx.enter_context(nc.psum_tensor(f"p_b{i}", [P, 512], F32)) for i in range(8)]
        xtb, mmb, qtb = banks[0:2], banks[3:8], [banks[2], banks[1]]

        wloaded = [sem(f"win_loaded{c}") for c in range(8)]
        sp_passed = sem("p_sp_passed")
        small_loaded, carry_zeroed = sem("p_small_loaded"), sem("carry_zeroed")
        x_loaded = Signal(sem("x_loaded"), 1, 16)
        sq_done, rstd_done, xn_ready = (Signal(sem(n), GS) for n in ("sq_done", "rstd_done", "xn_ready"))
        xt_done = Signal(sem("xt_done"), GS)
        ut_act, ut_dve = Signal(sem("ut_act"), GS), Signal(sem("ut_dve"), GS)
        uses = ["rw"] * RT + ["q", "k", "v", "og", "f"] * GS
        mm_done = Signal(sem("p_mm_done"), len(uses))
        free_act = Signal(sem("free_act"), 2 * GS)
        free_dve = Signal(sem("free_dve"), RT + 3 * GS)
        tmp_ready = Signal(sem("tmp_ready"), RT)
        st_done = [Signal(sem(f"st_done{r}"), 4, 16) for r in range(4)]
        sqk_done, rqk_done, qk_ready = (Signal(sem(n), 2 * GS) for n in ("sqk_done", "rqk_done", "qk_ready"))
        ssqk_done = Signal(sem("ssqk_done"), 2 * GS)
        qt_done = Signal(sem("qt_done"), 2 * GS)
        qkh_ready, qkl_ready = Signal(sem("qkh_ready"), 2 * GS), Signal(sem("qkl_ready"), 2 * GS)
        qt_stored = [Signal(sem(f"qt_stored{r}"), 2 * GS, 16) for r in range(2)]
        vog_ready = Signal(sem("vog_ready"), 2 * GS)
        vog_stored = [Signal(sem(f"vog_stored{r}"), GS, 16) for r in range(2)]

        def freed(n):
            a = sum(u in "qk" for u in uses[:n + 1])
            return (free_act, a) if uses[n] in "qk" else (free_dve, n + 1 - a)

        def wait_bank(pe, g, n):
            if n >= 5:
                s, k = freed(n - 5)
                pe.wait_ge(s.sem, s.this(g, k))
            else:
                s, k = freed(n - 5 + len(uses))
                pe.wait_ge(s.sem, s.last(g, k))

        with nc.Block() as block:
            @block.sync
            def _(sp):
                for s in (x_loaded, *st_done, *qt_stored, *vog_stored):
                    s.credit(sp)
                sp.dma_start(bf[:, :], io["b_f"].partition_broadcast(P)).then_inc(small_loaded, 16)
                sp.dma_start(gqk[:, 0, :], io["q_norm_g"].partition_broadcast(P)).then_inc(small_loaded, 16)
                sp.dma_start(gqk[:, 1, :], io["k_norm_g"].partition_broadcast(P)).then_inc(small_loaded, 16)
                x_of = lambda t0: io["x"][0, ds(t0, GT), :].rearrange("(s p) n -> p s n", p=P)
                with sp.Fori(0, NG) as g:
                    t0 = sp.snap(g * GT)
                    ts = [sp.snap(t0 + s * P) for s in range(GS)]
                    sp.wait_ge(xt_done.sem, xt_done.last(g, GS))
                    sp.dma_start(xs[:, :, :], x_of(t0)).then_inc(x_loaded.sem, 16)
                    for m in range(RT):
                        rows = P if m < RT - 1 else RLAST
                        wait_apart(sp, free_dve.sem, free_dve.this(g, m + 1), sp_passed)
                        sp.dma_start(dr["prw"][m * P:m * P + rows, ds(t0, GT)],
                                     stage[0:rows, m % 4, :]).then_inc(st_done[m % 4].sem, 16)
                    sp.sem_inc(st_done[3].sem, 16)
                    for s in range(GS):
                        sp.wait_ge(vog_ready.sem, vog_ready.this(g, 2 * s + 1))
                        sp.dma_start(dr["v"][ds(ts[s], P), :], vhl[:, :, :, :].rearrange("p h c d -> p (h c d)").bitcast(F32)
                                     ).then_inc(vog_stored[0].sem, 16)
                        sp.wait_ge(vog_ready.sem, vog_ready.this(g, 2 * s + 2))
                        sp.dma_start(dr["og"][ds(ts[s], P), :], ogs[:, :]).then_inc(vog_stored[1].sem, 16)
                        for r in range(2):
                            for part, src, name in ((qkh_ready, qkh, "qk"[r] + "h"), (qkl_ready, qkl, "qk"[r] + "l")):
                                wait_apart(sp, part.sem, part.this(g, 2 * s + r + 1), sp_passed)
                                sp.dma_start(dr[name][:, ds(ts[s], P)].rearrange("(j p) n -> p j n", p=P),
                                             src[:, r, :].rearrange("p (j n) -> p j n", j=WT).bitcast(F32)
                                             ).then_inc(qt_stored[r].sem, 16)
                for s in (*st_done, *qt_stored, *vog_stored):
                    sp.wait_ge(s.sem, s.this(NG - 1, s.per))

            @block.gpsimd
            def _(pool):
                rstd_done.credit(pool)
                rqk_done.credit(pool)
                pool.memset(carry[:, :], 0.0).then_inc(carry_zeroed, 1)
                for c in range(8):
                    lo, hi = c * 512, min(c * 512 + 512, INC)
                    pool.dma_start(win[:, :, lo:hi],
                                   io["w_in"][:, lo:hi].rearrange("(k p) n -> p k n", p=P)).then_inc(wloaded[c], 16)
                with pool.Fori(0, NG) as g:
                    for s in range(GS):
                        pool.wait_ge(sq_done.sem, sq_done.this(g, s + 1))
                        pool.tensor_tensor(rstd[:, s:s + 1], ss[:, s:s + 1], per["eps"][:, 0:1], ALU.add)
                        pool.drain()
                        pool.tensor_tensor(rstd[:, s:s + 1], rstd[:, s:s + 1], per["mhalf"][:, 0:1],
                                           ALU.pow).then_inc(rstd_done.sem, 1)
                    for n in range(2 * GS):
                        pool.wait_ge(ssqk_done.sem, ssqk_done.this(g, n + 1))
                        pool.tensor_tensor(rsq[:, n % 2, :], ssq[:, n % 2, :], per["eps"][:, :], ALU.add)
                        pool.drain()
                        pool.tensor_tensor(rsq[:, n % 2, :], rsq[:, n % 2, :], per["mhalf"][:, :],
                                           ALU.pow).then_inc(rqk_done.sem, 1)

            @block.tensor
            def _(pe):
                for s in (xt_done, mm_done, qt_done):
                    s.credit(pe)
                with pe.Fori(0, NG) as g:
                    for s in range(GS):
                        pe.wait_ge(xn_ready.sem, xn_ready.this(g, s + 1))
                        for ev in (ut_act, ut_dve):
                            pe.wait_ge(ev.sem, ev.this(g, s) if s else ev.last(g, GS))
                        if s == 0:
                            pe.wait_ge(qkl_ready.sem, qkl_ready.last(g, 2 * GS))
                        for k in range(KT):
                            mm = pe.transpose(xtb[k // 4][:, (k % 4) * P:(k % 4 + 1) * P],
                                              xs[:, s, k * P:(k + 1) * P], ident[:, :])
                        mm.then_inc(xt_done.sem, 1)
                    for ev in (ut_act, ut_dve):
                        pe.wait_ge(ev.sem, ev.this(g, GS))
                    n = 0
                    for m in range(RT):
                        cols = P if m < RT - 1 else RLAST
                        wait_bank(pe, g, n)
                        pe.wait_ge(wloaded[m * P // 512], 16)
                        for k in range(KT):
                            mm = pe.matmul(mmb[n % 5][0:cols, :], win[:, k, m * P:m * P + cols], ut[:, k, :],
                                           start=(k == 0), stop=(k == KT - 1))
                        mm.then_inc(mm_done.sem, 1)
                        n += 1
                    for s in range(GS):
                        for f in range(5):
                            lo, hi = RW + f * W, min(RW + f * W + W, INC)
                            wait_bank(pe, g, n)
                            for c in range(lo // 512, (hi - 1) // 512 + 1):
                                pe.wait_ge(wloaded[c], 16)
                            for k in range(KT):
                                mm = pe.matmul(mmb[n % 5][:, 0:hi - lo], ut[:, k, s * P:(s + 1) * P],
                                               win[:, k, lo:hi], start=(k == 0), stop=(k == KT - 1))
                            mm.then_inc(mm_done.sem, 1)
                            n += 1
                        for r in range(2):
                            pe.wait_ge(qk_ready.sem, qk_ready.this(g, 2 * s + r + 1))
                            k = 2 * (s - 1) + r + 1
                            pe.wait_ge(qkl_ready.sem, qkl_ready.this(g, k) if k > 0 else qkl_ready.last(g, 2 * GS + k))
                            for j in range(WT):
                                mm = pe.transpose(qtb[r][:, j * P:(j + 1) * P], qk[:, r, j * P:(j + 1) * P],
                                                  ident[:, :])
                            mm.then_inc(qt_done.sem, 1)

            @block.scalar
            def _(act):
                for s in (sq_done, ut_act, free_act, tmp_ready, sqk_done, qkh_ready):
                    s.credit(act)
                act.wait_ge(carry_zeroed, 1)
                with act.Fori(0, NG) as g:
                    for s in range(GS):
                        act.drain()
                        act.wait_ge(x_loaded.sem, x_loaded.this(g, 1))
                        if s == 0:
                            act.wait_ge(rstd_done.sem, rstd_done.last(g, GS))
                        act.activation(junk[:, :], xs[:, s, :], ACT.Square, scale=D ** -0.5,
                                       accum_out=ss[:, s:s + 1]).then_inc(sq_done.sem, 1)
                    act.wait_ge(mm_done.sem, mm_done.last(g, len(uses)))
                    for s in range(GS):
                        act.wait_ge(xt_done.sem, xt_done.this(g, s + 1))
                        for k in range(KT // 2):
                            ev = act.activation(ut[:, k, s * P:(s + 1) * P], xtb[0][:, k * P:(k + 1) * P], ACT.Identity,
                                                bias=per["modc"][:, k:k + 1], scale=per["nscale1"][:, k:k + 1])
                        ev.then_inc(ut_act.sem, 1)
                    for m in range(RT):
                        rows = P if m < RT - 1 else RLAST
                        act.wait_ge(mm_done.sem, mm_done.this(g, m + 1))
                        act.wait_ge(free_dve.sem, free_dve.this(g, m - 1) if m >= 2
                                    else free_dve.last(g, RT + m - 1))
                        act.copy(tmp[0:rows, m % 2, 0:1], carry[0:rows, m:m + 1])
                        act.activation(tmp[0:rows, m % 2, 1:GT + 1], mmb[m % 5][0:rows, :], ACT.Identity,
                                       scale=vc[0:rows, V_MU + m:V_MU + m + 1])
                        act.drain()
                        act.copy(carry[0:rows, m:m + 1], tmp[0:rows, m % 2, GT:GT + 1]).then_inc(tmp_ready.sem, 1)
                    for s in range(GS):
                        for r in range(2):
                            n = RT + 5 * s + r
                            act.wait_ge(mm_done.sem, mm_done.this(g, n + 1))
                            k = 2 * s + r - 1
                            act.wait_ge(qt_done.sem, qt_done.this(g, k) if k > 0 else qt_done.last(g, 2 * GS + k))
                            act.wait_ge(ssqk_done.sem, ssqk_done.this(g, k) if k > 0
                                        else ssqk_done.last(g, 2 * GS + k))
                            act.activation(sqb[:, r, :], mmb[n % 5][:, :], ACT.Square,
                                           scale=HD ** -0.5).then_inc(sqk_done.sem, 1)
                            act.copy(qk[:, r, :], mmb[n % 5][:, :]).then_inc(free_act.sem, 1)
                        for r in range(2):
                            act.wait_ge(qt_done.sem, qt_done.this(g, 2 * s + r + 1))
                            st = qt_stored[r]
                            act.wait_ge(st.sem, st.this(g, 2 * s) if s else st.last(g, 2 * GS))
                            act.copy(qkh[:, r, :], qtb[r][:, :]).then_inc(qkh_ready.sem, 1)

            @block.vector
            def _(dve):
                for s in (xn_ready, ut_dve, free_dve, ssqk_done, qk_ready, qkl_ready, vog_ready):
                    s.credit(dve)
                dve.wait_ge(small_loaded, 48)
                dve.tensor_scalar(gqk[:, 0, :], gqk[:, 0, :], HD ** -0.5, None, ALU.mult)
                with dve.Fori(0, NG) as g:
                    for s in range(GS):
                        dve.wait_ge(rstd_done.sem, rstd_done.this(g, s + 1))
                        dve.tensor_scalar(xs[:, s, :], xs[:, s, :], rstd[:, s:s + 1], None,
                                          ALU.mult).then_inc(xn_ready.sem, 1)
                    dve.wait_ge(mm_done.sem, mm_done.last(g, len(uses)))
                    for s in range(GS):
                        dve.wait_ge(xt_done.sem, xt_done.this(g, s + 1))
                        for k in range(KT // 2, KT):
                            ev = dve.tensor_scalar(ut[:, k, s * P:(s + 1) * P], xtb[1][:, (k - 4) * P:(k - 3) * P],
                                                   per["nscale1"][:, k:k + 1], per["modc"][:, k:k + 1],
                                                   ALU.mult, ALU.add)
                        ev.then_inc(ut_dve.sem, 1)
                    for m in range(RT):
                        rows = P if m < RT - 1 else RLAST
                        dve.wait_ge(tmp_ready.sem, tmp_ready.this(g, m + 1))
                        s = st_done[m % 4]
                        dve.wait_ge(s.sem, s.this(g, m // 4) if m >= 4 else s.last(g, 4))
                        dve.scalar_tensor_tensor(stage[0:rows, m % 4, :], mmb[m % 5][0:rows, :],
                                                 per["omu"][0:rows, m:m + 1], tmp[0:rows, m % 2, 0:GT],
                                                 ALU.mult, ALU.add).then_inc(free_dve.sem, 1)
                    for s in range(GS):
                        for r in range(2):
                            dve.wait_ge(sqk_done.sem, sqk_done.this(g, 2 * s + r + 1))
                            k = 2 * s + r - 1
                            dve.wait_ge(rqk_done.sem, rqk_done.this(g, k) if k > 0 else rqk_done.last(g, 2 * GS + k))
                            dve.tensor_reduce(ssq[:, r, :], sqb[:, r, :].rearrange("p (h d) -> p h d", h=NH),
                                              AX.X, ALU.add).then_inc(ssqk_done.sem, 1)
                            dve.wait_ge(rqk_done.sem, rqk_done.this(g, 2 * s + r + 1))
                            dve.wait_ge(free_act.sem, free_act.this(g, 2 * s + r + 1))
                            q3 = qk[:, r, :].rearrange("p (h d) -> p h d", h=NH)
                            dve.tensor_tensor(q3, q3, rsq[:, r, :].unsqueeze(2).to_broadcast([P, NH, HD]), ALU.mult)
                            dve.drain()
                            dve.tensor_tensor(q3, q3, gqk[:, r, :].unsqueeze(1).to_broadcast([P, NH, HD]),
                                              ALU.mult).then_inc(qk_ready.sem, 1)
                        for r in range(2):
                            n = RT + 5 * s + 2 + r
                            dve.wait_ge(mm_done.sem, mm_done.this(g, n + 1))
                            st = vog_stored[r]
                            dve.wait_ge(st.sem, st.this(g, s) if s else st.last(g, GS))
                            if r == 0:
                                vb = mmb[n % 5][:, :].rearrange("p (h d) -> p h d", h=NH)
                                dve.tensor_copy(vhl[:, :, 0, :], vb)
                                dve.drain()
                                dve.tensor_tensor(vhl[:, :, 1, :], vb, vhl[:, :, 0, :].bitcast(F32),
                                                  ALU.subtract).then_inc(free_dve.sem, 1)
                            else:
                                dve.tensor_copy(ogs[:, :], mmb[n % 5][:, :]).then_inc(free_dve.sem, 1)
                            dve.drain()
                            dve.sem_inc(vog_ready.sem, 1)
                        n = RT + 5 * s + 4
                        dve.wait_ge(mm_done.sem, mm_done.this(g, n + 1))
                        dve.tensor_tensor(per["fraw"][:, ds(g * GS + s, 1), :],
                                          mmb[n % 5][:, 0:NH].unsqueeze(1), bf[:, :].unsqueeze(1),
                                          ALU.add).then_inc(free_dve.sem, 1)
                        for r in range(2):
                            dve.wait_ge(qkh_ready.sem, qkh_ready.this(g, 2 * s + r + 1))
                            dve.tensor_tensor(qkl[:, r, :], qtb[r][:, :], qkh[:, r, :].bitcast(F32),
                                              ALU.subtract).then_inc(qkl_ready.sem, 1)


def block_rwkv(nc, io, per, dr):
    ident, vc = per["ident"], per["vc"]
    with ExitStack() as ctx:
        sb = lambda n, s, d=F32: ctx.enter_context(nc.sbuf_tensor(n, s, d))
        sem = ctx.enter_context(stage_semaphores(nc))
        sig = lambda n, per_turn=1, step=1: Signal(sem(n), per_turn, step)
        wud, wua = sb("wud", [LORA, W]), sb("wua", [P, W])
        wug0, wug1 = sb("wug0", [P, W]), sb("wug1", [GLORA - P, W])
        gnw = sb("gnw", [P, 2, W])
        hw0, ha0 = sb("hw0", [P, WT]), sb("ha0", [P, WT])
        pt = sb("r_pt", [P, RT, P])
        adas = sb("r_adas", [P, KT, 2 * P])
        th = sb("r_th", [LORA, P])
        sg = sb("r_sg", [P, 2, P])
        names = ["tw", "ta", "nlw", "lc", "lx", "e1", "e2", "e1x", "kkr", "sq", "t1", "kp", "pr", "kk", "bt", "zt"]
        f = {n: sb("r_" + n, [P, WT, P]) for n in names}
        kr = sb("r_kr", [P, WT, 2, P])
        ssm, rn, bon = sb("r_ssm", [P, NH]), sb("r_rn", [P, NH]), sb("r_bon", [P, NH])
        rnt = sb("r_rnt", [NH, P])
        v_t, b_t, z_t = sb("r_v", [P, W]), sb("r_b", [P, W]), sb("r_z", [P, W])
        sc = sb("r_sc", [P, NH, 4, P])
        tm, wm, gt = sb("r_tm", [P, NH, P]), sb("r_wm", [P, NH, P]), sb("r_gt", [P, NH, P])
        akv, xn, u = sb("r_akv", [P, W]), sb("r_xn", [P, W]), sb("r_u", [P, W])
        st = sb("r_state", [P, 2, WT, HD])
        y, yq = sb("r_y", [P, W]), sb("r_yq", [P, W])
        gs, gr = sb("r_gs", [P, 2, NH]), sb("r_gr", [P, NH])
        yo = sb("r_yo", [P, W])
        bk = [ctx.enter_context(nc.psum_tensor(f"r_b{i}", [P, 512], F32)) for i in range(8)]

        once_loaded, init_done = sem("r_once_loaded"), sem("r_init_done")
        pe_passed, sp_passed, dve_passed = sem("pe_passed"), sem("sp_passed"), sem("dve_passed")
        p_loaded, ada_loaded, y_stored = sig("p_loaded", 2, 16), sig("r_ada_loaded", 1, 16), sig("y_stored", 1, 16)
        th_ready, sgt_ready, sg_ready = sig("th_ready_"), sig("sgt_ready"), sig("sg_ready")
        zw_done, za_done, g_done = sig("zw_done"), sig("za_done"), sig("g_done")
        tw_ready, ta_ready, kkr_ready, sq_ready = sig("tw_ready"), sig("ta_ready"), sig("kkr_ready"), sig("sq_ready")
        l_ready, e_ready, pr_ready = sig("l_ready"), sig("e_ready"), sig("pr_ready")
        ss_done, ssm_ready, rn_ready = sig("ss_done"), sig("ssm_ready"), sig("rn_ready")
        rnt_done, rnt_ready, rnbc_done = sig("rnt_done"), sig("rnt_ready"), sig("rnbc_done")
        kk_ready, feats_ready = sig("kk_ready"), sig("feats_ready")
        bonus_done, bon_ready = sig("bonus_done"), sig("bon_ready")
        tr_done, tr_ready = sig("tr_done", 3), sig("tr_ready", 3)
        score_done, score_ready = sig("score_done", NH), sig("score_ready", NH)
        w2_ready, t2_done, t2_ready = sig("w2_ready"), sig("t2_done", 2), sig("t2_ready", 2)
        gt_done, gt_ready = sig("gt_done", 2 * LEVELS), sig("gt_ready", 2 * LEVELS)
        tgt_done, tw_upd = sig("tgt_done", 2 * LEVELS), sig("tw_upd", 2 * LEVELS)
        akv_done, akv_ready = sig("akv_done"), sig("akv_ready")
        x_done, x_ready, u_done, u_ready = sig("x_done", 2), sig("x_ready", 2), sig("u_done", 2), sig("u_ready", 2)
        dst_done, st_ready = sig("dst_done", 2), sig("st_ready", 2)
        y_done, y_ready, yc_ready, yq_ready = sig("y_done"), sig("y_ready"), sig("yc_ready"), sig("yq_ready")
        var_ready, gr_ready, yo_ready = sig("var_ready"), sig("gr_ready"), sig("yo_ready")
        ada_done, ada_ready = sig("r_ada_done"), sig("r_ada_ready")
        h3 = lambda ap: ap.rearrange("p (h d) -> p h d", h=NH)
        r_, k_, v_ = (pt[:, n * WT:(n + 1) * WT, :] for n in range(3))
        col = lambda base: vc[:, base:base + WT].unsqueeze(2).to_broadcast([P, WT, P])

        with nc.Block() as block:
            @block.sync
            def _(sp):
                for s in (p_loaded, ada_loaded, y_stored):
                    s.credit(sp)
                sp.dma_start(wud[:, :], io["w_up_decay"]).then_inc(once_loaded, 16)
                sp.dma_start(wua[LORA:P, :], io["w_up_a"]).then_inc(once_loaded, 16)
                sp.dma_start(wug0[:, :], io["w_up_g"][0:P, :]).then_inc(once_loaded, 16)
                sp.dma_start(wug1[:, :], io["w_up_g"][P:GLORA, :]).then_inc(once_loaded, 16)
                sp.dma_start(gnw[:, 0, :], io["gn_g"].partition_broadcast(P)).then_inc(once_loaded, 16)
                sp.dma_start(gnw[:, 1, :], io["gn_b"].partition_broadcast(P)).then_inc(once_loaded, 16)
                with sp.Fori(0, NT) as i:
                    t0 = sp.snap(i * P)
                    c0 = sp.snap(i * (2 * P))
                    wait_apart(sp, tr_done.sem, tr_done.last(i, 3), sp_passed)
                    sp.wait_ge(feats_ready.sem, feats_ready.last(i, 1))
                    sp.dma_start(pt[:, 0:RT - 1, :],
                                 dr["prw"][0:(RT - 1) * P, ds(t0, P)].rearrange("(m p) n -> p m n", p=P)
                                 ).then_inc(p_loaded.sem, 16)
                    sp.dma_start(pt[0:RLAST, RT - 1, :], dr["prw"][(RT - 1) * P:RW, ds(t0, P)]
                                 ).then_inc(p_loaded.sem, 16)
                    sp.wait_ge(ada_done.sem, ada_done.last(i, 1))
                    sp.dma_start(adas[:, :, :],
                                 io["w_ada"][:, ds(c0 + 2 * D, 2 * P)].rearrange("(k p) n -> p k n", p=P)
                                 ).then_inc(ada_loaded.sem, 16)
                    sp.wait_ge(yo_ready.sem, yo_ready.this(i, 1))
                    sp.dma_start(dr["yrw"][ds(t0, P), :], yo[:, :]).then_inc(y_stored.sem, 16)
                sp.wait_ge(y_stored.sem, y_stored.this(NT - 1, 1))

            @block.gpsimd
            def _(pool):
                rn_ready.credit(pool)
                gr_ready.credit(pool)
                pool.memset(xn[:, :], 0.0)
                pool.drain()
                pool.memset(st[:, :, :, :], 0.0).then_inc(init_done, 1)
                with pool.Fori(0, NT) as i:
                    pool.wait_ge(ssm_ready.sem, ssm_ready.this(i, 1))
                    pool.wait_ge(rnt_done.sem, rnt_done.last(i, 1))
                    pool.tensor_tensor(rn[:, :], ssm[:, :], per["mhalf"][:, :], ALU.pow).then_inc(rn_ready.sem, 1)
                    pool.wait_ge(var_ready.sem, var_ready.this(i, 1))
                    pool.tensor_tensor(gr[:, :], gs[:, 1, :], per["mhalf"][:, :], ALU.pow).then_inc(gr_ready.sem, 1)

            @block.tensor
            def _(pe):
                for s in (zw_done, za_done, g_done, ss_done, rnt_done, rnbc_done, bonus_done, tr_done, score_done,
                          t2_done, gt_done, tgt_done, akv_done, x_done, u_done, dst_done, y_done, ada_done):
                    s.credit(pe)
                pe.wait_ge(once_loaded, 16 * 6)
                with pe.Fori(0, NT) as i:
                    pe.wait_ge(th_ready.sem, th_ready.this(i, 1))
                    pe.wait_ge(y_ready.sem, y_ready.last(i, 1))
                    for j in range(WT):
                        mm = pe.matmul(bk[0][:, j * P:(j + 1) * P], wud[:, j * P:(j + 1) * P], th[:, :],
                                       start=True, stop=True)
                    mm.then_inc(zw_done.sem, 1)
                    for j in range(WT):
                        mm = pe.matmul(bk[1][:, j * P:(j + 1) * P], wua[LORA:P, j * P:(j + 1) * P],
                                       pt[LORA:P, RT - 3, :], start=True, stop=True)
                    mm.then_inc(za_done.sem, 1)
                    pe.wait_ge(sq_ready.sem, sq_ready.this(i, 1))
                    pe.wait_ge(ada_ready.sem, ada_ready.last(i, 1))
                    for j in range(WT):
                        mm = pe.matmul(bk[2][:, 2 * j:2 * j + 2], f["sq"][:, j, :], per["headcol"][:, :],
                                       start=True, stop=True)
                    mm.then_inc(ss_done.sem, 1)
                    pe.wait_ge(sg_ready.sem, sg_ready.this(i, 1))
                    pe.wait_ge(yo_ready.sem, yo_ready.last(i, 1))
                    pe.matmul(bk[3][:, :], sg[:, 0, :], wug0[:, :], start=True, stop=False)
                    pe.matmul(bk[3][:, :], sg[0:GLORA - P, 1, :], wug1[:, :], start=False,
                              stop=True).then_inc(g_done.sem, 1)
                    pe.wait_ge(ta_ready.sem, ta_ready.this(i, 1))
                    for j in range(WT):
                        mm = pe.transpose(bk[1][:, j * P:(j + 1) * P], v_[:, j, :], ident[:, :])
                    mm.then_inc(tr_done.sem, 1)
                    pe.wait_ge(pr_ready.sem, pr_ready.this(i, 1))
                    for j in range(WT):
                        mm = pe.matmul(bk[2][:, 16 + 2 * j:18 + 2 * j], f["pr"][:, j, :], per["headcol"][:, :],
                                       start=True, stop=True)
                    mm.then_inc(bonus_done.sem, 1)
                    pe.wait_ge(rn_ready.sem, rn_ready.this(i, 1))
                    pe.transpose(bk[2][0:NH, P:2 * P], rn[:, :], ident[:, :]).then_inc(rnt_done.sem, 1)
                    pe.wait_ge(rnt_ready.sem, rnt_ready.this(i, 1))
                    pe.wait_ge(tw_ready.sem, tw_ready.this(i, 1))
                    for j in range(WT):
                        mm = pe.matmul(bk[0][:, j * P:(j + 1) * P], per["headrow"][0:NH, j * P:(j + 1) * P],
                                       rnt[:, :], start=True, stop=True)
                    mm.then_inc(rnbc_done.sem, 1)
                    pe.wait_ge(feats_ready.sem, feats_ready.this(i, 1))
                    for n, name in ((0, "bt"), (1, "zt")):
                        if n == 1:
                            pe.wait_ge(tr_ready.sem, tr_ready.this(i, 1))
                        for j in range(WT):
                            mm = pe.transpose(bk[n][:, j * P:(j + 1) * P], f[name][:, j, :], ident[:, :])
                        mm.then_inc(tr_done.sem, 1)
                    for h in range(NH):
                        q, j = h % 2, h // 2
                        pe.wait_ge(score_ready.sem, score_ready.this(i, h - 1) if h >= 2 else
                                   score_ready.last(i, NH + h - 1))
                        if h < 2:
                            pe.wait_ge(x_ready.sem, x_ready.last(i, 2))
                        feat = slice(HD * q, HD * q + HD)
                        for n, name in ((0, "bt"), (1, "zt")):
                            mm = pe.matmul(bk[4 + q][:, n * 2 * P:(n + 1) * 2 * P], f[name][feat, j, :],
                                           kr[feat, j, :, :], start=True, stop=True)
                        mm.then_inc(score_done.sem, 1)
                    pe.wait_ge(w2_ready.sem, w2_ready.this(i, 1))
                    for a in range(2):
                        pe.wait_ge(u_ready.sem, u_ready.last(i, 2))
                        pe.wait_ge(st_ready.sem, st_ready.last(i, 2))
                        for h in range(4):
                            mm = pe.transpose(bk[6 + a][:, h * P:(h + 1) * P], wm[:, 4 * a + h, :], ident[:, :])
                        mm.then_inc(t2_done.sem, 1)
                    for lv in range(LEVELS):
                        for a in range(2):
                            n = 2 * lv + a
                            if lv == 0:
                                pe.wait_ge(t2_ready.sem, t2_ready.this(i, a + 1))
                                pe.wait_ge(score_ready.sem, score_ready.this(i, NH))
                            else:
                                pe.wait_ge(tw_upd.sem, tw_upd.this(i, n - 1))
                            for h in range(4 * a, 4 * a + 4):
                                mm = pe.matmul(bk[4 + a][:, (h % 4) * P:(h % 4 + 1) * P], sc[:, h, 0, :],
                                               tm[:, h, :], start=True, stop=True)
                            mm.then_inc(gt_done.sem, 1)
                        for a in range(2):
                            n = 2 * lv + a
                            tb, wb = (bk[6], bk[7]) if a == 0 else (bk[0], bk[1])
                            pe.wait_ge(gt_ready.sem, gt_ready.this(i, n + 1))
                            if lv == 0:
                                pe.wait_ge(t2_ready.sem, t2_ready.this(i, 2))
                                pe.wait_ge(tr_ready.sem, tr_ready.this(i, 3))
                            for h in range(4 * a, 4 * a + 4):
                                out = slice((h % 4) * P, (h % 4 + 1) * P)
                                if lv < LEVELS - 1:
                                    pe.matmul(tb[:, out], wm[:, h, :], gt[:, h, :], start=True, stop=True)
                                mm = pe.matmul(wb[:, out], gt[:, h, :], wm[:, h, :], start=True, stop=True)
                            mm.then_inc(tgt_done.sem, 1)
                    pe.wait_ge(bon_ready.sem, bon_ready.this(i, 1))
                    pe.wait_ge(rnt_ready.sem, rnt_ready.this(i, 1))
                    for h in range(NH):
                        mm = pe.matmul(bk[2][:, h * HD:(h + 1) * HD], sc[:, h, 2, :], v_t[:, h * HD:(h + 1) * HD],
                                       start=True, stop=True)
                    mm.then_inc(akv_done.sem, 1)
                    for c in range(2):
                        rows = slice(C * c, C * c + C)
                        pe.wait_ge(gt_ready.sem, gt_ready.this(i, 2 * LEVELS))
                        if c:
                            pe.wait_ge(x_ready.sem, x_ready.this(i, 1))
                        wait_apart(pe, st_ready.sem, st_ready.this(i, 1) if c else st_ready.last(i, 2), pe_passed)
                        for h in range(NH):
                            q, j = h % 2, h // 2
                            feat = slice(HD * q, HD * q + HD)
                            mm = pe.matmul(bk[4 + q][rows, j * HD:(j + 1) * HD], kr[feat, j, 0, rows],
                                           st[feat, c, j, :], start=True, stop=True)
                        mm.then_inc(x_done.sem, 1)
                        wait_apart(pe, tw_upd.sem, tw_upd.this(i, 2 * LEVELS), pe_passed)
                        for h in range(NH):
                            q, j = h % 2, h // 2
                            feat = slice(HD * q, HD * q + HD)
                            pe.matmul(bk[q][rows, j * HD:(j + 1) * HD], kr[feat, j, 1, rows], st[feat, c, j, :],
                                      start=(j == 0), stop=False, skip_group_check=True)
                        pe.wait_ge(x_ready.sem, x_ready.this(i, c + 1))
                        if c:
                            pe.wait_ge(u_ready.sem, u_ready.this(i, 1))
                        for h in range(NH):
                            mm = pe.matmul(bk[6][rows, h * HD:(h + 1) * HD], wm[:, h, rows],
                                           xn[:, h * HD:(h + 1) * HD], start=True, stop=True)
                        mm.then_inc(u_done.sem, 1)
                        if c:
                            pe.wait_ge(st_ready.sem, st_ready.this(i, 1))
                        wait_apart(pe, u_ready.sem, u_ready.this(i, c + 1), pe_passed)
                        for h in range(NH):
                            q, j = h % 2, h // 2
                            hs = slice(h * HD, (h + 1) * HD)
                            out = bk[7][HD * q:HD * q + HD, j * HD:(j + 1) * HD]
                            pe.matmul(out, b_t[rows, hs], u[rows, hs], start=True, stop=False)
                            mm = pe.matmul(out, z_t[rows, hs], v_t[rows, hs], start=False, stop=True)
                        mm.then_inc(dst_done.sem, 1)
                    for h in range(NH):
                        q, j = h % 2, h // 2
                        hs = slice(h * HD, (h + 1) * HD)
                        out = bk[q][:, j * HD:(j + 1) * HD]
                        pe.matmul(out, sc[:, h, 1, :], u[:, hs], start=False, stop=False, skip_group_check=True)
                        mm = pe.matmul(out, sc[:, h, 3, :], v_t[:, hs], start=False, stop=(j == WT - 1),
                                       skip_group_check=True)
                    mm.then_inc(y_done.sem, 1)
                    pe.wait_ge(ada_loaded.sem, ada_loaded.this(i, 1))
                    pe.wait_ge(akv_ready.sem, akv_ready.this(i, 1))
                    for m in range(2):
                        for k in range(KT):
                            mm = pe.matmul(bk[2][:, m:m + 1], adas[:, k, m * P:(m + 1) * P],
                                           per["silc"][:, k:k + 1], start=(k == 0), stop=(k == KT - 1))
                    mm.then_inc(ada_done.sem, 1)

            @block.scalar
            def _(act):
                for s in (th_ready, sgt_ready, tw_ready, ta_ready, sq_ready, e_ready, rnt_ready, tr_ready, t2_ready,
                          gt_ready, akv_ready, u_ready, y_ready, yq_ready):
                    s.credit(act)
                act.activation(hw0[:, :], vc[:, V_W0:V_W0 + WT], ACT.Copy, scale=0.5)
                act.activation(ha0[:, :], vc[:, V_A0:V_A0 + WT], ACT.Copy, scale=0.5)
                act.wait_ge(init_done, 1)
                with act.Fori(0, NT) as i:
                    act.wait_ge(p_loaded.sem, p_loaded.this(i, 2))
                    act.wait_ge(zw_done.sem, zw_done.last(i, 1))
                    act.activation(th[:, :], pt[0:LORA, RT - 3, :], ACT.Tanh).then_inc(th_ready.sem, 1)
                    act.wait_ge(g_done.sem, g_done.last(i, 1))
                    act.activation(sg[:, 0, :], pt[:, RT - 2, :], ACT.Tanh, scale=0.5)
                    act.activation(sg[0:GLORA - P, 1, :], pt[0:GLORA - P, RT - 1, :], ACT.Tanh,
                                   scale=0.5).then_inc(sgt_ready.sem, 1)
                    act.wait_ge(zw_done.sem, zw_done.this(i, 1))
                    act.wait_ge(l_ready.sem, l_ready.last(i, 1))
                    for j in range(WT):
                        ev = act.activation(f["tw"][:, j, :], bk[0][:, j * P:(j + 1) * P], ACT.Tanh, scale=0.5,
                                            bias=hw0[:, j:j + 1])
                    ev.then_inc(tw_ready.sem, 1)
                    act.wait_ge(za_done.sem, za_done.this(i, 1))
                    act.wait_ge(feats_ready.sem, feats_ready.last(i, 1))
                    for j in range(WT):
                        ev = act.activation(f["ta"][:, j, :], bk[1][:, j * P:(j + 1) * P], ACT.Tanh, scale=0.5,
                                            bias=ha0[:, j:j + 1])
                    ev.then_inc(ta_ready.sem, 1)
                    act.wait_ge(kkr_ready.sem, kkr_ready.this(i, 1))
                    act.wait_ge(ss_done.sem, ss_done.last(i, 1))
                    act.activation(f["sq"][:, :, :], f["kkr"][:, :, :], ACT.Square).then_inc(sq_ready.sem, 1)
                    act.wait_ge(l_ready.sem, l_ready.this(i, 1))
                    act.wait_ge(feats_ready.sem, feats_ready.last(i, 1))
                    act.wait_ge(st_ready.sem, st_ready.last(i, 2))
                    act.activation(f["e1"][:, :, :], f["lc"][:, :, :], ACT.Exp)
                    act.activation(f["e2"][:, :, :], f["lc"][:, :, :], ACT.Exp, scale=-1.0)
                    act.activation(f["e1x"][:, :, :], f["lx"][:, :, :], ACT.Exp).then_inc(e_ready.sem, 1)
                    act.wait_ge(tr_done.sem, tr_done.this(i, 1))
                    act.wait_ge(yo_ready.sem, yo_ready.last(i, 1))
                    act.copy(v_t[:, :], bk[1][:, :]).then_inc(tr_ready.sem, 1)
                    act.wait_ge(rnt_done.sem, rnt_done.this(i, 1))
                    act.wait_ge(rnbc_done.sem, rnbc_done.last(i, 1))
                    act.copy(rnt[:, :], bk[2][0:NH, P:2 * P]).then_inc(rnt_ready.sem, 1)
                    act.wait_ge(dst_done.sem, dst_done.last(i, 2))
                    for n, dst in ((0, b_t), (1, z_t)):
                        act.wait_ge(tr_done.sem, tr_done.this(i, n + 2))
                        act.copy(dst[:, :], bk[n][:, :]).then_inc(tr_ready.sem, 1)
                    for a in range(2):
                        act.wait_ge(t2_done.sem, t2_done.this(i, a + 1))
                        act.copy(tm[:, 4 * a:4 * a + 4, :], bk[6 + a][:, :].rearrange("p (h n) -> p h n", h=4)
                                 ).then_inc(t2_ready.sem, 1)
                    for n in range(2 * LEVELS):
                        a = n % 2
                        act.wait_ge(gt_done.sem, gt_done.this(i, n + 1))
                        act.wait_ge(tgt_done.sem, tgt_done.this(i, n - 1) if n >= 2
                                    else tgt_done.last(i, 2 * LEVELS + n - 1))
                        act.copy(gt[:, 4 * a:4 * a + 4, :], bk[4 + a][:, :].rearrange("p (h n) -> p h n", h=4)
                                 ).then_inc(gt_ready.sem, 1)
                    act.wait_ge(akv_done.sem, akv_done.this(i, 1))
                    act.wait_ge(x_ready.sem, x_ready.last(i, 2))
                    act.copy(akv[:, :], bk[2][:, :]).then_inc(akv_ready.sem, 1)
                    for c in range(2):
                        rows = slice(C * c, C * c + C)
                        act.wait_ge(u_done.sem, u_done.this(i, c + 1))
                        act.wait_ge(y_done.sem, y_done.last(i, 1))
                        act.copy(u[rows, :], bk[6][rows, :]).then_inc(u_ready.sem, 1)
                    act.wait_ge(y_done.sem, y_done.this(i, 1))
                    act.wait_ge(yo_ready.sem, yo_ready.last(i, 1))
                    for q in range(2):
                        ev = act.copy(y[:, :].rearrange("p (j q d) -> p j q d", q=2, d=HD)[:, :, q, :],
                                      bk[q][:, 0:WT * HD].rearrange("p (j d) -> p j d", d=HD))
                    ev.then_inc(y_ready.sem, 1)
                    act.wait_ge(yc_ready.sem, yc_ready.this(i, 1))
                    act.activation(yq[:, :], y[:, :], ACT.Square, scale=HD ** -0.5).then_inc(yq_ready.sem, 1)

            @block.vector
            def _(dve):
                for s in (sg_ready, kkr_ready, l_ready, pr_ready, ssm_ready, kk_ready, feats_ready, bon_ready,
                          score_ready, w2_ready, tw_upd, x_ready, st_ready, yc_ready, var_ready, yo_ready, ada_ready):
                    s.credit(dve)
                dve.wait_ge(once_loaded, 16 * 6)
                dve.wait_ge(init_done, 1)
                tt = dve.tensor_tensor
                with dve.Fori(0, NT) as i:
                    i2 = dve.snap(i * 2)
                    dve.wait_ge(p_loaded.sem, p_loaded.this(i, 2))
                    dve.wait_ge(sq_ready.sem, sq_ready.last(i, 1))
                    tt(f["kkr"][:, :, :], k_, col(V_KK), ALU.mult).then_inc(kkr_ready.sem, 1)
                    dve.wait_ge(sgt_ready.sem, sgt_ready.this(i, 1))
                    dve.tensor_scalar(sg[:, 0, :], sg[:, 0, :], 0.5, 0.5, ALU.mult, ALU.add)
                    dve.tensor_scalar(sg[0:GLORA - P, 1, :], sg[0:GLORA - P, 1, :], 0.5, 0.5, ALU.mult,
                                      ALU.add).then_inc(sg_ready.sem, 1)
                    dve.wait_ge(tw_ready.sem, tw_ready.this(i, 1))
                    dve.wait_ge(e_ready.sem, e_ready.last(i, 1))
                    dve.tensor_scalar(f["nlw"][:, :, :], f["tw"][:, :, :], 0.5 * LOGW, 0.5 * LOGW, ALU.mult, ALU.add)
                    dve.drain()
                    flat = lambda a: a[:, :, :].rearrange("p j n -> p (j n)")
                    dve.tensor_tensor_scan(flat(f["lc"]), per["reset"][:, :], flat(f["nlw"]), 0.0, ALU.mult, ALU.add)
                    dve.drain()
                    tt(f["lx"][:, :, :], f["lc"][:, :, :], f["nlw"][:, :, :], ALU.subtract).then_inc(l_ready.sem, 1)
                    dve.wait_ge(ta_ready.sem, ta_ready.this(i, 1))
                    dve.tensor_scalar(f["ta"][:, :, :], f["ta"][:, :, :], 0.5, 0.5, ALU.mult, ALU.add)
                    dve.drain()
                    dve.scalar_tensor_tensor(f["t1"][:, :, :], f["ta"][:, :, :], -1.0, col(V_KA), ALU.add, ALU.mult)
                    dve.drain()
                    dve.scalar_tensor_tensor(f["kp"][:, :, :], f["t1"][:, :, :], 1.0, k_, ALU.add, ALU.mult)
                    dve.wait_ge(ss_done.sem, ss_done.this(i, 1))
                    dve.wait_ge(rn_ready.sem, rn_ready.last(i, 1))
                    dve.tensor_scalar(ssm[:, :], bk[2][:, 0:NH], 1e-24, None, ALU.max).then_inc(ssm_ready.sem, 1)
                    dve.drain()
                    tt(f["t1"][:, :, :], f["kp"][:, :, :], col(V_RK), ALU.mult)
                    dve.drain()
                    dve.wait_ge(bonus_done.sem, bonus_done.last(i, 1))
                    tt(f["pr"][:, :, :], f["t1"][:, :, :], r_, ALU.mult).then_inc(pr_ready.sem, 1)
                    dve.wait_ge(e_ready.sem, e_ready.this(i, 1))
                    dve.wait_ge(y_done.sem, y_done.last(i, 1))
                    tt(kr[:, :, 1, :], r_, f["e1"][:, :, :], ALU.mult)
                    tt(f["zt"][:, :, :], f["kp"][:, :, :], f["e2"][:, :, :], ALU.mult)
                    dve.wait_ge(rnbc_done.sem, rnbc_done.this(i, 1))
                    tt(f["kk"][:, :, :], f["kkr"][:, :, :], bk[0][:, :].rearrange("p (j n) -> p j n", j=WT), ALU.mult)
                    dve.drain()
                    tt(kr[:, :, 0, :], f["kk"][:, :, :], f["e1x"][:, :, :], ALU.mult)
                    tt(f["bt"][:, :, :], f["kk"][:, :, :], f["ta"][:, :, :], ALU.mult)
                    dve.drain()
                    tt(f["bt"][:, :, :], f["bt"][:, :, :], f["e2"][:, :, :], ALU.mult).then_inc(feats_ready.sem, 1)
                    dve.wait_ge(bonus_done.sem, bonus_done.this(i, 1))
                    dve.tensor_copy(bon[:, :], bk[2][:, 16:16 + NH]).then_inc(bon_ready.sem, 1)
                    for h in range(NH):
                        dve.wait_ge(score_done.sem, score_done.this(i, h + 1))
                        tt(sc[:, h, :, :], bk[4 + h % 2][:, :].rearrange("p (n t) -> p n t", n=4),
                           per["smask"][:, :, :], ALU.mult).then_inc(score_ready.sem, 1)
                    dve.drain()
                    lvl = lambda m, n, heads: per[m][:, n, :].unsqueeze(1).to_broadcast([P, heads, P])
                    tt(wm[:, :, :], sc[:, :, 0, :], lvl("wmask", 0, NH), ALU.mult)
                    dve.drain()
                    tt(wm[:, :, :], wm[:, :, :], ident[:, :].unsqueeze(1).to_broadcast([P, NH, P]),
                       ALU.add).then_inc(w2_ready.sem, 1)
                    for lv in range(LEVELS):
                        for a in range(2):
                            n = 2 * lv + a
                            tb, wb = (bk[6], bk[7]) if a == 0 else (bk[0], bk[1])
                            hs = slice(4 * a, 4 * a + 4)
                            b3 = lambda b: b[:, :].rearrange("p (h n) -> p h n", h=4)
                            wait_apart(dve, tgt_done.sem, tgt_done.this(i, n + 1), dve_passed)
                            if lv < LEVELS - 1:
                                dve.copy_predicated(tm[:, hs, :], lvl("tmask", lv + 1, 4).bitcast(I32), b3(tb))
                            dve.copy_predicated(wm[:, hs, :], lvl("wmask", lv + 1, 4).bitcast(I32),
                                                b3(wb)).then_inc(tw_upd.sem, 1)
                    for c in range(2):
                        rows = slice(C * c, C * c + C)
                        dve.wait_ge(x_done.sem, x_done.this(i, c + 1))
                        dve.wait_ge(akv_ready.sem, akv_ready.this(i, 1))
                        jq = lambda ap: ap.rearrange("p (j q d) -> p j q d", q=2, d=HD)
                        for q in range(2):
                            ev = dve.scalar_tensor_tensor(
                                jq(xn[rows, :])[:, :, q, :], bk[4 + q][rows, 0:WT * HD].rearrange(
                                    "p (j d) -> p j d", d=HD), -1.0, jq(akv[rows, :])[:, :, q, :],
                                ALU.mult, ALU.subtract)
                        ev.then_inc(x_ready.sem, 1)
                        dve.wait_ge(dst_done.sem, dst_done.this(i, c + 1))
                        tt(st[:, 1 - c, :, :], st[:, c, :, :],
                           bk[7][:, 0:WT * HD].rearrange("p (j d) -> p j d", d=HD), ALU.add)
                        dve.drain()
                        end = f["e1"][:, :, C * c + C - 1:C * c + C].to_broadcast([P, WT, HD])
                        tt(st[:, 1 - c, :, :], st[:, 1 - c, :, :], end, ALU.mult).then_inc(st_ready.sem, 1)
                    dve.wait_ge(y_ready.sem, y_ready.this(i, 1))
                    dve.tensor_reduce(gs[:, 0, :], h3(y[:, :]), AX.X, ALU.add)
                    dve.drain()
                    dve.tensor_scalar(gs[:, 0, :], gs[:, 0, :], 1.0 / HD, None, ALU.mult)
                    dve.drain()
                    bc = lambda ap: ap.unsqueeze(2).to_broadcast([P, NH, HD])
                    tt(h3(y[:, :]), h3(y[:, :]), bc(gs[:, 0, :]), ALU.subtract).then_inc(yc_ready.sem, 1)
                    dve.wait_ge(yq_ready.sem, yq_ready.this(i, 1))
                    dve.wait_ge(gr_ready.sem, gr_ready.last(i, 1))
                    dve.tensor_reduce(gs[:, 1, :], h3(yq[:, :]), AX.X, ALU.add)
                    dve.drain()
                    dve.tensor_scalar(gs[:, 1, :], gs[:, 1, :], GN_EPS, None, ALU.add).then_inc(var_ready.sem, 1)
                    dve.wait_ge(gr_ready.sem, gr_ready.this(i, 1))
                    tt(h3(y[:, :]), h3(y[:, :]), bc(gr[:, :]), ALU.mult)
                    dve.drain()
                    tt(y[:, :], y[:, :], gnw[:, 0, :], ALU.mult)
                    tt(h3(yq[:, :]), h3(v_t[:, :]), bc(bon[:, :]), ALU.mult)
                    dve.drain()
                    tt(y[:, :], y[:, :], gnw[:, 1, :], ALU.add)
                    dve.drain()
                    tt(y[:, :], y[:, :], yq[:, :], ALU.add)
                    dve.drain()
                    dve.wait_ge(g_done.sem, g_done.this(i, 1))
                    dve.wait_ge(y_stored.sem, y_stored.last(i, 1))
                    tt(yo[:, :], y[:, :], bk[3][:, :], ALU.mult).then_inc(yo_ready.sem, 1)
                    dve.wait_ge(ada_done.sem, ada_done.this(i, 1))
                    dve.tensor_tensor(per["mod2"][:, ds(i2, 2)], bk[2][:, 0:2], vc[:, ds(i2 + 16, 2)],
                                      ALU.add).then_inc(ada_ready.sem, 1)


def block_fox(nc, io, per, dr):
    ident, oall = per["ident"], per["tiles"]
    KB = 512
    GQ = KB // P
    nb = [t // GQ + 1 for t in range(NT)]
    NSB, NB = 5, sum(nb)
    assert NB % NSB == 0
    first = [sum(nb[:t]) for t in range(NT + 1)]
    tile_of = [t for t in range(NT) for _ in range(nb[t])]
    blocks = [(G, j) for G in range(NG) for j in range(GQ * (G + 1))]
    NBL, LAG = len(blocks), 2
    NPT = LAG + 1
    gfirst = [blocks.index((G, 0)) for G in range(NG)] + [NBL]
    order = [("scores", n) for n in range(first[GQ])]

    def values_of(B):
        order.append(("values", B))
        if B - 1 in gfirst[1:]:
            order.append(("out", blocks[B - 1][0] - 1))

    for G in range(NG):
        ns = range(first[GQ * (G + 1)], first[min(GQ * (G + 2), NT)])
        bs = range(gfirst[G], gfirst[G + 1])
        for i in range(max(len(ns), len(bs))):
            if i * len(bs) // max(len(ns), len(bs)) < (i + 1) * len(bs) // max(len(ns), len(bs)):
                B = bs[0] + i * len(bs) // max(len(ns), len(bs))
                order.append(("turn", B))
                if B >= LAG:
                    values_of(B - LAG)
            if i < len(ns):
                order.append(("scores", ns[i]))
    for B in range(NBL - LAG, NBL):
        values_of(B)
    order.append(("out", NG - 1))
    uses = [(w, i) for w, i in order if w in ("turn", "out")]
    NU = len(uses)
    use = {wi: n for n, wi in enumerate(uses)}
    assert NU % 2 == 0
    with ExitStack() as ctx:
        sb = lambda n, s, d=F32: ctx.enter_context(nc.sbuf_tensor(n, s, d))
        sem = ctx.enter_context(stage_semaphores(nc))
        sig = lambda n, per_turn=1, step=1: Signal(sem(n), per_turn, step)
        k1, k2 = sb("a_k1", [P, 2, T], F32R), sb("a_k2", [P, 2, T], F32R)
        q1, q2 = sb("a_q1", [P, T], F32R), sb("a_q2", [P, T], F32R)
        va = sb("a_v", [P, 2, NT, P], F32R)
        lf = sb("a_lf", [P, NT * NH])
        e1, fneg = sb("a_e1", [P, NT * NH]), sb("a_fneg", [P, NT * NH])
        run = sb("a_run", [P, NT * NH])
        ft = sb("a_ft", [P, 2, P], F32R)
        dmask = sb("a_dmask", [P, P])
        dmask_r, ident_r = sb("a_dmask_r", [P, P], F32R), sb("a_ident_r", [P, P], F32R)
        prs = [sb(f"a_pr{i}", [P, GQ, KB * (NG - 1 + i)]) for i in range(2)]
        pr = lambda t, lo, hi: prs[t // GQ % 2][:, t % GQ, lo:hi]
        pth, ptl = sb("a_pth", [P, NPT, KB], F32R), sb("a_ptl", [P, NPT, KB], F32R)
        ot = sb("a_ot", [P, KB])
        osum = sb("a_osum", [P, GQ, HD])
        mx = sb("a_mx", [P, 4, 4])
        nmx = sb("a_nmx", [P, 2 * GQ])
        rs = sb("a_rs", [P, NT, 4])
        rsum, rinv = sb("a_rsum", [P, GQ]), sb("a_rinv", [P, GQ])
        sbk = [ctx.enter_context(nc.psum_tensor(f"a_s{i}", [P, 512], F32)) for i in range(NSB)]
        tbk = [ctx.enter_context(nc.psum_tensor(f"a_t{i}", [P, 512], F32)) for i in range(2)]
        obk = ctx.enter_context(nc.psum_tensor("a_o", [P, 512], F32))

        consts_ready = sem("a_consts_ready")
        lf_abs, lf_exp, lf_ln, lf_ready = sem("lf_abs"), sem("lf_exp"), sem("lf_ln"), sem("lf_ready")
        cum_done, run_ready, fneg_ready, ft_done, fth_ready, ftl_ready = (
            sem(n) for n in ("cum_done", "run_ready", "fneg_ready", "ft_done", "fth_ready", "ftl_ready"))
        f_stored, mask_split = sem("f_stored"), sem("mask_split")
        kv_loaded = [sig(f"kv_loaded{v}", 6, 16) for v in range(2)]
        q_loaded = [sig(f"q_loaded{G}", 3, 16) for G in range(NG)]
        s_done, max_ready, exp_ready = sig("s_done", NB), sig("max_ready", NT), sig("exp_ready", NB)
        t_done, t_read = sig("t_done", NU), sig("t_read", NU)
        hi_ready, pv_done = sig("hi_ready", NBL), sig("pv_done", NBL)
        ot_ready = sig("ot_ready", NG)

        with nc.Block() as block:
            @block.sync
            def _(sp):
                for s in (*q_loaded, *kv_loaded):
                    s.credit(sp)
                sp.wait_ge(fth_ready, 1)
                sp.wait_ge(ftl_ready, 1)
                sp.dma_start(dr["fneg"].rearrange("c r n -> r c n"), ft[:, :, :].bitcast(F32)).then_inc(f_stored, 16)
                sp.wait_ge(f_stored, 16)
                sp.wait_ge(consts_ready, 4)
                fneg_of = dr["fneg"].rearrange("c (t h) n -> h c t n", h=NH)
                with sp.Fori(0, NH // 2) as u:
                    for v in range(2):
                        h = sp.snap(2 * u + v)
                        row = sp.snap(h * HD)
                        sp.wait_ge(pv_done.sem, pv_done.last(h, 1))
                        for dst, name in ((k1[0:HD, v, :], "kh"), (k1[HD:P, v, :], "kl"), (k2[0:HD, v, :], "kh")):
                            sp.dma_start(dst.bitcast(F32), dr[name][ds(row, HD), :]).then_inc(kv_loaded[v].sem, 16)
                        for c in range(2):
                            sp.dma_start(k2[HD + c:HD + c + 1, v, :].rearrange("o (t n) -> o t n", n=P).bitcast(F32),
                                         fneg_of[ds(h, 1), c, :, :]).then_inc(kv_loaded[v].sem, 16)
                        sp.dma_start(va[:, v, :, :].bitcast(F32), dr["v"][:, ds(row * 2, P)].rearrange("(t p) n -> p t n", p=P)
                                     ).then_inc(kv_loaded[v].sem, 16)
                        for G in range(NG):
                            sp.wait_ge(s_done.sem, s_done.last(h, first[GQ * (G + 1)]))
                            cs = slice(G * KB, (G + 1) * KB)
                            for dst, name in ((q1[0:HD, cs], "qh"), (q1[HD:P, cs], "qh"), (q2[0:HD, cs], "ql")):
                                sp.dma_start(dst.bitcast(F32), dr[name][ds(row, HD), cs]).then_inc(q_loaded[G].sem, 16)

            @block.gpsimd
            def _(pool):
                pool.memset(dmask[:, :], 0.0)
                pool.drain()
                pool.affine_select(out=dmask[:, :], in_=dmask[:, :], compare_op=ALU.is_ge, fill=NEG, base=0,
                                   pattern=[[-1, P]], channel_multiplier=1).then_inc(consts_ready, 1)
                pool.drain()
                pool.memset(k2[HD:P, :, :].bitcast(F32), 0.0).then_inc(consts_ready, 1)
                pool.drain()
                pool.memset(q2[HD:P, :].bitcast(F32), 0.0).then_inc(consts_ready, 1)
                pool.drain()
                pool.memset(q2[HD:HD + 2, :].bitcast(F32), 1.0).then_inc(consts_ready, 1)

            @block.tensor
            def _(pe):
                for s in (s_done, t_done, pv_done):
                    s.credit(pe)
                pe.wait_ge(lf_ready, 1)
                pe.matmul(sbk[0][:, 0:NT * NH], per["tri"][:, :], lf[:, :], start=True, stop=True)
                pe.matmul(sbk[1][:, 0:NT * NH], per["ones"][:, :], lf[:, :], start=True,
                          stop=True).then_inc(cum_done, 1)
                pe.wait_ge(fneg_ready, 1)
                pe.transpose(sbk[2][:, 0:P], fneg[:, :], ident[:, :]).then_inc(ft_done, 1)
                pe.wait_ge(consts_ready, 4)
                pe.wait_ge(ftl_ready, 1)
                pe.wait_ge(mask_split, 1)

                def scores(h, v, n):
                    t, b = tile_of[n], n - first[tile_of[n]]
                    if b == 0 and t % GQ == 0:
                        pe.wait_ge(q_loaded[t // GQ].sem, q_loaded[t // GQ].this(h, 3))
                    pe.wait_ge(exp_ready.sem, exp_ready.this(h, n - NSB + 1) if n >= NSB
                               else exp_ready.last(h, NB + n - NSB + 1))
                    width = min(KB, (t + 1) * P - b * KB)
                    out = sbk[n % NSB][:, 0:width]
                    pe.matmul(out, q1[:, t * P:(t + 1) * P], k1[:, v, b * KB:b * KB + width], start=True, stop=False,
                              skip_group_check=True)
                    mm = pe.matmul(out, q2[:, t * P:(t + 1) * P], k2[:, v, b * KB:b * KB + width], start=False,
                                   stop=(b < nb[t] - 1), skip_group_check=True)
                    if b == nb[t] - 1:
                        mm = pe.matmul(sbk[n % NSB][:, width - P:width], ident_r[:, :], dmask_r[:, :], start=False,
                                       stop=True, skip_group_check=True)
                    mm.then_inc(s_done.sem, 1)

                def bank_read(h, n):
                    pe.wait_ge(t_read.sem, t_read.this(h, n - 1) if n >= 2 else t_read.last(h, NU + n - 1))

                def turn(h, B):
                    G, j = blocks[B]
                    n = use["turn", B]
                    pe.wait_ge(exp_ready.sem, exp_ready.this(h, first[GQ * G + GQ - 1] + j // GQ + 1))
                    bank_read(h, n)
                    for m in range(max(0, j - GQ * G), GQ):
                        mm = pe.transpose(tbk[n % 2][:, m * P:(m + 1) * P],
                                          pr(GQ * G + m, j * P, (j + 1) * P), ident[:, :])
                    mm.then_inc(t_done.sem, 1)

                def values(h, v, B):
                    G, j = blocks[B]
                    lo = max(0, j - GQ * G) * P
                    if j == 0:
                        pe.wait_ge(ot_ready.sem, ot_ready.this(h, G))
                    pe.wait_ge(t_read.sem, t_read.this(h, use["turn", B] + 1))
                    pe.matmul(obk[:, lo:KB], va[:, v, j, :], pth[:, B % NPT, lo:KB], start=(j == 0), stop=False,
                              skip_group_check=True)
                    pe.matmul(obk[:, lo:KB], va[:, v, j, :], ptl[:, B % NPT, lo:KB], start=False,
                              stop=(B + 1 in gfirst), skip_group_check=True).then_inc(pv_done.sem, 1)

                def out(h, G):
                    n = use["out", G]
                    pe.wait_ge(ot_ready.sem, ot_ready.this(h, G + 1))
                    bank_read(h, n)
                    for m in range(GQ):
                        mm = pe.transpose(tbk[n % 2][:, m * P:(m + 1) * P], ot[:, m * P:(m + 1) * P], ident[:, :])
                    mm.then_inc(t_done.sem, 1)

                with pe.Fori(0, NH // 2) as u:
                    for v in range(2):
                        h = pe.snap(2 * u + v)
                        pe.wait_ge(kv_loaded[v].sem, kv_loaded[v].this(u, 6))
                        for what, n in order:
                            if what == "scores":
                                scores(h, v, n)
                            elif what == "turn":
                                turn(h, n)
                            elif what == "values":
                                values(h, v, n)
                            else:
                                out(h, n)

            @block.scalar
            def _(act):
                for s in (exp_ready, hi_ready, ot_ready):
                    s.credit(act)
                act.wait_ge(lf_abs, 1)
                act.activation(e1[:, :], e1[:, :], ACT.Exp, scale=-1.0).then_inc(lf_exp, 1)
                act.wait_ge(lf_exp, 1)
                act.activation(e1[:, :], e1[:, :], ACT.Ln, bias=per["ones"][:, 0:1]).then_inc(lf_ln, 1)
                act.wait_ge(ft_done, 1)
                act.copy(ft[:, 0, :], sbk[2][:, 0:P]).then_inc(fth_ready, 1)

                def exp(h, n):
                    t, b = tile_of[n], n - first[tile_of[n]]
                    if b == 0:
                        act.wait_ge(max_ready.sem, max_ready.this(h, t + 1))
                        if t % GQ == 0:
                            G = t // GQ
                            act.wait_ge(t_done.sem, t_done.this(h, use["turn", gfirst[G - 1] - 1] + 1) if G >= 2
                                        else t_done.last(h, use["turn", gfirst[G + 3] - 1] + 1))
                            act.wait_ge(t_read.sem, t_read.last(h, use["out", G] + 1))
                    width = min(KB, (t + 1) * P - b * KB)
                    s = t % (2 * GQ)
                    act.activation(pr(t, b * KB, b * KB + width), sbk[n % NSB][:, 0:width], ACT.Exp,
                                   bias=nmx[:, s:s + 1], accum_out=rs[:, t, b:b + 1]).then_inc(exp_ready.sem, 1)

                def hi(h, B):
                    G, j = blocks[B]
                    lo = max(0, j - GQ * G) * P
                    n = use["turn", B]
                    act.wait_ge(t_done.sem, t_done.this(h, n + 1))
                    act.wait_ge(pv_done.sem, pv_done.this(h, B + 1 - NPT) if B >= NPT
                                else pv_done.last(h, NBL + B + 1 - NPT))
                    act.copy(pth[:, B % NPT, lo:KB], tbk[n % 2][:, lo:KB]).then_inc(hi_ready.sem, 1)

                def out_copy(h, G):
                    act.wait_ge(pv_done.sem, pv_done.this(h, gfirst[G + 1]))
                    act.wait_ge(t_done.sem, t_done.this(h, use["out", G - 1] + 1) if G else t_done.last(h, NU))
                    act.copy(ot[:, :], obk[:, :]).then_inc(ot_ready.sem, 1)

                with act.Fori(0, NH) as h:
                    done = seen = 0
                    for what, n in order:
                        if what == "scores":
                            if n + 1 == first[GQ]:
                                while done <= n:
                                    exp(h, done)
                                    done += 1
                        elif what == "turn":
                            G, j = blocks[n]
                            while done <= first[GQ * G + GQ - 1] + j // GQ:
                                exp(h, done)
                                done += 1
                            if done < first[seen]:
                                exp(h, done)
                                done += 1
                            hi(h, n)
                        elif what == "values" and n + 1 in gfirst:
                            out_copy(h, blocks[n][0])
                        if what == "scores" and done < first[seen] and first[seen] - done > 3:
                            exp(h, done)
                            done += 1
                        if what == "scores":
                            seen = tile_of[n] + (n + 1 == first[tile_of[n] + 1])

            @block.vector
            def _(dve):
                for s in (max_ready, t_read):
                    s.credit(dve)
                fr = per["fraw"][:, :, :].rearrange("p t h -> p (t h)")
                dve.tensor_scalar(lf[:, :], fr, -1.0, None, ALU.mult)
                dve.drain()
                dve.tensor_tensor(e1[:, :], lf[:, :], fr, ALU.max).then_inc(lf_abs, 1)
                dve.drain()
                dve.tensor_scalar(lf[:, :], fr, 0.0, None, ALU.min)
                dve.drain()
                dve.wait_ge(lf_ln, 1)
                dve.tensor_tensor(lf[:, :], lf[:, :], e1[:, :], ALU.subtract).then_inc(lf_ready, 1)
                dve.wait_ge(cum_done, 1)
                dve.memset(run[:, 0:NH], 0.0)
                for t in range(1, NT):
                    dve.drain()
                    dve.tensor_tensor(run[:, t * NH:(t + 1) * NH], run[:, (t - 1) * NH:t * NH],
                                      sbk[1][:, (t - 1) * NH:t * NH], ALU.add)
                dve.drain()
                dve.scalar_tensor_tensor(fneg[:, :], sbk[0][:, 0:NT * NH], -1.0, run[:, :], ALU.mult,
                                         ALU.subtract).then_inc(fneg_ready, 1)
                dve.wait_ge(fth_ready, 1)
                dve.tensor_tensor(ft[:, 1, :], sbk[2][:, 0:P], ft[:, 0, :].bitcast(F32), ALU.subtract
                                  ).then_inc(ftl_ready, 1)
                dve.wait_ge(consts_ready, 4)
                dve.tensor_copy(dmask_r[:, :], dmask[:, :])
                dve.tensor_copy(ident_r[:, :], ident[:, :]).then_inc(mask_split, 1)

                def maximum(h, n):
                    t, b = tile_of[n], n - first[tile_of[n]]
                    width = min(KB, (t + 1) * P - b * KB)
                    dve.wait_ge(s_done.sem, s_done.this(h, n + 1))
                    if b < nb[t] - 1:
                        dve.tensor_reduce(mx[:, t % 4, b:b + 1], sbk[n % NSB][:, 0:width], AX.X, ALU.max)
                    else:
                        s = t % (2 * GQ)
                        if nb[t] == 1:
                            dve.wait_ge(exp_ready.sem, exp_ready.last(h, first[NT + t - 7]))
                            dve.tensor_reduce(nmx[:, s:s + 1], sbk[n % NSB][:, 0:width], AX.X, ALU.max,
                                              negate=True).then_inc(max_ready.sem, 1)
                            return
                        dve.tensor_reduce(mx[:, t % 4, b:b + 1], sbk[n % NSB][:, 0:width], AX.X, ALU.max)
                        dve.drain()
                        dve.wait_ge(exp_ready.sem, exp_ready.this(h, first[t - 7]) if t >= 8
                                    else exp_ready.last(h, first[NT + t - 7]))
                        dve.tensor_reduce(nmx[:, s:s + 1], mx[:, t % 4, 0:nb[t]], AX.X, ALU.max,
                                          negate=True).then_inc(max_ready.sem, 1)

                def lo_part(h, B):
                    G, j = blocks[B]
                    lo = max(0, j - GQ * G) * P
                    dve.wait_ge(hi_ready.sem, hi_ready.this(h, B + 1))
                    dve.tensor_tensor(ptl[:, B % NPT, lo:KB], tbk[use["turn", B] % 2][:, lo:KB],
                                      pth[:, B % NPT, lo:KB].bitcast(F32), ALU.subtract).then_inc(t_read.sem, 1)

                def out(h, G):
                    n = use["out", G]
                    dve.tensor_reduce(rsum[:, :], rs[:, GQ * G:GQ * (G + 1), 0:G + 1], AX.X, ALU.add)
                    dve.drain()
                    dve.reciprocal(rinv[:, :], rsum[:, :])
                    dve.wait_ge(t_done.sem, t_done.this(h, n + 1))
                    both = tbk[n % 2][:, :].rearrange("p (t c d) -> p t c d", t=GQ, c=2)
                    dve.tensor_copy(osum[:, :, :], both[:, :, 0, :])
                    dve.drain()
                    dve.tensor_tensor(osum[:, :, :], osum[:, :, :], both[:, :, 1, :], ALU.add)
                    dve.drain()
                    dve.tensor_tensor(oall[:, GQ * G:GQ * (G + 1), ds(h * HD, HD)], osum[:, :, :],
                                      rinv[:, :].unsqueeze(2).to_broadcast([P, GQ, HD]),
                                      ALU.mult).then_inc(t_read.sem, 1)

                with dve.Fori(0, NH) as h:
                    low = 0
                    for what, n in order:
                        if what == "scores":
                            maximum(h, n)
                            continue
                        if what == "turn":
                            while low < n:
                                lo_part(h, low)
                                low += 1
                        elif what == "out":
                            while use.get(("turn", low), NU) < use["out", n]:
                                lo_part(h, low)
                                low += 1
                            out(h, n)
                        elif n >= NBL - LAG:
                            while low < NBL:
                                lo_part(h, low)
                                low += 1


def block_out_proj(nc, io, per, dr):
    ident, vc = per["ident"], per["vc"]
    oall = per["tiles"]
    with ExitStack() as ctx:
        sb = lambda n, s, d=F32: ctx.enter_context(nc.sbuf_tensor(n, s, d))
        sem = ctx.enter_context(stage_semaphores(nc))
        sig = lambda n, per_turn=1, step=1: Signal(sem(n), per_turn, step)
        wo = sb("o_wo", [P, KT, D])
        fg = sb("o_fg", [P, W])
        g1 = sb("o_g1", [P, D])
        gcol = sb("o_gcol", [P, 2, KT, P])
        yc = sb("o_yc", [P, D])
        og = sb("o_og", [P, W])
        sg = sb("o_sg", [P, W])
        xt = sb("o_xt", [P, D])
        fq = sb("o_fq", [P, W])
        fs, fr = sb("o_fs", [P, NH]), sb("o_fr", [P, NH])
        yt = sb("o_yt", [P, KT, P])
        h2 = sb("o_h2", [P, D])
        junk = sb("o_junk", [P, D])
        xn = sb("o_xn", [P, D])
        u2 = sb("o_u2", [P, KT, P])
        hs, hr = sb("o_hs", [P, 1]), sb("o_hr", [P, 1])
        bk = [ctx.enter_context(nc.psum_tensor(f"o_b{i}", [P, 512], F32)) for i in range(8)]

        act_passed, sp_passed = sem("o_act_passed"), sem("o_sp_passed")
        wo_loaded, fg_loaded = sem("wo_loaded"), sem("fg_loaded")
        gcol_ready, gbc_done = sem("gcol_ready"), sem("gbc_done")
        yr_loaded, og_loaded, x_loaded = (sig(n, 1, 16) for n in ("o_yr_loaded", "o_og_loaded", "o_x_loaded"))
        h2_stored, u2_stored = sig("h2_stored", 1, 16), sig("u2_stored", 1, 16)
        sg_ready, fq_ready, fs_ready, fr_ready = (sig(n) for n in ("o_sg_ready", "o_fq_ready", "o_fs_ready",
                                                                  "o_fr_ready"))
        yc_ready, yt_done, mm_done, h2_ready = sig("o_yc_ready"), sig("yt_done"), sig("o_mm_done"), sig("h2_ready")
        yt_act, yt_dve = sig("yt_act"), sig("yt_dve")
        hs_ready, hr_ready, xn_ready = sig("o_hs_ready"), sig("o_hr_ready"), sig("o_xn_ready")
        ut_done, ut_act, ut_dve = sig("o_ut_done"), sig("o_ut_act"), sig("o_ut_dve")
        h3 = lambda ap: ap.rearrange("p (h d) -> p h d", h=NH)
        bc = lambda ap: ap.unsqueeze(2).to_broadcast([P, NH, HD])

        with nc.Block() as block:
            @block.sync
            def _(sp):
                for s in (yr_loaded, og_loaded, x_loaded, h2_stored, u2_stored):
                    s.credit(sp)
                sp.dma_start(fg[:, :], io["fox_out_g"].partition_broadcast(P)).then_inc(fg_loaded, 16)
                sp.dma_start(wo[:, :, :], io["w_o"].rearrange("(k p) n -> p k n", p=P)).then_inc(wo_loaded, 16)
                with sp.Fori(0, NT) as t:
                    t0 = sp.snap(t * P)
                    sp.wait_ge(fr_ready.sem, fr_ready.last(t, 1))
                    sp.wait_ge(yc_ready.sem, yc_ready.last(t, 1))
                    sp.dma_start(og[:, :], dr["og"][ds(t0, P), :]).then_inc(og_loaded.sem, 16)
                    sp.wait_ge(yt_done.sem, yt_done.last(t, 1))
                    sp.dma_start(yc[:, 0:W], dr["yrw"][ds(t0, P), :]).then_inc(yr_loaded.sem, 16)
                    sp.wait_ge(h2_ready.sem, h2_ready.last(t, 1))
                    sp.dma_start(xt[:, :], io["x"][0, ds(t0, P), :]).then_inc(x_loaded.sem, 16)
                    sp.wait_ge(h2_ready.sem, h2_ready.this(t, 1))
                    sp.dma_start(dr["h2"][ds(t0, P), :], h2[:, :]).then_inc(h2_stored.sem, 16)
                    sp.wait_ge(ut_act.sem, ut_act.this(t, 1))
                    wait_apart(sp, ut_dve.sem, ut_dve.this(t, 1), sp_passed)
                    sp.dma_start(dr["u2t"][:, ds(t0, P)].rearrange("(k p) n -> p k n", p=P), u2[:, :, :]
                                 ).then_inc(u2_stored.sem, 16)
                sp.wait_ge(h2_stored.sem, h2_stored.this(NT - 1, 1))
                sp.wait_ge(u2_stored.sem, u2_stored.this(NT - 1, 1))

            @block.gpsimd
            def _(pool):
                fr_ready.credit(pool)
                hr_ready.credit(pool)
                with pool.Fori(0, NT) as t:
                    pool.wait_ge(fs_ready.sem, fs_ready.this(t, 1))
                    pool.tensor_tensor(fr[:, :], fs[:, :], per["eps"][:, :], ALU.add)
                    pool.drain()
                    pool.tensor_tensor(fr[:, :], fr[:, :], per["mhalf"][:, :], ALU.pow).then_inc(fr_ready.sem, 1)
                    pool.wait_ge(hs_ready.sem, hs_ready.this(t, 1))
                    pool.tensor_tensor(hr[:, :], hs[:, :], per["eps"][:, 0:1], ALU.add)
                    pool.drain()
                    pool.tensor_tensor(hr[:, :], hr[:, :], per["mhalf"][:, 0:1], ALU.pow).then_inc(hr_ready.sem, 1)

            @block.tensor
            def _(pe):
                for s in (yt_done, mm_done, ut_done):
                    s.credit(pe)
                pe.wait_ge(gcol_ready, 1)
                for n in range(2):
                    for k in range(KT):
                        mm = pe.matmul(bk[2 * n + k // 4][:, (k % 4) * P:(k % 4 + 1) * P], gcol[:, n, k, :],
                                       ident[:, :], start=True, stop=True)
                mm.then_inc(gbc_done, 1)
                pe.wait_ge(h2_ready.sem, 1)
                pe.wait_ge(wo_loaded, 16)
                with pe.Fori(0, NT) as t:
                    pe.wait_ge(yc_ready.sem, yc_ready.this(t, 1))
                    pe.wait_ge(yt_act.sem, yt_act.last(t, 1))
                    pe.wait_ge(yt_dve.sem, yt_dve.last(t, 1))
                    for k in range(KT):
                        mm = pe.transpose(bk[k // 4][:, (k % 4) * P:(k % 4 + 1) * P], yc[:, k * P:(k + 1) * P],
                                          ident[:, :])
                    mm.then_inc(yt_done.sem, 1)
                    pe.wait_ge(yt_act.sem, yt_act.this(t, 1))
                    pe.wait_ge(yt_dve.sem, yt_dve.this(t, 1))
                    pe.wait_ge(h2_ready.sem, h2_ready.last(t, 1))
                    for n in range(2):
                        for k in range(KT):
                            mm = pe.matmul(bk[2 + n][:, :], yt[:, k, :], wo[:, k, n * 512:(n + 1) * 512],
                                           start=(k == 0), stop=(k == KT - 1))
                    mm.then_inc(mm_done.sem, 1)
                    pe.wait_ge(xn_ready.sem, xn_ready.this(t, 1))
                    pe.wait_ge(ut_act.sem, ut_act.last(t, 1))
                    pe.wait_ge(ut_dve.sem, ut_dve.last(t, 1))
                    for k in range(KT):
                        mm = pe.transpose(bk[4 + k // 4][:, (k % 4) * P:(k % 4 + 1) * P], xn[:, k * P:(k + 1) * P],
                                          ident[:, :])
                    mm.then_inc(ut_done.sem, 1)

            @block.scalar
            def _(act):
                for s in (sg_ready, fq_ready, yt_act, hs_ready, ut_act):
                    s.credit(act)
                with act.Fori(0, NT) as t:
                    wait_apart(act, fs_ready.sem, fs_ready.last(t, 1), act_passed)
                    act.activation(fq[:, :].unsqueeze(1), oall[:, ds(t, 1), 0:W], ACT.Square,
                                   scale=HD ** -0.5).then_inc(fq_ready.sem, 1)
                    act.wait_ge(og_loaded.sem, og_loaded.this(t, 1))
                    act.wait_ge(yc_ready.sem, yc_ready.last(t, 1))
                    act.activation(sg[:, :], og[:, :], ACT.Tanh, scale=0.5).then_inc(sg_ready.sem, 1)
                    act.wait_ge(yt_done.sem, yt_done.this(t, 1))
                    act.wait_ge(mm_done.sem, mm_done.last(t, 1))
                    act.copy(yt[:, 0:4, :], bk[0][:, :].rearrange("p (k n) -> p k n", k=4)).then_inc(yt_act.sem, 1)
                    act.wait_ge(h2_ready.sem, h2_ready.this(t, 1))
                    act.wait_ge(hr_ready.sem, hr_ready.last(t, 1))
                    act.activation(junk[:, :], h2[:, :], ACT.Square, scale=D ** -0.5,
                                   accum_out=hs[:, :]).then_inc(hs_ready.sem, 1)
                    act.wait_ge(u2_stored.sem, u2_stored.last(t, 1))
                    act.wait_ge(ut_done.sem, ut_done.this(t, 1))
                    for k in range(4):
                        ev = act.activation(u2[:, k, :], bk[4][:, k * P:(k + 1) * P], ACT.Identity,
                                            bias=per["mod2"][:, 8 + k:9 + k], scale=per["nscale2"][:, k:k + 1])
                    ev.then_inc(ut_act.sem, 1)

            @block.vector
            def _(dve):
                for s in (fs_ready, yc_ready, yt_dve, xn_ready, ut_dve):
                    s.credit(dve)
                tt = dve.tensor_tensor
                dve.scalar_tensor_tensor(per["nscale2"][:, :], per["mod2"][:, 16:24], 1.0, vc[:, V_G2:V_G2 + 8],
                                         ALU.add, ALU.mult)
                for n, at in ((0, 0), (1, 24)):
                    ev = dve.tensor_copy(gcol[:, n, :, :], per["mod2"][:, at:at + 8].unsqueeze(2).to_broadcast(
                        [P, KT, P]))
                    dve.drain()
                dve.sem_inc(gcol_ready, 1)
                dve.wait_ge(gbc_done, 1)
                for n, dst in ((0, g1[:, :]), (1, per["g2row"][:, :])):
                    for m in range(2):
                        dve.tensor_copy(dst[:, m * 512:(m + 1) * 512], bk[2 * n + m][:, :])
                dve.drain()
                h2_ready.credit(dve)
                dve.wait_ge(fg_loaded, 16)
                with dve.Fori(0, NT) as t:
                    dve.wait_ge(fq_ready.sem, fq_ready.this(t, 1))
                    dve.wait_ge(fr_ready.sem, fr_ready.last(t, 1))
                    dve.tensor_reduce(fs[:, :], h3(fq[:, :]), AX.X, ALU.add).then_inc(fs_ready.sem, 1)
                    dve.wait_ge(sg_ready.sem, sg_ready.this(t, 1))
                    dve.tensor_scalar(sg[:, :], sg[:, :], 0.5, 0.5, ALU.mult, ALU.add)
                    dve.drain()
                    tt(sg[:, :], sg[:, :], fg[:, :], ALU.mult)
                    dve.wait_ge(fr_ready.sem, fr_ready.this(t, 1))
                    dve.wait_ge(yt_done.sem, yt_done.last(t, 1))
                    tt(h3(yc[:, W:D]), oall[:, ds(t, 1), 0:W].rearrange("p o (h d) -> p (o h) d", h=NH),
                       bc(fr[:, :]), ALU.mult)
                    dve.drain()
                    dve.wait_ge(yr_loaded.sem, yr_loaded.this(t, 1))
                    tt(yc[:, W:D], yc[:, W:D], sg[:, :], ALU.mult).then_inc(yc_ready.sem, 1)
                    dve.wait_ge(yt_done.sem, yt_done.this(t, 1))
                    dve.wait_ge(mm_done.sem, mm_done.last(t, 1))
                    dve.tensor_copy(yt[:, 4:8, :], bk[1][:, :].rearrange("p (k n) -> p k n", k=4)
                                    ).then_inc(yt_dve.sem, 1)
                    dve.wait_ge(mm_done.sem, mm_done.this(t, 1))
                    dve.wait_ge(h2_stored.sem, h2_stored.last(t, 1))
                    dve.wait_ge(hs_ready.sem, hs_ready.last(t, 1))
                    for n in range(2):
                        cs = slice(n * 512, (n + 1) * 512)
                        tt(h2[:, cs], bk[2 + n][:, :], g1[:, cs], ALU.mult)
                    dve.drain()
                    dve.wait_ge(x_loaded.sem, x_loaded.this(t, 1))
                    tt(h2[:, :], h2[:, :], xt[:, :], ALU.add).then_inc(h2_ready.sem, 1)
                    dve.drain()
                    dve.wait_ge(hr_ready.sem, hr_ready.this(t, 1))
                    dve.wait_ge(ut_done.sem, ut_done.last(t, 1))
                    dve.tensor_scalar(xn[:, :], h2[:, :], hr[:, 0:1], None, ALU.mult).then_inc(xn_ready.sem, 1)
                    dve.wait_ge(u2_stored.sem, u2_stored.last(t, 1))
                    dve.wait_ge(ut_done.sem, ut_done.this(t, 1))
                    for k in range(4, 8):
                        ev = dve.tensor_scalar(u2[:, k, :], bk[5][:, (k - 4) * P:(k - 3) * P],
                                               per["nscale2"][:, k:k + 1], per["mod2"][:, 8 + k:9 + k],
                                               ALU.mult, ALU.add)
                    ev.then_inc(ut_dve.sem, 1)


def block_mlp(nc, io, per, dr):
    FC = 256
    CW = KT * FC
    N1, N2 = FF // FC, FF // 512
    FT, FH = FF // P, FC // P
    NW = N1 + 2 * N2
    CH, AHEAD = NW + 2, 4
    HR, PB = 3, 4
    assert CH % 2 == 0
    with ExitStack() as ctx:
        sb = lambda n, s, d=F32: ctx.enter_context(nc.sbuf_tensor(n, s, d))
        sem = ctx.enter_context(stage_semaphores(nc))
        sig = lambda n, per_turn=1, step=1: Signal(sem(n), per_turn, step)
        raw = sb("m_raw", [P, 2, CW])
        wh, wl = sb("m_wh", [P, 2, CW], F32R), sb("m_wl", [P, 2, CW], F32R)
        uh, ul = sb("m_uh", [P, KT, GT], F32R), sb("m_ul", [P, KT, GT], F32R)
        hid = sb("m_hid", [P, FT, GT])
        hh, hl = sb("m_hh", [P, HR, GT], F32R), sb("m_hl", [P, HR, GT], F32R)
        rl = sb("m_rl", [P, PB, GT])
        h3 = sb("m_h3", [P, GS, D])
        tmp = sb("m_tmp", [P, 2, 512])
        junk = sb("m_junk", [P, D])
        fgr = sb("m_fgr", [P, D])
        hs, hr = sb("m_hs", [P, GS]), sb("m_hr", [P, GS])
        bk = [ctx.enter_context(nc.psum_tensor(f"m_b{i}", [P, 512], F32)) for i in range(8)]
        down_banks = ([bk[2], bk[3], bk[0], bk[1]], bk[4:8])
        fg_loaded, sp_passed = sem("m_fg_loaded"), sem("m_sp_passed")
        raw_loaded = [sig(f"raw_loaded{r}", CH // 2, 16) for r in range(2)]
        w_hi, w_split = sig("w_hi", CH), sig("w_split", CH)
        h2_loaded, out_stored = sig("m_h2_loaded", 1, 16), sig("out_stored", GS, 16)
        up_done, rl_ready, hid_ready = sig("up_done", FT), sig("rl_ready", FT), sig("hid_ready", FT)
        hid_hi, hid_split, hid_used = sig("hid_hi", 2 * FT), sig("hid_split", 2 * FT), sig("hid_used", 2 * FT)
        down_ev = sig("down_ev", 2)
        hs_ready, hr_ready, out_ready = sig("m_hs_ready", GS), sig("m_hr_ready", GS), sig("m_out_ready", GS)

        def split_slots(L):
            if L % CH in (NW - 2, NW - 1):
                i = L % CH - (NW - 2)
                return tuple(u[:, 4 * i:4 * i + 4, :].rearrange("p k n -> p (k n)") for u in (uh, ul))
            return wh[:, L % 2, :], wl[:, L % 2, :]

        def splits_of(c):
            return (c,) if c < NW - 2 else (NW - 2, NW - 1) if c == NW - 2 else (NW,)

        def hidden_of(c):
            m = 4 * (c - N1)
            return range(m + 2 if m else 0, min(m + 6, 2 * FT))

        with nc.Block() as block:
            @block.sync
            def _(sp):
                raw_loaded[0].credit(sp, AHEAD // 2)
                raw_loaded[1].credit(sp, AHEAD // 2)
                h2_loaded.credit(sp)

                def load(g, L, group):
                    if L >= 2 - AHEAD:
                        wait_apart(sp, w_split.sem, w_split.this(g, L - 1), sp_passed)
                    slot = raw[:, L % 2, :]
                    if L % CH in (NW - 2, NW - 1):
                        i = L % CH - (NW - 2)
                        src = dr["u2t"][i * 512:(i + 1) * 512, group].rearrange("(k p) n -> p k n", p=P)
                        slot = slot.rearrange("p (k n) -> p k n", k=4)
                    else:
                        c = (L + 2) % CH
                        if c < N1:
                            src = io["w_mlp1"][:, c * FC:(c + 1) * FC].rearrange("(k p) n -> p k n", p=P)
                            slot = slot.rearrange("p (k n) -> p k n", k=KT)
                        else:
                            half, m = divmod(c - N1, N2)
                            src = io["w_mlp2"][m * 512:(m + 1) * 512, half * 512:(half + 1) * 512].rearrange(
                                "(f p) n -> p f n", p=P)
                            slot = slot.rearrange("p (f n) -> p f n", f=4)
                    sp.dma_start(slot, src).then_inc(raw_loaded[L % 2].sem, 16)

                for L in range(-AHEAD, 0):
                    load(0, L, slice(0, GT))
                with sp.Fori(0, NG) as g:
                    t0 = sp.snap(g * GT)
                    t1 = sp.snap((g + 1) % NG * GT)
                    for L in range(CH):
                        load(g, L, ds(t1, GT))
                        if L == N1:
                            wait_apart(sp, out_stored.sem, out_stored.last(g, GS), sp_passed)
                            sp.dma_start(h3[:, :, :], dr["h2"][ds(t0, GT), :].rearrange("(s p) n -> p s n", p=P)
                                         ).then_inc(h2_loaded.sem, 16)
                for r in raw_loaded:
                    sp.wait_ge(r.sem, r.this(NG - 1, CH // 2))

            @block.gpsimd
            def _(pool):
                hr_ready.credit(pool)
                with pool.Fori(0, NG) as g:
                    for s in range(GS):
                        pool.wait_ge(hs_ready.sem, hs_ready.this(g, s + 1))
                        pool.tensor_tensor(hr[:, s:s + 1], hs[:, s:s + 1], per["eps"][:, 0:1], ALU.add)
                        pool.drain()
                        pool.tensor_tensor(hr[:, s:s + 1], hr[:, s:s + 1], per["mhalf"][:, 0:1],
                                           ALU.pow).then_inc(hr_ready.sem, 1)

            @block.tensor
            def _(pe):
                up_done.credit(pe)
                hid_used.credit(pe)
                with pe.Fori(0, NG) as g:
                    for c in range(N1):
                        pe.wait_ge(w_split.sem, w_split.this(g, c - 1))
                        w1h, w1l = (w[:, c % 2, :].rearrange("p (k n) -> p k n", k=KT) for w in (wh, wl))
                        for m in range(FH):
                            f = c * FH + m
                            pe.wait_ge(rl_ready.sem, rl_ready.this(g, f + 1 - PB))
                            if f == 0:
                                pe.wait_ge(down_ev.sem, down_ev.last(g, 1))
                            cs = slice(m * P, (m + 1) * P)
                            for k in range(KT):
                                pe.matmul(bk[f % PB][:, :], w1h[:, k, cs], uh[:, k, :], start=(k == 0), stop=False)
                                pe.matmul(bk[f % PB][:, :], w1h[:, k, cs], ul[:, k, :], start=False, stop=False)
                                mm = pe.matmul(bk[f % PB][:, :], w1l[:, k, cs], uh[:, k, :], start=False,
                                               stop=(k == KT - 1))
                            mm.then_inc(up_done.sem, 1)
                    pe.wait_ge(rl_ready.sem, rl_ready.this(g, FT))
                    for half in range(2):
                        banks = down_banks[half]
                        if half:
                            pe.wait_ge(down_ev.sem, down_ev.last(g, 2))
                        for m in range(N2):
                            c = N1 + half * N2 + m
                            pe.wait_ge(w_split.sem, w_split.this(g, c - 1))
                            w2h, w2l = (w[:, c % 2, :].rearrange("p (f n) -> p f n", f=4) for w in (wh, wl))
                            for fi in range(4):
                                F = FT * half + 4 * m + fi
                                pe.wait_ge(hid_split.sem, hid_split.this(g, F + 1))
                                first, last = F % FT == 0, F % FT == FT - 1
                                for s in range(GS):
                                    cs = slice(s * P, (s + 1) * P)
                                    pe.matmul(banks[s][:, :], hh[:, F % HR, cs], w2h[:, fi, :], start=first, stop=False)
                                    pe.matmul(banks[s][:, :], hh[:, F % HR, cs], w2l[:, fi, :], start=False, stop=False)
                                    mm = pe.matmul(banks[s][:, :], hl[:, F % HR, cs], w2h[:, fi, :], start=False,
                                                   stop=last)
                                mm.then_inc(hid_used.sem, 1)

            @block.scalar
            def _(act):
                for s in (rl_ready, hid_hi, hs_ready, out_stored):
                    s.credit(act)
                w_hi.credit(act, AHEAD)
                act.dma_start(fgr[:, :], io["final_g"].partition_broadcast(P)).then_inc(fg_loaded, 16)

                def split(g, L):
                    act.wait_ge(raw_loaded[L % 2].sem, raw_loaded[L % 2].this(g, L // 2 + 1))
                    if L >= 0:
                        c = L if L < NW - 2 else N1 - 1 if L < NW else L - 2
                        if c < N1:
                            act.wait_ge(up_done.sem, up_done.this(g, FH * (c + 1)))
                        else:
                            act.wait_ge(hid_used.sem, hid_used.this(g, 4 * (c - N1 + 1)))
                    act.copy(split_slots(L)[0], raw[:, L % 2, :]).then_inc(w_hi.sem, 1)

                for L in range(-AHEAD, 0):
                    split(0, L)
                with act.Fori(0, NG) as g:
                    t0 = act.snap(g * GT)
                    ts = [act.snap(t0 + s * P) for s in range(GS)]
                    for c in range(NW):
                        for f in range(FH * c, FH * (c + 1)) if c < N1 else ():
                            act.wait_ge(up_done.sem, up_done.this(g, f + 1))
                            act.wait_ge(hid_ready.sem, hid_ready.this(g, f + 1 - PB))
                            act.activation(rl[:, f % PB, :], bk[f % PB][:, :], ACT.Relu).then_inc(rl_ready.sem, 1)
                        for F in hidden_of(c) if c >= N1 else ():
                            if F < FT:
                                act.wait_ge(hid_ready.sem, hid_ready.this(g, F + 1))
                            act.wait_ge(hid_used.sem, hid_used.this(g, F + 1 - HR))
                            act.copy(hh[:, F % HR, :], hid[:, F % FT, :]).then_inc(hid_hi.sem, 1)
                        for L in splits_of(c):
                            split(g, L)
                    split(g, NW + 1)
                    for s in range(GS):
                        act.drain()
                        if s == 0:
                            act.wait_ge(hr_ready.sem, hr_ready.last(g, GS))
                            act.wait_ge(down_ev.sem, down_ev.this(g, 2))
                        act.activation(junk[:, :], h3[:, s, :], ACT.Square, scale=D ** -0.5,
                                       accum_out=hs[:, s:s + 1]).then_inc(hs_ready.sem, 1)
                    for s in range(GS):
                        act.wait_ge(out_ready.sem, out_ready.this(g, s + 1))
                        act.dma_start(io["out"][0, ds(ts[s], P), :], h3[:, s, :]).then_inc(out_stored.sem, 16)
                act.wait_ge(out_stored.sem, out_stored.this(NG - 1, GS))

            @block.vector
            def _(dve):
                for s in (hid_ready, hid_split, down_ev, out_ready):
                    s.credit(dve)
                w_split.credit(dve, AHEAD)
                tt = dve.tensor_tensor

                def split(g, L):
                    hi, lo = split_slots(L)
                    dve.wait_ge(w_hi.sem, w_hi.this(g, L + 1))
                    tt(lo, raw[:, L % 2, :], hi.bitcast(F32), ALU.subtract).then_inc(w_split.sem, 1)

                def evict(g, half):
                    cs = slice(half * 512, (half + 1) * 512)
                    dve.wait_ge(hid_used.sem, hid_used.this(g, FT * (half + 1)))
                    for s in range(GS):
                        tt(tmp[:, s % 2, :], down_banks[half][s][:, :], per["g2row"][:, cs], ALU.mult)
                        dve.drain()
                        ev = tt(h3[:, s, cs], h3[:, s, cs], tmp[:, s % 2, :], ALU.add)
                    ev.then_inc(down_ev.sem, 1)

                for L in range(-AHEAD, 0):
                    split(0, L)
                dve.wait_ge(fg_loaded, 16)
                with dve.Fori(0, NG) as g:
                    for c in range(NW):
                        for f in range(FH * c, FH * (c + 1)) if c < N1 else ():
                            dve.wait_ge(rl_ready.sem, rl_ready.this(g, f + 1))
                            tt(hid[:, f, :], rl[:, f % PB, :], rl[:, f % PB, :], ALU.mult).then_inc(hid_ready.sem, 1)
                        for F in hidden_of(c) if c >= N1 else ():
                            if F < FT:
                                dve.wait_ge(hid_ready.sem, hid_ready.this(g, F + 1))
                            dve.wait_ge(hid_hi.sem, hid_hi.this(g, F + 1))
                            tt(hl[:, F % HR, :], hid[:, F % FT, :], hh[:, F % HR, :].bitcast(F32),
                               ALU.subtract).then_inc(hid_split.sem, 1)
                        for L in splits_of(c):
                            split(g, L)
                        if c == N1 + N2:
                            dve.wait_ge(h2_loaded.sem, h2_loaded.this(g, 1))
                            evict(g, 0)
                    split(g, NW + 1)
                    evict(g, 1)
                    for s in range(GS):
                        dve.wait_ge(hr_ready.sem, hr_ready.this(g, s + 1))
                        dve.scalar_tensor_tensor(h3[:, s, :], h3[:, s, :], hr[:, s:s + 1], fgr[:, :], ALU.mult,
                                                 ALU.mult).then_inc(out_ready.sem, 1)


KEPT = {"ident": [P, P], "ones": [P, P], "tri": [P, P], "vc": [P, V_N], "modc": [P, 16], "mod2": [P, 32],
        "nscale1": [P, 8], "nscale2": [P, 8], "silc": [P, 8], "omu": [P, RT], "fraw": [P, NT, NH], "eps": [P, 8],
        "mhalf": [P, 8]}
MASKS = {"smask": [P, 4, P], "tmask": [P, LEVELS + 1, P], "wmask": [P, LEVELS + 1, P], "headcol": [P, 2],
         "headrow": [P, W], "reset": [P, W]}
SCRATCH = {"prw": [RW, T], "og": [T, W], "yrw": [T, W], "h2": [T, D], "u2t": [D, T],
           "qh": [W, T], "ql": [W, T], "kh": [W, T], "kl": [W, T], "v": [T, 2 * W], "fneg": [2, P, P]}


_INS = ["x", "c", "w_ada", "b_ada", "norm1_g", "w_in", "mu_shift", "w0", "w_up_decay", "a0", "w_up_a", "w_up_g",
        "k_k", "k_a", "r_k", "gn_g", "gn_b", "b_f", "q_norm_g", "k_norm_g", "fox_out_g", "w_o", "norm2_g",
        "w_mlp1", "w_mlp2", "final_g"]


def build(nc, io):
    dr = {n: nc.dram_tensor(f"scratch_{n}", shape, F32, kind="Internal").ap() for n, shape in SCRATCH.items()}
    keep = lambda ctx, shapes: {n: ctx.enter_context(nc.sbuf_tensor(n, shape, F32)) for n, shape in shapes.items()}
    with ExitStack() as ctx:
        per = keep(ctx, KEPT)
        with ExitStack() as masks_ctx:
            masks = keep(masks_ctx, MASKS)
            block_constants(nc, io, {**per, **masks}, dr)
            block_project(nc, io, per, dr)
            block_rwkv(nc, io, {**per, **masks}, dr)
        per |= keep(ctx, {"g2row": [P, D]})
        with ExitStack() as tiles_ctx:
            tiles = keep(tiles_ctx, {"tiles": [P, NT, W]})
            block_fox(nc, io, {**per, **tiles}, dr)
            block_out_proj(nc, io, {**per, **tiles}, dr)
        block_mlp(nc, io, per, dr)


def kernel(**inputs):
    import numpy as np
    import concourse.bacc as bacc
    from concourse.bass_utils import run_bass_kernel_spmd

    nc = bacc.Bacc("TRN2", target_bir_lowering=False, num_devices=1)
    arrays, io = {}, {}
    for name in _INS:
        a = np.ascontiguousarray(inputs[name])
        arrays[f"in_{name}"] = a
        io[name] = nc.dram_tensor(f"in_{name}", a.shape, mybir.dt.from_np(a.dtype), kind="ExternalInput").ap()
    io["out"] = nc.dram_tensor("out", [1, T, D], F32, kind="ExternalOutput").ap()
    build(nc, io)
    r = run_bass_kernel_spmd(nc, [arrays], core_ids=[0])
    return r.results[0]["out"]
```

```python
from contextlib import ExitStack, contextmanager

import concourse.bass as bass
from concourse import mybir

F32 = mybir.dt.float32
F32R = mybir.dt.float32r
I32 = mybir.dt.int32
ALU = mybir.AluOpType
ACT = mybir.ActivationFunctionType
AX = mybir.AxisListType
ds = bass.ds

P = 128
D = 1024
T = 2048
KT = D // P
NT = T // P
W = 512
HD = 64
NH = W // HD
WT = W // P
LORA = 64
GLORA = 160
RW = 3 * W + 2 * LORA + GLORA
FX = 4 * W + NH
INC = RW + FX
RT = -(-RW // P)
RLAST = RW - (RT - 1) * P
FF = 4 * D
GT = 512
NG = T // GT
GS = GT // P
C = 64
EPS = 1e-6
GN_EPS = 64e-5
NEG = -1e30
LEVELS = 5
LOGW = -0.6065306597126334

V_BADA, V_G1, V_G2, V_MU, V_W0, V_A0, V_KK, V_KA, V_RK, V_C = 0, 48, 56, 64, 79, 83, 87, 91, 95, 99
V_N = 107


class Signal:

    def __init__(self, sem, per, step=1):
        self.sem, self.per, self.step = sem, per, step

    def credit(self, eng, ahead=0):
        eng.sem_inc(self.sem, (self.per - ahead) * self.step)

    def this(self, i, k):
        return i * (self.per * self.step) + (self.per + k) * self.step

    def last(self, i, k):
        return i * (self.per * self.step) + k * self.step


@contextmanager
def stage_semaphores(nc):
    taken = []

    def take(name):
        taken.append(nc.alloc_semaphore(name=name))
        return taken[-1]

    yield take
    nc.clear_and_free_semaphores(taken)
    nc.all_engine_barrier()


def wait_apart(eng, sem, value, passed):
    eng.wait_ge(sem, value)
    eng.sem_inc(passed, 1)


def block_constants(nc, io, per, dr):
    ident, vc, modc = per["ident"], per["vc"], per["modc"]
    with ExitStack() as ctx:
        sb = lambda n, s, d=F32: ctx.enter_context(nc.sbuf_tensor(n, s, d))
        sem = ctx.enter_context(stage_semaphores(nc))
        vrows = sb("vrows", [P, P])
        wada = sb("wada", [P, 4, KT, 512])
        sil = sb("sil", [P, 8])
        trp = ctx.enter_context(nc.psum_tensor("c_trp", [P, 512], F32))
        modp = ctx.enter_context(nc.psum_tensor("c_modp", [P, 512], F32))
        vec_zeroed, vec_loaded, ident_zeroed = sem("vec_zeroed"), sem("vec_loaded"), sem("ident_zeroed")
        ident_ready, vec_turned, vc_ready = sem("ident_ready"), sem("vec_turned"), sem("vc_ready")
        th_ready, sil_ready, mod_done = sem("th_ready"), sem("sil_ready"), sem("mod_done")
        ada_loaded = [sem(f"ada_loaded{c}") for c in range(4)]

        with nc.Block() as block:
            @block.sync
            def _(sp):
                sp.wait_ge(vec_zeroed, 1)
                rows = lambda name, n: io[name].rearrange("(a b) -> a b", b=P)
                for at, name, n in ((V_BADA, "b_ada", 48), (V_G1, "norm1_g", 8), (V_G2, "norm2_g", 8),
                                    (V_W0, "w0", 4), (V_A0, "a0", 4), (V_KK, "k_k", 4), (V_KA, "k_a", 4)):
                    sp.dma_start(vrows[at:at + n, :], rows(name, n)).then_inc(vec_loaded, 16)
                sp.dma_start(vrows[V_MU:V_MU + RT - 1, :],
                             io["mu_shift"][0:(RT - 1) * P].rearrange("(a b) -> a b", b=P)).then_inc(vec_loaded, 16)
                sp.dma_start(vrows[V_MU + RT - 1:V_MU + RT, 0:RLAST],
                             io["mu_shift"][(RT - 1) * P:RW].rearrange("(a b) -> a b", a=1)).then_inc(vec_loaded, 16)
                sp.dma_start(vrows[V_RK:V_RK + 4, :],
                             io["r_k"].rearrange("(a b) d -> a (b d)", b=2)).then_inc(vec_loaded, 16)
                sp.dma_start(vrows[V_C:V_C + 8, :],
                             io["c"].rearrange("o (a b) -> (o a) b", b=P)).then_inc(vec_loaded, 16)
                for c in range(4):
                    sp.dma_start(wada[:, c, :, :],
                                 io["w_ada"][:, c * 512:(c + 1) * 512].rearrange("(k p) n -> p k n", p=P)
                                 ).then_inc(ada_loaded[c], 16)

            @block.gpsimd
            def _(pool):
                pool.memset(vrows[:, :], 0.0).then_inc(vec_zeroed, 1)
                pool.memset(ident[:, :], 0.0).then_inc(ident_zeroed, 1)
                pool.memset(per["ones"][:, :], 1.0)
                pool.memset(per["mhalf"][:, :], -0.5)
                pool.memset(per["eps"][:, :], EPS)
                pool.wait_ge(ident_zeroed, 1)
                pool.affine_select(out=ident[:, :], in_=ident[:, :], compare_op=ALU.not_equal, fill=1.0,
                                   base=0, pattern=[[-1, P]], channel_multiplier=1).then_inc(ident_ready, 1)

                def keep(m, pattern, base, mult):
                    pool.drain()
                    pool.affine_select(out=m, in_=m, compare_op=ALU.is_ge, fill=0.0, base=base,
                                       pattern=pattern, channel_multiplier=mult)

                sm = per["smask"]
                pool.memset(sm[:, 0:1, :], -1.0)
                pool.memset(sm[:, 1:4, :], 1.0)
                for n in range(4):
                    m = sm[:, n, :]
                    keep(m, [[1, P]], -1 if n % 2 == 0 else 0, -1)
                    keep(m.rearrange("p (b t) -> p b t", b=2), [[-C, 2], [0, C]], 0, 1)
                pool.memset(per["tri"][:, :], 1.0)
                keep(per["tri"][:, :], [[1, P]], 0, -1)
                for n in range(LEVELS + 1):
                    b = 1 << n
                    for m, half in ((per["tmask"][:, n, :], 0), (per["wmask"][:, n, :], 1)):
                        pool.memset(m, 1.0)
                        m4 = m.rearrange("p (u h w) -> p u h w", h=2, w=b)
                        nb = P // (2 * b)
                        lo = 0 if half else b
                        keep(m4, [[-2 * b, nb], [0, 2], [0, b]], -lo, 1)
                        keep(m4, [[2 * b, nb], [0, 2], [0, b]], lo + b - 1, -1)
                        if half:
                            keep(m4, [[0, nb], [1, 2], [0, b]], -1, 0)
                        else:
                            keep(m4, [[0, nb], [-1, 2], [0, b]], 0, 0)
                pool.memset(per["headcol"][:, :], 1.0)
                keep(per["headcol"][:, 0:1], [[0, 1]], HD - 1, -1)
                keep(per["headcol"][:, 1:2], [[0, 1]], -HD, 1)
                pool.memset(per["headrow"][:, :], 1.0)
                hr = per["headrow"][:, :].rearrange("p (h d) -> p h d", h=NH)
                keep(hr, [[-1, NH], [0, HD]], 0, 1)
                keep(hr, [[1, NH], [0, HD]], 0, -1)
                pool.memset(per["reset"][:, :], 1.0)
                pool.drain()
                pool.memset(per["reset"][:, :].rearrange("p (n c) -> p n c", c=C)[:, :, 0:1], 0.0)

            @block.tensor
            def _(pe):
                pe.wait_ge(ident_ready, 1)
                pe.wait_ge(vec_loaded, 16 * 11)
                pe.transpose(trp[:, 0:P], vrows[:, :], ident[:, :]).then_inc(vec_turned, 1)
                pe.wait_ge(sil_ready, 1)
                for c in range(4):
                    pe.wait_ge(ada_loaded[c], 16)
                    for m in range(4):
                        for k in range(KT):
                            mm = pe.matmul(modp[:, 4 * c + m:4 * c + m + 1], wada[:, c, k, m * P:(m + 1) * P],
                                           sil[:, k:k + 1], start=(k == 0), stop=(k == KT - 1))
                mm.then_inc(mod_done, 1)

            @block.scalar
            def _(act):
                act.wait_ge(vc_ready, 1)
                act.activation(sil[:, :], vc[:, V_C:V_C + 8], ACT.Tanh, scale=0.5).then_inc(th_ready, 1)

            @block.vector
            def _(dve):
                dve.wait_ge(vec_turned, 1)
                dve.tensor_copy(vc[:, :], trp[:, 0:V_N]).then_inc(vc_ready, 1)
                dve.wait_ge(th_ready, 1)
                dve.tensor_scalar(sil[:, :], sil[:, :], 0.5, 0.5, ALU.mult, ALU.add)
                dve.drain()
                dve.tensor_tensor(per["silc"][:, :], sil[:, :], vc[:, V_C:V_C + 8], ALU.mult)
                dve.drain()
                dve.tensor_copy(sil[:, :], per["silc"][:, :]).then_inc(sil_ready, 1)
                dve.tensor_scalar(per["omu"][:, :], vc[:, V_MU:V_MU + RT], -1.0, 1.0, ALU.mult, ALU.add)
                dve.wait_ge(mod_done, 1)
                dve.tensor_tensor(modc[:, 0:16], modp[:, 0:16], vc[:, V_BADA:V_BADA + 16], ALU.add)
                dve.drain()
                dve.scalar_tensor_tensor(per["nscale1"][:, :], modc[:, 8:16], 1.0, vc[:, V_G1:V_G1 + 8],
                                         ALU.add, ALU.mult)


def block_project(nc, io, per, dr):
    ident, vc = per["ident"], per["vc"]
    with ExitStack() as ctx:
        sb = lambda n, s, d=F32: ctx.enter_context(nc.sbuf_tensor(n, s, d))
        sem = ctx.enter_context(stage_semaphores(nc))
        win = sb("win", [P, KT, INC])
        xs = sb("xs", [P, GS, D])
        ut = sb("ut", [P, KT, GT])
        junk = sb("p_junk", [P, D])
        ss = sb("p_ss", [P, GS])
        rstd = sb("p_rstd", [P, GS])
        tmp = sb("p_tmp", [P, 2, GT + 1])
        carry = sb("p_carry", [P, RT])
        stage = sb("p_stage", [P, 4, GT])
        qk = sb("p_qk", [P, 2, W])
        sqb = sb("p_sqb", [P, 2, W])
        ssq = sb("p_ssq", [P, 2, NH])
        rsq = sb("p_rsq", [P, 2, NH])
        qkh, qkl = sb("p_qkh", [P, 2, W], F32R), sb("p_qkl", [P, 2, W], F32R)
        vhl = sb("p_vhl", [P, NH, 2, HD], F32R)
        ogs = sb("p_ogs", [P, W])
        gqk = sb("p_gqk", [P, 2, HD])
        bf = sb("p_bf", [P, NH])
        banks = [ctx.enter_context(nc.psum_tensor(f"p_b{i}", [P, 512], F32)) for i in range(8)]
        xtb, mmb, qtb = banks[0:2], banks[3:8], [banks[2], banks[1]]

        wloaded = [sem(f"win_loaded{c}") for c in range(8)]
        sp_passed = sem("p_sp_passed")
        small_loaded, carry_zeroed = sem("p_small_loaded"), sem("carry_zeroed")
        x_loaded = Signal(sem("x_loaded"), 1, 16)
        sq_done, rstd_done, xn_ready = (Signal(sem(n), GS) for n in ("sq_done", "rstd_done", "xn_ready"))
        xt_done = Signal(sem("xt_done"), GS)
        ut_act, ut_dve = Signal(sem("ut_act"), GS), Signal(sem("ut_dve"), GS)
        uses = ["rw"] * RT + ["q", "k", "v", "og", "f"] * GS
        mm_done = Signal(sem("p_mm_done"), len(uses))
        free_act = Signal(sem("free_act"), 2 * GS)
        free_dve = Signal(sem("free_dve"), RT + 3 * GS)
        tmp_ready = Signal(sem("tmp_ready"), RT)
        st_done = [Signal(sem(f"st_done{r}"), 4, 16) for r in range(4)]
        sqk_done, rqk_done, qk_ready = (Signal(sem(n), 2 * GS) for n in ("sqk_done", "rqk_done", "qk_ready"))
        ssqk_done = Signal(sem("ssqk_done"), 2 * GS)
        qt_done = Signal(sem("qt_done"), 2 * GS)
        qkh_ready, qkl_ready = Signal(sem("qkh_ready"), 2 * GS), Signal(sem("qkl_ready"), 2 * GS)
        qt_stored = [Signal(sem(f"qt_stored{r}"), 2 * GS, 16) for r in range(2)]
        vog_ready = Signal(sem("vog_ready"), 2 * GS)
        vog_stored = [Signal(sem(f"vog_stored{r}"), GS, 16) for r in range(2)]

        def freed(n):
            a = sum(u in "qk" for u in uses[:n + 1])
            return (free_act, a) if uses[n] in "qk" else (free_dve, n + 1 - a)

        def wait_bank(pe, g, n):
            if n >= 5:
                s, k = freed(n - 5)
                pe.wait_ge(s.sem, s.this(g, k))
            else:
                s, k = freed(n - 5 + len(uses))
                pe.wait_ge(s.sem, s.last(g, k))

        with nc.Block() as block:
            @block.sync
            def _(sp):
                for s in (x_loaded, *st_done, *qt_stored, *vog_stored):
                    s.credit(sp)
                sp.dma_start(bf[:, :], io["b_f"].partition_broadcast(P)).then_inc(small_loaded, 16)
                sp.dma_start(gqk[:, 0, :], io["q_norm_g"].partition_broadcast(P)).then_inc(small_loaded, 16)
                sp.dma_start(gqk[:, 1, :], io["k_norm_g"].partition_broadcast(P)).then_inc(small_loaded, 16)
                x_of = lambda t0: io["x"][0, ds(t0, GT), :].rearrange("(s p) n -> p s n", p=P)
                with sp.Fori(0, NG) as g:
                    t0 = sp.snap(g * GT)
                    ts = [sp.snap(t0 + s * P) for s in range(GS)]
                    sp.wait_ge(xt_done.sem, xt_done.last(g, GS))
                    sp.dma_start(xs[:, :, :], x_of(t0)).then_inc(x_loaded.sem, 16)
                    for m in range(RT):
                        rows = P if m < RT - 1 else RLAST
                        wait_apart(sp, free_dve.sem, free_dve.this(g, m + 1), sp_passed)
                        sp.dma_start(dr["prw"][m * P:m * P + rows, ds(t0, GT)],
                                     stage[0:rows, m % 4, :]).then_inc(st_done[m % 4].sem, 16)
                    sp.sem_inc(st_done[3].sem, 16)
                    for s in range(GS):
                        sp.wait_ge(vog_ready.sem, vog_ready.this(g, 2 * s + 1))
                        sp.dma_start(dr["v"][ds(ts[s], P), :], vhl[:, :, :, :].rearrange("p h c d -> p (h c d)").bitcast(F32)
                                     ).then_inc(vog_stored[0].sem, 16)
                        sp.wait_ge(vog_ready.sem, vog_ready.this(g, 2 * s + 2))
                        sp.dma_start(dr["og"][ds(ts[s], P), :], ogs[:, :]).then_inc(vog_stored[1].sem, 16)
                        for r in range(2):
                            for part, src, name in ((qkh_ready, qkh, "qk"[r] + "h"), (qkl_ready, qkl, "qk"[r] + "l")):
                                wait_apart(sp, part.sem, part.this(g, 2 * s + r + 1), sp_passed)
                                sp.dma_start(dr[name][:, ds(ts[s], P)].rearrange("(j p) n -> p j n", p=P),
                                             src[:, r, :].rearrange("p (j n) -> p j n", j=WT).bitcast(F32)
                                             ).then_inc(qt_stored[r].sem, 16)
                for s in (*st_done, *qt_stored, *vog_stored):
                    sp.wait_ge(s.sem, s.this(NG - 1, s.per))

            @block.gpsimd
            def _(pool):
                rstd_done.credit(pool)
                rqk_done.credit(pool)
                pool.memset(carry[:, :], 0.0).then_inc(carry_zeroed, 1)
                with pool.Fori(0, NG) as g:
                    for s in range(GS):
                        pool.wait_ge(sq_done.sem, sq_done.this(g, s + 1))
                        pool.tensor_tensor(rstd[:, s:s + 1], ss[:, s:s + 1], per["eps"][:, 0:1], ALU.add)
                        pool.drain()
                        pool.tensor_tensor(rstd[:, s:s + 1], rstd[:, s:s + 1], per["mhalf"][:, 0:1],
                                           ALU.pow).then_inc(rstd_done.sem, 1)
                    for n in range(2 * GS):
                        pool.wait_ge(ssqk_done.sem, ssqk_done.this(g, n + 1))
                        pool.tensor_tensor(rsq[:, n % 2, :], ssq[:, n % 2, :], per["eps"][:, :], ALU.add)
                        pool.drain()
                        pool.tensor_tensor(rsq[:, n % 2, :], rsq[:, n % 2, :], per["mhalf"][:, :],
                                           ALU.pow).then_inc(rqk_done.sem, 1)

            @block.tensor
            def _(pe):
                for s in (xt_done, mm_done, qt_done):
                    s.credit(pe)
                with pe.Fori(0, NG) as g:
                    for s in range(GS):
                        pe.wait_ge(xn_ready.sem, xn_ready.this(g, s + 1))
                        for ev in (ut_act, ut_dve):
                            pe.wait_ge(ev.sem, ev.this(g, s) if s else ev.last(g, GS))
                        if s == 0:
                            pe.wait_ge(qkl_ready.sem, qkl_ready.last(g, 2 * GS))
                        for k in range(KT):
                            mm = pe.transpose(xtb[k // 4][:, (k % 4) * P:(k % 4 + 1) * P],
                                              xs[:, s, k * P:(k + 1) * P], ident[:, :])
                        mm.then_inc(xt_done.sem, 1)
                    for ev in (ut_act, ut_dve):
                        pe.wait_ge(ev.sem, ev.this(g, GS))
                    n = 0
                    for m in range(RT):
                        cols = P if m < RT - 1 else RLAST
                        wait_bank(pe, g, n)
                        pe.wait_ge(wloaded[m * P // 512], 16)
                        for k in range(KT):
                            mm = pe.matmul(mmb[n % 5][0:cols, :], win[:, k, m * P:m * P + cols], ut[:, k, :],
                                           start=(k == 0), stop=(k == KT - 1))
                        mm.then_inc(mm_done.sem, 1)
                        n += 1
                    for s in range(GS):
                        for f in range(5):
                            lo, hi = RW + f * W, min(RW + f * W + W, INC)
                            wait_bank(pe, g, n)
                            for c in range(lo // 512, (hi - 1) // 512 + 1):
                                pe.wait_ge(wloaded[c], 16)
                            for k in range(KT):
                                mm = pe.matmul(mmb[n % 5][:, 0:hi - lo], ut[:, k, s * P:(s + 1) * P],
                                               win[:, k, lo:hi], start=(k == 0), stop=(k == KT - 1))
                            mm.then_inc(mm_done.sem, 1)
                            n += 1
                        for r in range(2):
                            pe.wait_ge(qk_ready.sem, qk_ready.this(g, 2 * s + r + 1))
                            k = 2 * (s - 1) + r + 1
                            pe.wait_ge(qkl_ready.sem, qkl_ready.this(g, k) if k > 0 else qkl_ready.last(g, 2 * GS + k))
                            for j in range(WT):
                                mm = pe.transpose(qtb[r][:, j * P:(j + 1) * P], qk[:, r, j * P:(j + 1) * P],
                                                  ident[:, :])
                            mm.then_inc(qt_done.sem, 1)

            @block.scalar
            def _(act):
                for s in (sq_done, ut_act, free_act, tmp_ready, sqk_done, qkh_ready):
                    s.credit(act)
                for c in range(8):
                    lo, hi = c * 512, min(c * 512 + 512, INC)
                    act.dma_start(win[:, :, lo:hi],
                                  io["w_in"][:, lo:hi].rearrange("(k p) n -> p k n", p=P)).then_inc(wloaded[c], 16)
                act.wait_ge(carry_zeroed, 1)
                with act.Fori(0, NG) as g:
                    for s in range(GS):
                        act.drain()
                        act.wait_ge(x_loaded.sem, x_loaded.this(g, 1))
                        if s == 0:
                            act.wait_ge(rstd_done.sem, rstd_done.last(g, GS))
                        act.activation(junk[:, :], xs[:, s, :], ACT.Square, scale=D ** -0.5,
                                       accum_out=ss[:, s:s + 1]).then_inc(sq_done.sem, 1)
                    act.wait_ge(mm_done.sem, mm_done.last(g, len(uses)))
                    for s in range(GS):
                        act.wait_ge(xt_done.sem, xt_done.this(g, s + 1))
                        for k in range(KT // 2):
                            ev = act.activation(ut[:, k, s * P:(s + 1) * P], xtb[0][:, k * P:(k + 1) * P], ACT.Identity,
                                                bias=per["modc"][:, k:k + 1], scale=per["nscale1"][:, k:k + 1])
                        ev.then_inc(ut_act.sem, 1)
                    for m in range(RT):
                        rows = P if m < RT - 1 else RLAST
                        act.wait_ge(mm_done.sem, mm_done.this(g, m + 1))
                        act.wait_ge(free_dve.sem, free_dve.this(g, m - 1) if m >= 2
                                    else free_dve.last(g, RT + m - 1))
                        act.copy(tmp[0:rows, m % 2, 0:1], carry[0:rows, m:m + 1])
                        act.activation(tmp[0:rows, m % 2, 1:GT + 1], mmb[m % 5][0:rows, :], ACT.Identity,
                                       scale=vc[0:rows, V_MU + m:V_MU + m + 1])
                        act.drain()
                        act.copy(carry[0:rows, m:m + 1], tmp[0:rows, m % 2, GT:GT + 1]).then_inc(tmp_ready.sem, 1)
                    for s in range(GS):
                        for r in range(2):
                            n = RT + 5 * s + r
                            act.wait_ge(mm_done.sem, mm_done.this(g, n + 1))
                            k = 2 * s + r - 1
                            act.wait_ge(qt_done.sem, qt_done.this(g, k) if k > 0 else qt_done.last(g, 2 * GS + k))
                            act.wait_ge(ssqk_done.sem, ssqk_done.this(g, k) if k > 0
                                        else ssqk_done.last(g, 2 * GS + k))
                            act.activation(sqb[:, r, :], mmb[n % 5][:, :], ACT.Square,
                                           scale=HD ** -0.5).then_inc(sqk_done.sem, 1)
                            act.copy(qk[:, r, :], mmb[n % 5][:, :]).then_inc(free_act.sem, 1)
                        for r in range(2):
                            act.wait_ge(qt_done.sem, qt_done.this(g, 2 * s + r + 1))
                            st = qt_stored[r]
                            act.wait_ge(st.sem, st.this(g, 2 * s) if s else st.last(g, 2 * GS))
                            act.copy(qkh[:, r, :], qtb[r][:, :]).then_inc(qkh_ready.sem, 1)

            @block.vector
            def _(dve):
                for s in (xn_ready, ut_dve, free_dve, ssqk_done, qk_ready, qkl_ready, vog_ready):
                    s.credit(dve)
                dve.wait_ge(small_loaded, 48)
                dve.tensor_scalar(gqk[:, 0, :], gqk[:, 0, :], HD ** -0.5, None, ALU.mult)
                with dve.Fori(0, NG) as g:
                    for s in range(GS):
                        dve.wait_ge(rstd_done.sem, rstd_done.this(g, s + 1))
                        dve.tensor_scalar(xs[:, s, :], xs[:, s, :], rstd[:, s:s + 1], None,
                                          ALU.mult).then_inc(xn_ready.sem, 1)
                    dve.wait_ge(mm_done.sem, mm_done.last(g, len(uses)))
                    for s in range(GS):
                        dve.wait_ge(xt_done.sem, xt_done.this(g, s + 1))
                        for k in range(KT // 2, KT):
                            ev = dve.tensor_scalar(ut[:, k, s * P:(s + 1) * P], xtb[1][:, (k - 4) * P:(k - 3) * P],
                                                   per["nscale1"][:, k:k + 1], per["modc"][:, k:k + 1],
                                                   ALU.mult, ALU.add)
                        ev.then_inc(ut_dve.sem, 1)
                    for m in range(RT):
                        rows = P if m < RT - 1 else RLAST
                        dve.wait_ge(tmp_ready.sem, tmp_ready.this(g, m + 1))
                        s = st_done[m % 4]
                        dve.wait_ge(s.sem, s.this(g, m // 4) if m >= 4 else s.last(g, 4))
                        dve.scalar_tensor_tensor(stage[0:rows, m % 4, :], mmb[m % 5][0:rows, :],
                                                 per["omu"][0:rows, m:m + 1], tmp[0:rows, m % 2, 0:GT],
                                                 ALU.mult, ALU.add).then_inc(free_dve.sem, 1)
                    for s in range(GS):
                        for r in range(2):
                            dve.wait_ge(sqk_done.sem, sqk_done.this(g, 2 * s + r + 1))
                            k = 2 * s + r - 1
                            dve.wait_ge(rqk_done.sem, rqk_done.this(g, k) if k > 0 else rqk_done.last(g, 2 * GS + k))
                            dve.tensor_reduce(ssq[:, r, :], sqb[:, r, :].rearrange("p (h d) -> p h d", h=NH),
                                              AX.X, ALU.add).then_inc(ssqk_done.sem, 1)
                            dve.wait_ge(rqk_done.sem, rqk_done.this(g, 2 * s + r + 1))
                            dve.wait_ge(free_act.sem, free_act.this(g, 2 * s + r + 1))
                            q3 = qk[:, r, :].rearrange("p (h d) -> p h d", h=NH)
                            dve.tensor_tensor(q3, q3, rsq[:, r, :].unsqueeze(2).to_broadcast([P, NH, HD]), ALU.mult)
                            dve.drain()
                            dve.tensor_tensor(q3, q3, gqk[:, r, :].unsqueeze(1).to_broadcast([P, NH, HD]),
                                              ALU.mult).then_inc(qk_ready.sem, 1)
                        for r in range(2):
                            n = RT + 5 * s + 2 + r
                            dve.wait_ge(mm_done.sem, mm_done.this(g, n + 1))
                            st = vog_stored[r]
                            dve.wait_ge(st.sem, st.this(g, s) if s else st.last(g, GS))
                            if r == 0:
                                vb = mmb[n % 5][:, :].rearrange("p (h d) -> p h d", h=NH)
                                dve.tensor_copy(vhl[:, :, 0, :], vb)
                                dve.drain()
                                dve.tensor_tensor(vhl[:, :, 1, :], vb, vhl[:, :, 0, :].bitcast(F32),
                                                  ALU.subtract).then_inc(free_dve.sem, 1)
                            else:
                                dve.tensor_copy(ogs[:, :], mmb[n % 5][:, :]).then_inc(free_dve.sem, 1)
                            dve.drain()
                            dve.sem_inc(vog_ready.sem, 1)
                        n = RT + 5 * s + 4
                        dve.wait_ge(mm_done.sem, mm_done.this(g, n + 1))
                        dve.tensor_tensor(per["fraw"][:, ds(g * GS + s, 1), :],
                                          mmb[n % 5][:, 0:NH].unsqueeze(1), bf[:, :].unsqueeze(1),
                                          ALU.add).then_inc(free_dve.sem, 1)
                        for r in range(2):
                            dve.wait_ge(qkh_ready.sem, qkh_ready.this(g, 2 * s + r + 1))
                            dve.tensor_tensor(qkl[:, r, :], qtb[r][:, :], qkh[:, r, :].bitcast(F32),
                                              ALU.subtract).then_inc(qkl_ready.sem, 1)


def block_rwkv(nc, io, per, dr):
    ident, vc = per["ident"], per["vc"]
    QN, QH = 4, NH // 4
    NINV = QN * LEVELS
    with ExitStack() as ctx:
        sb = lambda n, s, d=F32: ctx.enter_context(nc.sbuf_tensor(n, s, d))
        sem = ctx.enter_context(stage_semaphores(nc))
        sig = lambda n, per_turn=1, step=1: Signal(sem(n), per_turn, step)
        wud, wua = sb("wud", [LORA, W]), sb("wua", [P, W])
        wug0, wug1 = sb("wug0", [P, W]), sb("wug1", [GLORA - P, W])
        gnw = sb("gnw", [P, 2, W])
        hw0, ha0 = sb("hw0", [P, WT]), sb("ha0", [P, WT])
        pt = sb("r_pt", [P, RT, P])
        adas = sb("r_adas", [P, KT, 2 * P])
        th = sb("r_th", [LORA, P])
        sg = sb("r_sg", [P, 2, P])
        names = ["tw", "ta", "nlw", "lc", "lx", "e2", "e1x", "kkr", "sq", "t1", "kp", "pr", "kk", "bt", "zt"]
        f = {n: sb("r_" + n, [P, WT, P]) for n in names}
        two = lambda n, s: [sb(f"{n}{p}", s) for p in range(2)]
        kr, e1 = two("r_kr", [P, WT, 2, P]), two("r_e1", [P, WT, P])
        padded = sb("r_padded", [P, 2, 2, WT, P])
        ssm, rn, bon = sb("r_ssm", [P, NH]), sb("r_rn", [P, NH]), two("r_bon", [P, NH])
        rnt = sb("r_rnt", [NH, P])
        v_t, bz_t = two("r_v", [P, W]), two("r_bz", [P, 2, 2, W])
        sc, gate = two("r_sc", [P, NH, 4, P]), two("r_gate", [P, W])
        tm, wm, gt = sb("r_tm", [P, NH, P]), two("r_wm", [P, NH, P]), sb("r_gt", [P, NH, P])
        xn, u = sb("r_xn", [P, W]), sb("r_u", [P, W])
        st = sb("r_state", [P, 2, WT, P])
        y, yq = sb("r_y", [P, W]), sb("r_yq", [P, W])
        gs, gr = sb("r_gs", [P, 2, NH]), sb("r_gr", [P, NH])
        yo = sb("r_yo", [P, W])
        bk = [ctx.enter_context(nc.psum_tensor(f"r_b{i}", [P, 512], F32)) for i in range(8)]

        once_loaded, init_done = sem("r_once_loaded"), sem("r_init_done")
        pe_passed, sp_passed, dve_passed = sem("pe_passed"), sem("sp_passed"), sem("dve_passed")
        p_loaded, ada_loaded, y_stored = sig("p_loaded", 2, 16), sig("r_ada_loaded", 1, 16), sig("y_stored", 1, 16)
        th_ready, sgt_ready, sg_ready = sig("th_ready_"), sig("sgt_ready"), sig("sg_ready")
        zw_done, za_done, g_done = sig("zw_done"), sig("za_done"), sig("g_done")
        tw_ready, ta_ready, kkr_ready, sq_ready = sig("tw_ready"), sig("ta_ready"), sig("kkr_ready"), sig("sq_ready")
        l_ready, e_ready, pr_ready = sig("l_ready"), sig("e_ready"), sig("pr_ready")
        ss_done, ssm_ready, rn_ready = sig("ss_done"), sig("ssm_ready"), sig("rn_ready")
        rnt_done, rnt_ready, rnbc_done = sig("rnt_done"), sig("rnt_ready"), sig("rnbc_done")
        kp_ready, feats_ready = sig("kp_ready"), sig("feats_ready")
        bonus_done, bon_ready = sig("bonus_done"), sig("bon_ready")
        tr_done, tr_ready, pad_ready, gate_ready = sig("tr_done", 3), sig("tr_ready", 3), sig("pad_ready"), sig("gate_ready")
        score_done, score_ready = sig("score_done", NH), sig("score_ready", NH)
        w2_ready, t2_done, t2_ready = sig("w2_ready"), sig("t2_done", 2), sig("t2_ready", 2)
        gt_done, gt_ready = sig("gt_done", NINV), sig("gt_ready", NINV)
        tgt_done, tw_upd = sig("tgt_done", NINV), sig("tw_upd", NINV)
        x_done, x_ready, u_done, u_ready = sig("x_done", 2), sig("x_ready", 2), sig("u_done", 2), sig("u_ready", 2)
        dst_done, st_ready = sig("dst_done", 2), sig("st_ready", 2)
        y_done, y_ready, yc_ready, yq_ready = sig("y_done"), sig("y_ready"), sig("yc_ready"), sig("yq_ready")
        var_ready, gr_ready, yo_ready = sig("var_ready"), sig("gr_ready"), sig("yo_ready")
        ada_done, ada_ready = sig("r_ada_done"), sig("r_ada_ready")
        h3 = lambda ap: ap.rearrange("p (h d) -> p h d", h=NH)
        bc = lambda ap: ap.unsqueeze(2).to_broadcast([P, NH, HD])
        r_, k_, v_ = (pt[:, n * WT:(n + 1) * WT, :] for n in range(3))
        col = lambda base: vc[:, base:base + WT].unsqueeze(2).to_broadcast([P, WT, P])

        inv = lambda lo, hi: [(f"inv{n}", 1) for n in range(lo, hi)]
        tw_banks = [bk[6], bk[7], bk[0], bk[1]]
        TURN = [("X0", 0), ("S0", 1), ("S1", 1), ("U0", 0), ("S2", 1), ("D0", 0), ("S3", 1), ("X1", 0), ("W2", 1),
                ("Yv", 0), ("U1", 0), ("D1", 0), ("T2", 1), ("Yu", 0), ("G0", 1), ("ADA", 0), *inv(0, 2), ("OUT1", 0),
                *inv(2, 3), ("A1a", 2), *inv(3, 4), ("OUT2", 0), *inv(4, 5), ("A1b", 2), ("A1c", 2), *inv(5, 6),
                ("OUT3", 0), *inv(6, 7), ("A1d", 2), *inv(7, 8), ("A2a", 2), *inv(8, 9), ("A2f", 2), *inv(9, 10),
                ("A2k", 2), *inv(10, 11), ("A2g", 2), *inv(11, 12), ("A2v", 2), *inv(12, 13), ("A2b", 2),
                *inv(13, 14), ("A2c", 2), *inv(14, 15), ("A2d", 2), ("A3a", 2), *inv(15, 16), ("A3b", 2),
                *inv(16, NINV), ("A3c", 2), ("A3d", 2), ("A3e", 2)]

        def run(eng, front, back):
            def turn(tiles, p, least=0):
                for step, ahead in TURN:
                    if least <= ahead < len(tiles):
                        (front if ahead else back)(step, tiles[ahead], (p + ahead) % 2)

            turn((-2, -1, 0), 0, 2)
            turn((-1, 0, 1), 1, 1)
            with eng.Fori(0, NT // 2 - 1) as pair:
                t0 = eng.snap(2 * pair)
                t1, t2, t3 = (eng.snap(t0 + n) for n in (1, 2, 3))
                turn((t0, t1, t2), 0)
                turn((t1, t2, t3), 1)
            turn((NT - 2, NT - 1), 0)
            turn((NT - 1,), 1)

        def wait_two_before(eng, s, i, k):
            if not (isinstance(i, int) and i < 2):
                eng.wait_ge(s.sem, s.last(i - 1, k))

        with nc.Block() as block:
            @block.sync
            def _(sp):
                for s in (p_loaded, ada_loaded, y_stored):
                    s.credit(sp)
                sp.dma_start(wud[:, :], io["w_up_decay"]).then_inc(once_loaded, 16)
                sp.dma_start(wua[LORA:P, :], io["w_up_a"]).then_inc(once_loaded, 16)
                sp.dma_start(wug0[:, :], io["w_up_g"][0:P, :]).then_inc(once_loaded, 16)
                sp.dma_start(wug1[:, :], io["w_up_g"][P:GLORA, :]).then_inc(once_loaded, 16)
                sp.dma_start(gnw[:, 0, :], io["gn_g"].partition_broadcast(P)).then_inc(once_loaded, 16)
                sp.dma_start(gnw[:, 1, :], io["gn_b"].partition_broadcast(P)).then_inc(once_loaded, 16)

                def front(step, i, p):
                    if step == "A1a":
                        tile = ds(i * P, P) if isinstance(i, int) else ds(sp.snap(i * P), P)
                        wait_apart(sp, tr_done.sem, tr_done.last(i, 3), sp_passed)
                        wait_apart(sp, feats_ready.sem, feats_ready.last(i, 1), sp_passed)
                        sp.dma_start(pt[:, 0:RT - 1, :],
                                     dr["prw"][0:(RT - 1) * P, tile].rearrange("(m p) n -> p m n", p=P)
                                     ).then_inc(p_loaded.sem, 16)
                        sp.dma_start(pt[0:RLAST, RT - 1, :], dr["prw"][(RT - 1) * P:RW, tile]
                                     ).then_inc(p_loaded.sem, 16)

                def back(step, i, p):
                    if step == "X1":
                        cols = i * (2 * P) + 2 * D
                        wait_apart(sp, ada_done.sem, ada_done.last(i, 1), sp_passed)
                        sp.dma_start(adas[:, :, :],
                                     io["w_ada"][:, ds(cols if isinstance(i, int) else sp.snap(cols), 2 * P)].rearrange(
                                         "(k p) n -> p k n", p=P)).then_inc(ada_loaded.sem, 16)
                    if step == "OUT3":
                        t0 = i * P if isinstance(i, int) else sp.snap(i * P)
                        wait_apart(sp, yo_ready.sem, yo_ready.this(i, 1), sp_passed)
                        sp.dma_start(dr["yrw"][ds(t0, P), :], yo[:, :]).then_inc(y_stored.sem, 16)

                run(sp, front, back)
                sp.wait_ge(y_stored.sem, y_stored.this(NT - 1, 1))

            @block.gpsimd
            def _(pool):
                for s in (rn_ready, gr_ready, pr_ready, yo_ready):
                    s.credit(pool)
                pool.wait_ge(once_loaded, 16 * 6)
                for zeroed in (xn, u, st, padded, *bz_t):
                    pool.drain()
                    last = pool.memset(zeroed.ap(), 0.0)
                last.then_inc(init_done, 1)

                def front(step, i, p):
                    if step == "A2a":
                        pool.wait_ge(ssm_ready.sem, ssm_ready.this(i, 1))
                        pool.wait_ge(rnt_done.sem, rnt_done.last(i, 1))
                        pool.tensor_tensor(rn[:, :], ssm[:, :], per["mhalf"][:, :], ALU.pow).then_inc(rn_ready.sem, 1)
                    elif step == "A2k":
                        pool.wait_ge(kp_ready.sem, kp_ready.this(i, 1))
                        pool.wait_ge(bonus_done.sem, bonus_done.last(i, 1))
                        pool.tensor_tensor(f["pr"][:, :, :], f["kp"][:, :, :], col(V_RK), ALU.mult)
                        pool.drain()
                        pool.tensor_tensor(f["pr"][:, :, :], f["pr"][:, :, :], r_, ALU.mult).then_inc(pr_ready.sem, 1)

                def back(step, i, p):
                    if step == "OUT2":
                        pool.wait_ge(var_ready.sem, var_ready.this(i, 1))
                        pool.tensor_tensor(gr[:, :], gs[:, 1, :], per["mhalf"][:, :], ALU.pow
                                           ).then_inc(gr_ready.sem, 1)
                        pool.tensor_tensor(h3(yq[:, :]), h3(v_t[p][:, :]), bc(bon[p][:, :]), ALU.mult)
                    elif step == "OUT3":
                        tt = pool.tensor_tensor
                        pool.drain()
                        tt(h3(y[:, :]), h3(y[:, :]), bc(gr[:, :]), ALU.mult)
                        pool.drain()
                        tt(y[:, :], y[:, :], gnw[:, 0, :], ALU.mult)
                        pool.drain()
                        tt(y[:, :], y[:, :], gnw[:, 1, :], ALU.add)
                        pool.drain()
                        tt(y[:, :], y[:, :], yq[:, :], ALU.add)
                        pool.drain()
                        pool.wait_ge(y_stored.sem, y_stored.last(i, 1))
                        tt(yo[:, :], y[:, :], gate[p][:, :], ALU.mult).then_inc(yo_ready.sem, 1)

                run(pool, front, back)

            @block.tensor
            def _(pe):
                for s in (zw_done, za_done, g_done, ss_done, rnt_done, rnbc_done, bonus_done, tr_done, score_done,
                          t2_done, gt_done, tgt_done, x_done, u_done, dst_done, y_done, ada_done):
                    s.credit(pe)
                pe.wait_ge(once_loaded, 16 * 6)
                pe.wait_ge(init_done, 1)

                def grow(i, p, n):
                    if n < QN:
                        pe.wait_ge(t2_ready.sem, t2_ready.this(i, 2))
                    else:
                        pe.wait_ge(tw_upd.sem, tw_upd.this(i, n + 1 - QN))
                    for m in range(QH):
                        h = n % QN * QH + m
                        mm = pe.matmul(bk[4 + n % 2][:, m * P:(m + 1) * P], sc[p][:, h, 0, :],
                                       tm[:, h, :], start=True, stop=True)
                    mm.then_inc(gt_done.sem, 1)

                def front(step, i, p):
                    if step == "A1b":
                        pe.wait_ge(th_ready.sem, th_ready.this(i, 1))
                        wait_two_before(pe, ada_ready, i, 1)
                        wait_two_before(pe, y_ready, i, 1)
                        for j in range(WT):
                            mm = pe.matmul(bk[2][:, j * P:(j + 1) * P], wud[:, j * P:(j + 1) * P], th[:, :],
                                           start=True, stop=True)
                        mm.then_inc(zw_done.sem, 1)
                        for j in range(WT):
                            mm = pe.matmul(bk[3][:, j * P:(j + 1) * P], wua[LORA:P, j * P:(j + 1) * P],
                                           pt[LORA:P, RT - 3, :], start=True, stop=True)
                        mm.then_inc(za_done.sem, 1)
                    elif step == "A1d":
                        pe.wait_ge(sq_ready.sem, sq_ready.this(i, 1))
                        pe.wait_ge(tw_ready.sem, tw_ready.this(i, 1))
                        for j in range(WT):
                            mm = pe.matmul(bk[2][:, 2 * j:2 * j + 2], f["sq"][:, j, :], per["headcol"][:, :],
                                           start=True, stop=True)
                        mm.then_inc(ss_done.sem, 1)
                        pe.wait_ge(sg_ready.sem, sg_ready.this(i, 1))
                        pe.wait_ge(ta_ready.sem, ta_ready.this(i, 1))
                        pe.matmul(bk[3][:, :], sg[:, 0, :], wug0[:, :], start=True, stop=False)
                        pe.matmul(bk[3][:, :], sg[0:GLORA - P, 1, :], wug1[:, :], start=False,
                                  stop=True).then_inc(g_done.sem, 1)
                    elif step == "A2v":
                        pe.wait_ge(gate_ready.sem, gate_ready.this(i, 1))
                        for j in range(WT):
                            mm = pe.transpose(bk[3][:, j * P:(j + 1) * P], v_[:, j, :], ident[:, :])
                        mm.then_inc(tr_done.sem, 1)
                    elif step == "A2b":
                        pe.wait_ge(ssm_ready.sem, ssm_ready.this(i, 1))
                        pe.wait_ge(pr_ready.sem, pr_ready.this(i, 1))
                        for j in range(WT):
                            mm = pe.matmul(bk[2][:, 16 + 2 * j:18 + 2 * j], f["pr"][:, j, :], per["headcol"][:, :],
                                           start=True, stop=True)
                        mm.then_inc(bonus_done.sem, 1)
                    elif step == "A2c":
                        pe.wait_ge(rn_ready.sem, rn_ready.this(i, 1))
                        pe.wait_ge(bon_ready.sem, bon_ready.this(i, 1))
                        pe.transpose(bk[2][0:NH, P:2 * P], rn[:, :], ident[:, :]).then_inc(rnt_done.sem, 1)
                    elif step == "A2d":
                        pe.wait_ge(rnt_ready.sem, rnt_ready.this(i, 1))
                        for j in range(WT):
                            mm = pe.matmul(bk[2][:, j * P:(j + 1) * P], per["headrow"][0:NH, j * P:(j + 1) * P],
                                           rnt[:, :], start=True, stop=True)
                        mm.then_inc(rnbc_done.sem, 1)
                    elif step in ("A3c", "A3d"):
                        n = int(step == "A3d")
                        pe.wait_ge(feats_ready.sem, feats_ready.this(i, 1))
                        if n:
                            pe.wait_ge(tr_ready.sem, tr_ready.this(i, 1))
                        for j in range(WT):
                            mm = pe.transpose(bk[2 + n][:, j * P:(j + 1) * P], f[("bt", "zt")[n]][:, j, :], ident[:, :])
                        mm.then_inc(tr_done.sem, 1)
                    elif step[0] == "S":
                        s = int(step[1])
                        if s == 0:
                            pe.wait_ge(pad_ready.sem, pad_ready.this(i, 1))
                            pe.wait_ge(tw_upd.sem, tw_upd.last(i, NINV))
                        for h in (2 * s, 2 * s + 1):
                            q, j = h % 2, h // 2
                            if h >= 2:
                                pe.wait_ge(score_ready.sem, score_ready.this(i, h - 1))
                            for n in range(2):
                                mm = pe.matmul(bk[6 + q][:, n * 2 * P:(n + 1) * 2 * P], padded[:, n, q, j, :],
                                               kr[p][:, j, :, :], start=True, stop=True)
                            mm.then_inc(score_done.sem, 1)
                    elif step == "T2":
                        pe.wait_ge(w2_ready.sem, w2_ready.this(i, 1))
                        pe.wait_ge(gt_ready.sem, gt_ready.last(i, NINV))
                        for a in range(2):
                            for h in range(4):
                                mm = pe.transpose(bk[4 + a][:, h * P:(h + 1) * P], wm[p][:, 4 * a + h, :], ident[:, :])
                            mm.then_inc(t2_done.sem, 1)
                    elif step == "G0":
                        grow(i, p, 0)
                        grow(i, p, 1)
                    elif step[:3] == "inv":
                        n = int(step[3:])
                        lv, tw = n // QN, tw_banks[n % QN]
                        pe.wait_ge(gt_ready.sem, gt_ready.this(i, n + 1))
                        if n == 2:
                            pe.wait_ge(x_ready.sem, x_ready.last(i, 2))
                            pe.wait_ge(u_ready.sem, u_ready.last(i, 2))
                        for m in range(QH):
                            h = n % QN * QH + m
                            if lv < LEVELS - 1:
                                pe.matmul(tw[:, m * P:(m + 1) * P], wm[p][:, h, :], gt[:, h, :], start=True, stop=True)
                            mm = pe.matmul(tw[:, (QH + m) * P:(QH + m + 1) * P], gt[:, h, :], wm[p][:, h, :],
                                           start=True, stop=True)
                        mm.then_inc(tgt_done.sem, 1)
                        if n + 2 < NINV:
                            grow(i, p, n + 2)

                def back(step, i, p):
                    c = int(step[1]) if step[0] in "XUD" else 0
                    rows = slice(C * c, C * c + C)
                    if step[0] == "X":
                        if c == 0:
                            pe.wait_ge(x_ready.sem, x_ready.last(i, 2))
                            pe.wait_ge(tw_upd.sem, tw_upd.this(i, NINV))
                            for h in range(NH):
                                pe.matmul(bk[0][:, h * HD:(h + 1) * HD], sc[p][:, h, 2, :],
                                          v_t[p][:, h * HD:(h + 1) * HD], start=(h == 0), stop=False,
                                          skip_group_check=True)
                        pe.wait_ge(st_ready.sem, st_ready.this(i, 1) if c else st_ready.last(i, 2))
                        if c:
                            pe.wait_ge(x_ready.sem, x_ready.this(i, 1))
                        for j in range(WT):
                            mm = pe.matmul(bk[0][rows, j * P:(j + 1) * P], kr[p][:, j, 0, rows], st[:, c, j, :],
                                           start=False, stop=(j == WT - 1), skip_group_check=True)
                        mm.then_inc(x_done.sem, 1)
                        if c == 0:
                            pe.wait_ge(y_ready.sem, y_ready.last(i, 1))
                            if not (isinstance(i, int) and i == NT - 1):
                                pe.wait_ge(tr_ready.sem, tr_ready.this(i + 1, 3))
                        for j in range(WT):
                            pe.matmul(bk[3][rows, j * P:(j + 1) * P], kr[p][:, j, 1, rows], st[:, c, j, :],
                                      start=(j == 0), stop=False, skip_group_check=True)
                    elif step[0] == "U":
                        pe.wait_ge(tw_upd.sem, tw_upd.this(i, NINV))
                        pe.wait_ge(x_ready.sem, x_ready.this(i, c + 1))
                        pe.wait_ge(u_ready.sem, u_ready.this(i, 1) if c else u_ready.last(i, 2))
                        for h in range(NH):
                            mm = pe.matmul(bk[1][rows, h * HD:(h + 1) * HD], wm[p][:, h, rows],
                                           xn[:, h * HD:(h + 1) * HD], start=True, stop=True)
                        mm.then_inc(u_done.sem, 1)
                    elif step[0] == "D":
                        pe.wait_ge(u_ready.sem, u_ready.this(i, c + 1))
                        if c:
                            pe.wait_ge(st_ready.sem, st_ready.this(i, 1))
                        else:
                            pe.wait_ge(ada_ready.sem, ada_ready.last(i, 1))
                        for j in range(WT):
                            cols = slice(j * P, (j + 1) * P)
                            pe.matmul(bk[2][:, cols], bz_t[p][:, 0, c, cols], u[:, cols], start=True, stop=False)
                            mm = pe.matmul(bk[2][:, cols], bz_t[p][:, 1, c, cols], v_t[p][:, cols], start=False,
                                           stop=True)
                        mm.then_inc(dst_done.sem, 1)
                    elif step in ("Yv", "Yu"):
                        n, from_ = (3, v_t[p]) if step == "Yv" else (1, u)
                        for h in range(NH):
                            hs = slice(h * HD, (h + 1) * HD)
                            mm = pe.matmul(bk[3][:, hs], sc[p][:, h, n, :], from_[:, hs], start=False,
                                           stop=(n == 1 and h == NH - 1), skip_group_check=True)
                        if step == "Yu":
                            mm.then_inc(y_done.sem, 1)
                    elif step == "ADA":
                        pe.wait_ge(ada_loaded.sem, ada_loaded.this(i, 1))
                        pe.wait_ge(st_ready.sem, st_ready.this(i, 2))
                        for m in range(2):
                            for k in range(KT):
                                mm = pe.matmul(bk[2][:, m:m + 1], adas[:, k, m * P:(m + 1) * P],
                                               per["silc"][:, k:k + 1], start=(k == 0), stop=(k == KT - 1))
                        mm.then_inc(ada_done.sem, 1)

                run(pe, front, back)

            @block.scalar
            def _(act):
                for s in (th_ready, sgt_ready, tw_ready, ta_ready, sq_ready, e_ready, rnt_ready, tr_ready, t2_ready,
                          gt_ready, pad_ready, gate_ready, u_ready, y_ready, yq_ready):
                    s.credit(act)
                act.activation(hw0[:, :], vc[:, V_W0:V_W0 + WT], ACT.Copy, scale=0.5)
                act.activation(ha0[:, :], vc[:, V_A0:V_A0 + WT], ACT.Copy, scale=0.5)
                act.wait_ge(init_done, 1)

                def front(step, i, p):
                    if step == "A1a":
                        act.wait_ge(p_loaded.sem, p_loaded.this(i, 2))
                        act.wait_ge(zw_done.sem, zw_done.last(i, 1))
                        act.activation(th[:, :], pt[0:LORA, RT - 3, :], ACT.Tanh).then_inc(th_ready.sem, 1)
                        act.wait_ge(g_done.sem, g_done.last(i, 1))
                        act.activation(sg[:, 0, :], pt[:, RT - 2, :], ACT.Tanh, scale=0.5)
                        act.activation(sg[0:GLORA - P, 1, :], pt[0:GLORA - P, RT - 1, :], ACT.Tanh,
                                       scale=0.5).then_inc(sgt_ready.sem, 1)
                    elif step == "A1c":
                        act.wait_ge(kkr_ready.sem, kkr_ready.this(i, 1))
                        act.wait_ge(ss_done.sem, ss_done.last(i, 1))
                        act.activation(f["sq"][:, :, :], f["kkr"][:, :, :], ACT.Square).then_inc(sq_ready.sem, 1)
                        act.wait_ge(zw_done.sem, zw_done.this(i, 1))
                        act.wait_ge(l_ready.sem, l_ready.last(i, 1))
                        for j in range(WT):
                            ev = act.activation(f["tw"][:, j, :], bk[2][:, j * P:(j + 1) * P], ACT.Tanh, scale=0.5,
                                                bias=hw0[:, j:j + 1])
                        ev.then_inc(tw_ready.sem, 1)
                        act.wait_ge(za_done.sem, za_done.this(i, 1))
                        act.wait_ge(feats_ready.sem, feats_ready.last(i, 1))
                        for j in range(WT):
                            ev = act.activation(f["ta"][:, j, :], bk[3][:, j * P:(j + 1) * P], ACT.Tanh, scale=0.5,
                                                bias=ha0[:, j:j + 1])
                        ev.then_inc(ta_ready.sem, 1)
                    elif step == "A2a":
                        act.wait_ge(l_ready.sem, l_ready.this(i, 1))
                        wait_two_before(act, st_ready, i, 2)
                        act.activation(e1[p][:, :, :], f["lc"][:, :, :], ACT.Exp)
                    elif step == "A2f":
                        act.activation(f["e2"][:, :, :], f["lc"][:, :, :], ACT.Exp, scale=-1.0)
                        act.activation(f["e1x"][:, :, :], f["lx"][:, :, :], ACT.Exp).then_inc(e_ready.sem, 1)
                    elif step == "A2g":
                        wait_two_before(act, yo_ready, i, 1)
                        act.wait_ge(g_done.sem, g_done.this(i, 1))
                        act.copy(gate[p][:, :], bk[3][:, :]).then_inc(gate_ready.sem, 1)
                    elif step == "A2b":
                        wait_two_before(act, y_done, i, 1)
                        act.wait_ge(tr_done.sem, tr_done.this(i, 1))
                        act.copy(v_t[p][:, :], bk[3][:, :]).then_inc(tr_ready.sem, 1)
                    elif step == "A2c":
                        act.wait_ge(rnt_done.sem, rnt_done.this(i, 1))
                        act.wait_ge(rnbc_done.sem, rnbc_done.last(i, 1))
                        act.copy(rnt[:, :], bk[2][0:NH, P:2 * P]).then_inc(rnt_ready.sem, 1)
                    elif step == "A3e":
                        act.wait_ge(feats_ready.sem, feats_ready.this(i, 1))
                        act.wait_ge(score_done.sem, score_done.last(i, NH))
                        for n, name in ((0, "bt"), (1, "zt")):
                            for q in range(2):
                                ch = slice(HD * q, HD * q + HD)
                                ev = act.copy(padded[ch, n, q, :, :], f[name][ch, :, :])
                        ev.then_inc(pad_ready.sem, 1)
                    elif step == "A3d":
                        for n in range(2):
                            act.wait_ge(tr_done.sem, tr_done.this(i, n + 2))
                            for c in range(2):
                                tok = slice(C * c, C * c + C)
                                ev = act.copy(bz_t[p][tok, n, c, :], bk[2 + n][tok, :])
                            ev.then_inc(tr_ready.sem, 1)
                    elif step == "T2":
                        for a in range(2):
                            act.wait_ge(t2_done.sem, t2_done.this(i, a + 1))
                            act.copy(tm[:, 4 * a:4 * a + 4, :], bk[4 + a][:, :].rearrange("p (h n) -> p h n", h=4)
                                     ).then_inc(t2_ready.sem, 1)
                    elif step[:3] == "inv":
                        n = int(step[3:])
                        for m in (0, 1, 2) if n == 0 else (n + 2,) if n + 2 < NINV else ():
                            hs = slice(m % QN * QH, (m % QN + 1) * QH)
                            act.wait_ge(gt_done.sem, gt_done.this(i, m + 1))
                            act.wait_ge(tgt_done.sem, tgt_done.this(i, m + 1 - QN) if m >= QN
                                        else tgt_done.last(i, NINV + m + 1 - QN))
                            act.copy(gt[:, hs, :], bk[4 + m % 2][:, 0:QH * P].rearrange("p (h n) -> p h n", h=QH)
                                     ).then_inc(gt_ready.sem, 1)

                def back(step, i, p):
                    if step[0] == "U":
                        c = int(step[1])
                        rows = slice(C * c, C * c + C)
                        act.wait_ge(u_done.sem, u_done.this(i, c + 1))
                        act.wait_ge(y_done.sem, y_done.last(i, 1))
                        act.copy(u[rows, :], bk[1][rows, :]).then_inc(u_ready.sem, 1)
                    elif step == "Yu":
                        act.wait_ge(y_done.sem, y_done.this(i, 1))
                        act.wait_ge(yo_ready.sem, yo_ready.last(i, 1))
                        act.copy(y[:, :], bk[3][:, :]).then_inc(y_ready.sem, 1)
                    elif step == "OUT1":
                        act.wait_ge(yc_ready.sem, yc_ready.this(i, 1))
                        act.activation(yq[:, :], y[:, :], ACT.Square, scale=HD ** -0.5).then_inc(yq_ready.sem, 1)

                run(act, front, back)

            @block.vector
            def _(dve):
                for s in (sg_ready, kkr_ready, l_ready, kp_ready, ssm_ready, feats_ready, bon_ready,
                          score_ready, w2_ready, tw_upd, x_ready, st_ready, yc_ready, var_ready, ada_ready):
                    s.credit(dve)
                dve.wait_ge(once_loaded, 16 * 6)
                dve.wait_ge(init_done, 1)
                tt = dve.tensor_tensor
                lvl = lambda m, n, heads: per[m][:, n, :].unsqueeze(1).to_broadcast([P, heads, P])
                flat = lambda a: a[:, :, :].rearrange("p j n -> p (j n)")

                def front(step, i, p):
                    if step == "A1a":
                        dve.wait_ge(p_loaded.sem, p_loaded.this(i, 2))
                        dve.wait_ge(sq_ready.sem, sq_ready.last(i, 1))
                        tt(f["kkr"][:, :, :], k_, col(V_KK), ALU.mult).then_inc(kkr_ready.sem, 1)
                        dve.wait_ge(sgt_ready.sem, sgt_ready.this(i, 1))
                        dve.tensor_scalar(sg[:, 0, :], sg[:, 0, :], 0.5, 0.5, ALU.mult, ALU.add)
                        dve.tensor_scalar(sg[0:GLORA - P, 1, :], sg[0:GLORA - P, 1, :], 0.5, 0.5, ALU.mult,
                                          ALU.add).then_inc(sg_ready.sem, 1)
                    elif step == "A2a":
                        dve.wait_ge(tw_ready.sem, tw_ready.this(i, 1))
                        dve.wait_ge(e_ready.sem, e_ready.last(i, 1))
                        dve.tensor_scalar(f["nlw"][:, :, :], f["tw"][:, :, :], 0.5 * LOGW, 0.5 * LOGW, ALU.mult,
                                          ALU.add)
                        dve.drain()
                        dve.tensor_tensor_scan(flat(f["lc"]), per["reset"][:, :], flat(f["nlw"]), 0.0, ALU.mult,
                                               ALU.add)
                        dve.wait_ge(ss_done.sem, ss_done.this(i, 1))
                        dve.wait_ge(rn_ready.sem, rn_ready.last(i, 1))
                        dve.tensor_scalar(ssm[:, :], bk[2][:, 0:NH], 1e-24, None, ALU.max).then_inc(ssm_ready.sem, 1)
                        dve.drain()
                        tt(f["lx"][:, :, :], f["lc"][:, :, :], f["nlw"][:, :, :], ALU.subtract
                           ).then_inc(l_ready.sem, 1)
                    elif step == "A2k":
                        dve.wait_ge(ta_ready.sem, ta_ready.this(i, 1))
                        dve.tensor_scalar(f["ta"][:, :, :], f["ta"][:, :, :], 0.5, 0.5, ALU.mult, ALU.add)
                        dve.drain()
                        dve.scalar_tensor_tensor(f["t1"][:, :, :], f["ta"][:, :, :], -1.0, col(V_KA), ALU.add,
                                                 ALU.mult)
                        dve.drain()
                        dve.wait_ge(pr_ready.sem, pr_ready.last(i, 1))
                        dve.scalar_tensor_tensor(f["kp"][:, :, :], f["t1"][:, :, :], 1.0, k_, ALU.add, ALU.mult
                                                 ).then_inc(kp_ready.sem, 1)
                    elif step == "A2b":
                        wait_two_before(dve, yo_ready, i, 1)
                        dve.wait_ge(bonus_done.sem, bonus_done.this(i, 1))
                        dve.tensor_copy(bon[p][:, :], bk[2][:, 16:16 + NH]).then_inc(bon_ready.sem, 1)
                    elif step == "A3a":
                        dve.wait_ge(e_ready.sem, e_ready.this(i, 1))
                        wait_two_before(dve, y_done, i, 1)
                        dve.wait_ge(tr_done.sem, tr_done.last(i, 3))
                        dve.wait_ge(pad_ready.sem, pad_ready.last(i, 1))
                        tt(kr[p][:, :, 1, :], r_, e1[p][:, :, :], ALU.mult)
                        tt(f["zt"][:, :, :], f["kp"][:, :, :], f["e2"][:, :, :], ALU.mult)
                    elif step == "A3b":
                        dve.wait_ge(rnbc_done.sem, rnbc_done.this(i, 1))
                        tt(f["kk"][:, :, :], f["kkr"][:, :, :], bk[2][:, :].rearrange("p (j n) -> p j n", j=WT),
                           ALU.mult)
                        dve.drain()
                        tt(f["bt"][:, :, :], f["kk"][:, :, :], f["ta"][:, :, :], ALU.mult)
                        tt(kr[p][:, :, 0, :], f["kk"][:, :, :], f["e1x"][:, :, :], ALU.mult)
                        dve.drain()
                        tt(f["bt"][:, :, :], f["bt"][:, :, :], f["e2"][:, :, :], ALU.mult
                           ).then_inc(feats_ready.sem, 1)
                    elif step[0] == "S":
                        if step == "S0":
                            dve.wait_ge(x_done.sem, x_done.last(i, 1))
                        for h in (2 * int(step[1]), 2 * int(step[1]) + 1):
                            dve.wait_ge(score_done.sem, score_done.this(i, h + 1))
                            tt(sc[p][:, h, :, :], bk[6 + h % 2][:, :].rearrange("p (n t) -> p n t", n=4),
                               per["smask"][:, :, :], ALU.mult).then_inc(score_ready.sem, 1)
                    elif step == "W2":
                        dve.drain()
                        tt(wm[p][:, :, :], sc[p][:, :, 0, :], lvl("wmask", 0, NH), ALU.mult)
                        dve.drain()
                        tt(wm[p][:, :, :], wm[p][:, :, :], ident[:, :].unsqueeze(1).to_broadcast([P, NH, P]),
                           ALU.add).then_inc(w2_ready.sem, 1)
                    elif step[:3] == "inv":
                        n = int(step[3:])
                        lv = n // QN
                        hs = slice(n % QN * QH, (n % QN + 1) * QH)
                        tw = tw_banks[n % QN][:, :].rearrange("p (x h n) -> p x h n", x=2, h=QH)
                        wait_apart(dve, tgt_done.sem, tgt_done.this(i, n + 1), dve_passed)
                        if lv < LEVELS - 1:
                            dve.copy_predicated(tm[:, hs, :], lvl("tmask", lv + 1, QH).bitcast(I32), tw[:, 0])
                        dve.copy_predicated(wm[p][:, hs, :], lvl("wmask", lv + 1, QH).bitcast(I32),
                                            tw[:, 1]).then_inc(tw_upd.sem, 1)

                def back(step, i, p):
                    c = int(step[1]) if step[0] in "XD" else 0
                    if step[0] == "X":
                        rows = slice(C * c, C * c + C)
                        dve.wait_ge(x_done.sem, x_done.this(i, c + 1))
                        dve.tensor_scalar(xn[rows, :], bk[0][rows, :], -1.0, None, ALU.mult).then_inc(x_ready.sem, 1)
                    elif step[0] == "D":
                        dve.wait_ge(dst_done.sem, dst_done.this(i, c + 1))
                        blocks = [slice(HD * q, HD * q + HD) for q in range(2)]
                        new = [st[b, 1 - c, :, b] for b in blocks]
                        for q, b in enumerate(blocks):
                            tt(new[q], st[b, c, :, b], bk[2][b, :].rearrange("p (j n) -> p j n", j=WT)[:, :, b],
                               ALU.add)
                        dve.drain()
                        for q, b in enumerate(blocks):
                            end = e1[p][b, :, C * c + C - 1:C * c + C].to_broadcast([HD, WT, HD])
                            ev = tt(new[q], new[q], end, ALU.mult)
                        ev.then_inc(st_ready.sem, 1)
                    elif step == "OUT1":
                        dve.wait_ge(y_ready.sem, y_ready.this(i, 1))
                        dve.tensor_reduce(gs[:, 0, :], h3(y[:, :]), AX.X, ALU.add)
                        dve.drain()
                        dve.tensor_scalar(gs[:, 0, :], gs[:, 0, :], 1.0 / HD, None, ALU.mult)
                        dve.drain()
                        tt(h3(y[:, :]), h3(y[:, :]), bc(gs[:, 0, :]), ALU.subtract).then_inc(yc_ready.sem, 1)
                    elif step == "OUT2":
                        dve.wait_ge(yq_ready.sem, yq_ready.this(i, 1))
                        dve.wait_ge(gr_ready.sem, gr_ready.last(i, 1))
                        dve.tensor_reduce(gs[:, 1, :], h3(yq[:, :]), AX.X, ALU.add)
                        dve.drain()
                        dve.tensor_scalar(gs[:, 1, :], gs[:, 1, :], GN_EPS, None, ALU.add).then_inc(var_ready.sem, 1)
                    elif step == "ADA":
                        at = (lambda x: x) if isinstance(i, int) else dve.snap
                        wait_apart(dve, ada_done.sem, ada_done.this(i, 1), dve_passed)
                        dve.tensor_tensor(per["mod2"][:, ds(at(i * 2), 2)], bk[2][:, 0:2],
                                          vc[:, ds(at(i * 2 + 16), 2)], ALU.add).then_inc(ada_ready.sem, 1)

                run(dve, front, back)


def block_fox(nc, io, per, dr):
    ident, oall = per["ident"], per["tiles"]
    KB = 512
    GQ = KB // P
    nb = [t // GQ + 1 for t in range(NT)]
    NSB, NB = 5, sum(nb)
    assert NB % NSB == 0
    first = [sum(nb[:t]) for t in range(NT + 1)]
    tile_of = [t for t in range(NT) for _ in range(nb[t])]
    blocks = [(G, j) for G in range(NG) for j in range(GQ * (G + 1))]
    NBL, LAG = len(blocks), 2
    NPT = LAG + 1
    gfirst = [blocks.index((G, 0)) for G in range(NG)] + [NBL]
    order = [("scores", n) for n in range(first[GQ])]

    def values_of(B):
        order.append(("values", B))
        if B - 1 in gfirst[1:]:
            order.append(("out", blocks[B - 1][0] - 1))

    for G in range(NG):
        ns = range(first[GQ * (G + 1)], first[min(GQ * (G + 2), NT)])
        bs = range(gfirst[G], gfirst[G + 1])
        for i in range(max(len(ns), len(bs))):
            if i * len(bs) // max(len(ns), len(bs)) < (i + 1) * len(bs) // max(len(ns), len(bs)):
                B = bs[0] + i * len(bs) // max(len(ns), len(bs))
                order.append(("turn", B))
                if B >= LAG:
                    values_of(B - LAG)
            if i < len(ns):
                order.append(("scores", ns[i]))
    for B in range(NBL - LAG, NBL):
        values_of(B)
    order.append(("out", NG - 1))
    uses = [(w, i) for w, i in order if w in ("turn", "out")]
    NU = len(uses)
    use = {wi: n for n, wi in enumerate(uses)}
    assert NU % 2 == 0
    with ExitStack() as ctx:
        sb = lambda n, s, d=F32: ctx.enter_context(nc.sbuf_tensor(n, s, d))
        sem = ctx.enter_context(stage_semaphores(nc))
        sig = lambda n, per_turn=1, step=1: Signal(sem(n), per_turn, step)
        k1, k2 = sb("a_k1", [P, 2, T], F32R), sb("a_k2", [P, 2, T], F32R)
        q1, q2 = sb("a_q1", [P, T], F32R), sb("a_q2", [P, T], F32R)
        va = sb("a_v", [P, 2, NT, P], F32R)
        lf = sb("a_lf", [P, NT * NH])
        e1, fneg = sb("a_e1", [P, NT * NH]), sb("a_fneg", [P, NT * NH])
        run = sb("a_run", [P, NT * NH])
        ft = sb("a_ft", [P, 2, P], F32R)
        dmask = sb("a_dmask", [P, P])
        dmask_r, ident_r = sb("a_dmask_r", [P, P], F32R), sb("a_ident_r", [P, P], F32R)
        prs = [sb(f"a_pr{i}", [P, GQ, KB * (NG - 1 + i)]) for i in range(2)]
        pr = lambda t, lo, hi: prs[t // GQ % 2][:, t % GQ, lo:hi]
        pth, ptl = sb("a_pth", [P, NPT, KB], F32R), sb("a_ptl", [P, NPT, KB], F32R)
        ot = sb("a_ot", [P, KB])
        osum = sb("a_osum", [P, GQ, HD])
        mx = sb("a_mx", [P, 4, 4])
        nmx = sb("a_nmx", [P, 2 * GQ])
        rs = sb("a_rs", [P, NT, 4])
        rsum, rinv = sb("a_rsum", [P, GQ]), sb("a_rinv", [P, GQ])
        sbk = [ctx.enter_context(nc.psum_tensor(f"a_s{i}", [P, 512], F32)) for i in range(NSB)]
        tbk = [ctx.enter_context(nc.psum_tensor(f"a_t{i}", [P, 512], F32)) for i in range(2)]
        obk = ctx.enter_context(nc.psum_tensor("a_o", [P, 512], F32))

        consts_ready = sem("a_consts_ready")
        lf_abs, lf_exp, lf_ln, lf_ready = sem("lf_abs"), sem("lf_exp"), sem("lf_ln"), sem("lf_ready")
        cum_done, fneg_ready, ft_done, fth_ready, ftl_ready = (
            sem(n) for n in ("cum_done", "fneg_ready", "ft_done", "fth_ready", "ftl_ready"))
        f_stored, mask_split = sem("f_stored"), sem("mask_split")
        kv_loaded = [sig(f"kv_loaded{v}", 6, 16) for v in range(2)]
        q_loaded = [sig(f"q_loaded{G}", 3, 16) for G in range(NG)]
        s_done, max_ready, exp_ready = sig("s_done", NB), sig("max_ready", NT), sig("exp_ready", NB)
        t_done, t_read = sig("t_done", NU), sig("t_read", NU)
        hi_ready, pv_done = sig("hi_ready", NBL), sig("pv_done", NBL)
        ot_ready = sig("ot_ready", NG)

        with nc.Block() as block:
            @block.sync
            def _(sp):
                for s in (*q_loaded, *kv_loaded):
                    s.credit(sp)
                sp.wait_ge(fth_ready, 1)
                sp.wait_ge(ftl_ready, 1)
                sp.dma_start(dr["fneg"].rearrange("c r n -> r c n"), ft[:, :, :].bitcast(F32)).then_inc(f_stored, 16)
                sp.wait_ge(f_stored, 16)
                sp.wait_ge(consts_ready, 4)
                fneg_of = dr["fneg"].rearrange("c (t h) n -> h c t n", h=NH)
                with sp.Fori(0, NH // 2) as u:
                    for v in range(2):
                        h = sp.snap(2 * u + v)
                        row = sp.snap(h * HD)
                        sp.wait_ge(pv_done.sem, pv_done.last(h, 1))
                        for dst, name in ((k1[0:HD, v, :], "kh"), (k1[HD:P, v, :], "kl"), (k2[0:HD, v, :], "kh")):
                            sp.dma_start(dst.bitcast(F32), dr[name][ds(row, HD), :]).then_inc(kv_loaded[v].sem, 16)
                        for c in range(2):
                            sp.dma_start(k2[HD + c:HD + c + 1, v, :].rearrange("o (t n) -> o t n", n=P).bitcast(F32),
                                         fneg_of[ds(h, 1), c, :, :]).then_inc(kv_loaded[v].sem, 16)
                        sp.dma_start(va[:, v, :, :].bitcast(F32), dr["v"][:, ds(row * 2, P)].rearrange("(t p) n -> p t n", p=P)
                                     ).then_inc(kv_loaded[v].sem, 16)
                        for G in range(NG):
                            sp.wait_ge(s_done.sem, s_done.last(h, first[GQ * (G + 1)]))
                            cs = slice(G * KB, (G + 1) * KB)
                            for dst, name in ((q1[0:HD, cs], "qh"), (q1[HD:P, cs], "qh"), (q2[0:HD, cs], "ql")):
                                sp.dma_start(dst.bitcast(F32), dr[name][ds(row, HD), cs]).then_inc(q_loaded[G].sem, 16)

            @block.gpsimd
            def _(pool):
                pool.memset(dmask[:, :], 0.0)
                pool.drain()
                pool.affine_select(out=dmask[:, :], in_=dmask[:, :], compare_op=ALU.is_ge, fill=NEG, base=0,
                                   pattern=[[-1, P]], channel_multiplier=1).then_inc(consts_ready, 1)
                pool.drain()
                pool.memset(k2[HD:P, :, :].bitcast(F32), 0.0).then_inc(consts_ready, 1)
                pool.drain()
                pool.memset(q2[HD:P, :].bitcast(F32), 0.0).then_inc(consts_ready, 1)
                pool.drain()
                pool.memset(q2[HD:HD + 2, :].bitcast(F32), 1.0).then_inc(consts_ready, 1)

            @block.tensor
            def _(pe):
                for s in (s_done, t_done, pv_done):
                    s.credit(pe)
                pe.wait_ge(lf_ready, 1)
                pe.matmul(sbk[0][:, 0:NT * NH], per["tri"][:, :], lf[:, :], start=True, stop=True)
                pe.matmul(sbk[1][:, 0:NT * NH], per["ones"][:, :], lf[:, :], start=True,
                          stop=True).then_inc(cum_done, 1)
                pe.wait_ge(fneg_ready, 1)
                pe.transpose(sbk[2][:, 0:P], fneg[:, :], ident[:, :]).then_inc(ft_done, 1)
                pe.wait_ge(consts_ready, 4)
                pe.wait_ge(ftl_ready, 1)
                pe.wait_ge(mask_split, 1)

                def scores(h, v, n):
                    t, b = tile_of[n], n - first[tile_of[n]]
                    if b == 0 and t % GQ == 0:
                        pe.wait_ge(q_loaded[t // GQ].sem, q_loaded[t // GQ].this(h, 3))
                    pe.wait_ge(exp_ready.sem, exp_ready.this(h, n - NSB + 1) if n >= NSB
                               else exp_ready.last(h, NB + n - NSB + 1))
                    width = min(KB, (t + 1) * P - b * KB)
                    out = sbk[n % NSB][:, 0:width]
                    pe.matmul(out, q1[:, t * P:(t + 1) * P], k1[:, v, b * KB:b * KB + width], start=True, stop=False,
                              skip_group_check=True)
                    mm = pe.matmul(out, q2[:, t * P:(t + 1) * P], k2[:, v, b * KB:b * KB + width], start=False,
                                   stop=(b < nb[t] - 1), skip_group_check=True)
                    if b == nb[t] - 1:
                        mm = pe.matmul(sbk[n % NSB][:, width - P:width], ident_r[:, :], dmask_r[:, :], start=False,
                                       stop=True, skip_group_check=True)
                    mm.then_inc(s_done.sem, 1)

                def bank_read(h, n):
                    pe.wait_ge(t_read.sem, t_read.this(h, n - 1) if n >= 2 else t_read.last(h, NU + n - 1))

                def turn(h, B):
                    G, j = blocks[B]
                    n = use["turn", B]
                    pe.wait_ge(exp_ready.sem, exp_ready.this(h, first[GQ * G + GQ - 1] + j // GQ + 1))
                    bank_read(h, n)
                    for m in range(max(0, j - GQ * G), GQ):
                        mm = pe.transpose(tbk[n % 2][:, m * P:(m + 1) * P],
                                          pr(GQ * G + m, j * P, (j + 1) * P), ident[:, :])
                    mm.then_inc(t_done.sem, 1)

                def values(h, v, B):
                    G, j = blocks[B]
                    lo = max(0, j - GQ * G) * P
                    if j == 0:
                        pe.wait_ge(ot_ready.sem, ot_ready.this(h, G))
                    pe.wait_ge(t_read.sem, t_read.this(h, use["turn", B] + 1))
                    pe.matmul(obk[:, lo:KB], va[:, v, j, :], pth[:, B % NPT, lo:KB], start=(j == 0), stop=False,
                              skip_group_check=True)
                    pe.matmul(obk[:, lo:KB], va[:, v, j, :], ptl[:, B % NPT, lo:KB], start=False,
                              stop=(B + 1 in gfirst), skip_group_check=True).then_inc(pv_done.sem, 1)

                def out(h, G):
                    n = use["out", G]
                    pe.wait_ge(ot_ready.sem, ot_ready.this(h, G + 1))
                    bank_read(h, n)
                    for m in range(GQ):
                        mm = pe.transpose(tbk[n % 2][:, m * P:(m + 1) * P], ot[:, m * P:(m + 1) * P], ident[:, :])
                    mm.then_inc(t_done.sem, 1)

                with pe.Fori(0, NH // 2) as u:
                    for v in range(2):
                        h = pe.snap(2 * u + v)
                        pe.wait_ge(kv_loaded[v].sem, kv_loaded[v].this(u, 6))
                        for what, n in order:
                            if what == "scores":
                                scores(h, v, n)
                            elif what == "turn":
                                turn(h, n)
                            elif what == "values":
                                values(h, v, n)
                            else:
                                out(h, n)

            @block.scalar
            def _(act):
                for s in (exp_ready, hi_ready, ot_ready):
                    s.credit(act)
                act.wait_ge(lf_abs, 1)
                act.activation(e1[:, :], e1[:, :], ACT.Exp, scale=-1.0).then_inc(lf_exp, 1)
                act.wait_ge(lf_exp, 1)
                act.activation(e1[:, :], e1[:, :], ACT.Ln, bias=per["ones"][:, 0:1]).then_inc(lf_ln, 1)
                act.wait_ge(ft_done, 1)
                act.copy(ft[:, 0, :], sbk[2][:, 0:P]).then_inc(fth_ready, 1)

                def exp(h, n):
                    t, b = tile_of[n], n - first[tile_of[n]]
                    if b == 0:
                        act.wait_ge(max_ready.sem, max_ready.this(h, t + 1))
                        if t % GQ == 0:
                            G = t // GQ
                            act.wait_ge(t_done.sem, t_done.this(h, use["turn", gfirst[G - 1] - 1] + 1) if G >= 2
                                        else t_done.last(h, use["turn", gfirst[G + 3] - 1] + 1))
                            act.wait_ge(t_read.sem, t_read.last(h, use["out", G] + 1))
                    width = min(KB, (t + 1) * P - b * KB)
                    s = t % (2 * GQ)
                    act.activation(pr(t, b * KB, b * KB + width), sbk[n % NSB][:, 0:width], ACT.Exp,
                                   bias=nmx[:, s:s + 1], accum_out=rs[:, t, b:b + 1]).then_inc(exp_ready.sem, 1)

                def hi(h, B):
                    G, j = blocks[B]
                    lo = max(0, j - GQ * G) * P
                    n = use["turn", B]
                    act.wait_ge(t_done.sem, t_done.this(h, n + 1))
                    act.wait_ge(pv_done.sem, pv_done.this(h, B + 1 - NPT) if B >= NPT
                                else pv_done.last(h, NBL + B + 1 - NPT))
                    act.copy(pth[:, B % NPT, lo:KB], tbk[n % 2][:, lo:KB]).then_inc(hi_ready.sem, 1)

                def out_copy(h, G):
                    act.wait_ge(pv_done.sem, pv_done.this(h, gfirst[G + 1]))
                    act.wait_ge(t_done.sem, t_done.this(h, use["out", G - 1] + 1) if G else t_done.last(h, NU))
                    act.copy(ot[:, :], obk[:, :]).then_inc(ot_ready.sem, 1)

                with act.Fori(0, NH) as h:
                    done = seen = 0
                    for what, n in order:
                        if what == "scores":
                            if n + 1 == first[GQ]:
                                while done <= n:
                                    exp(h, done)
                                    done += 1
                        elif what == "turn":
                            G, j = blocks[n]
                            while done <= first[GQ * G + GQ - 1] + j // GQ:
                                exp(h, done)
                                done += 1
                            if done < first[seen]:
                                exp(h, done)
                                done += 1
                            hi(h, n)
                        elif what == "values" and n + 1 in gfirst:
                            out_copy(h, blocks[n][0])
                        if what == "scores" and done < first[seen] and first[seen] - done > 3:
                            exp(h, done)
                            done += 1
                        if what == "scores":
                            seen = tile_of[n] + (n + 1 == first[tile_of[n] + 1])

            @block.vector
            def _(dve):
                for s in (max_ready, t_read):
                    s.credit(dve)
                fr = per["fraw"][:, :, :].rearrange("p t h -> p (t h)")
                dve.tensor_scalar(lf[:, :], fr, -1.0, None, ALU.mult)
                dve.drain()
                dve.tensor_tensor(e1[:, :], lf[:, :], fr, ALU.max).then_inc(lf_abs, 1)
                dve.drain()
                dve.tensor_scalar(lf[:, :], fr, 0.0, None, ALU.min)
                dve.drain()
                dve.wait_ge(lf_ln, 1)
                dve.tensor_tensor(lf[:, :], lf[:, :], e1[:, :], ALU.subtract).then_inc(lf_ready, 1)
                dve.wait_ge(cum_done, 1)
                dve.memset(run[:, 0:NH], 0.0)
                for t in range(1, NT):
                    dve.drain()
                    dve.tensor_tensor(run[:, t * NH:(t + 1) * NH], run[:, (t - 1) * NH:t * NH],
                                      sbk[1][:, (t - 1) * NH:t * NH], ALU.add)
                dve.drain()
                dve.scalar_tensor_tensor(fneg[:, :], sbk[0][:, 0:NT * NH], -1.0, run[:, :], ALU.mult,
                                         ALU.subtract).then_inc(fneg_ready, 1)
                dve.wait_ge(fth_ready, 1)
                dve.tensor_tensor(ft[:, 1, :], sbk[2][:, 0:P], ft[:, 0, :].bitcast(F32), ALU.subtract
                                  ).then_inc(ftl_ready, 1)
                dve.wait_ge(consts_ready, 4)
                dve.tensor_copy(dmask_r[:, :], dmask[:, :])
                dve.tensor_copy(ident_r[:, :], ident[:, :]).then_inc(mask_split, 1)

                def maximum(h, n):
                    t, b = tile_of[n], n - first[tile_of[n]]
                    width = min(KB, (t + 1) * P - b * KB)
                    dve.wait_ge(s_done.sem, s_done.this(h, n + 1))
                    if b < nb[t] - 1:
                        dve.tensor_reduce(mx[:, t % 4, b:b + 1], sbk[n % NSB][:, 0:width], AX.X, ALU.max)
                    else:
                        s = t % (2 * GQ)
                        if nb[t] == 1:
                            dve.wait_ge(exp_ready.sem, exp_ready.last(h, first[NT + t - 7]))
                            dve.tensor_reduce(nmx[:, s:s + 1], sbk[n % NSB][:, 0:width], AX.X, ALU.max,
                                              negate=True).then_inc(max_ready.sem, 1)
                            return
                        dve.tensor_reduce(mx[:, t % 4, b:b + 1], sbk[n % NSB][:, 0:width], AX.X, ALU.max)
                        dve.drain()
                        dve.wait_ge(exp_ready.sem, exp_ready.this(h, first[t - 7]) if t >= 8
                                    else exp_ready.last(h, first[NT + t - 7]))
                        dve.tensor_reduce(nmx[:, s:s + 1], mx[:, t % 4, 0:nb[t]], AX.X, ALU.max,
                                          negate=True).then_inc(max_ready.sem, 1)

                def lo_part(h, B):
                    G, j = blocks[B]
                    lo = max(0, j - GQ * G) * P
                    dve.wait_ge(hi_ready.sem, hi_ready.this(h, B + 1))
                    dve.tensor_tensor(ptl[:, B % NPT, lo:KB], tbk[use["turn", B] % 2][:, lo:KB],
                                      pth[:, B % NPT, lo:KB].bitcast(F32), ALU.subtract).then_inc(t_read.sem, 1)

                def out(h, G):
                    n = use["out", G]
                    dve.tensor_reduce(rsum[:, :], rs[:, GQ * G:GQ * (G + 1), 0:G + 1], AX.X, ALU.add)
                    dve.drain()
                    dve.reciprocal(rinv[:, :], rsum[:, :])
                    dve.wait_ge(t_done.sem, t_done.this(h, n + 1))
                    both = tbk[n % 2][:, :].rearrange("p (t c d) -> p t c d", t=GQ, c=2)
                    dve.tensor_copy(osum[:, :, :], both[:, :, 0, :])
                    dve.drain()
                    dve.tensor_tensor(osum[:, :, :], osum[:, :, :], both[:, :, 1, :], ALU.add)
                    dve.drain()
                    dve.tensor_tensor(oall[:, GQ * G:GQ * (G + 1), ds(h * HD, HD)], osum[:, :, :],
                                      rinv[:, :].unsqueeze(2).to_broadcast([P, GQ, HD]),
                                      ALU.mult).then_inc(t_read.sem, 1)

                with dve.Fori(0, NH) as h:
                    low = 0
                    for what, n in order:
                        if what == "scores":
                            maximum(h, n)
                            continue
                        if what == "turn":
                            while low < n:
                                lo_part(h, low)
                                low += 1
                        elif what == "out":
                            while use.get(("turn", low), NU) < use["out", n]:
                                lo_part(h, low)
                                low += 1
                            out(h, n)
                        elif n >= NBL - LAG:
                            while low < NBL:
                                lo_part(h, low)
                                low += 1


def block_out_proj(nc, io, per, dr):
    ident, vc = per["ident"], per["vc"]
    oall = per["tiles"]
    with ExitStack() as ctx:
        sb = lambda n, s, d=F32: ctx.enter_context(nc.sbuf_tensor(n, s, d))
        sem = ctx.enter_context(stage_semaphores(nc))
        sig = lambda n, per_turn=1, step=1: Signal(sem(n), per_turn, step)
        raw = sb("o_raw", [P, 2, D])
        woh, wol = sb("o_woh", [P, KT, D], F32R), sb("o_wol", [P, KT, D], F32R)
        fg = sb("o_fg", [P, W])
        g1 = sb("o_g1", [P, D])
        gcol = sb("o_gcol", [P, 2, KT, P])
        yc = sb("o_yc", [P, D])
        og = sb("o_og", [P, W])
        sg = sb("o_sg", [P, W])
        xt = sb("o_xt", [P, D])
        fq = sb("o_fq", [P, W])
        fs, fr = sb("o_fs", [P, NH]), sb("o_fr", [P, NH])
        yth, ytl = ([sb(f"o_{n}{p}", [P, KT, P], F32R) for p in range(2)] for n in ("yth", "ytl"))
        h2 = sb("o_h2", [P, D])
        junk = sb("o_junk", [P, D])
        xn = sb("o_xn", [P, D])
        u2 = sb("o_u2", [P, KT, P])
        hs, hr = sb("o_hs", [P, 1]), sb("o_hr", [P, 1])
        bk = [ctx.enter_context(nc.psum_tensor(f"o_b{i}", [P, 512], F32)) for i in range(8)]
        y_banks = (bk[2:4], bk[6:8])

        act_passed, sp_passed, dve_passed = sem("o_act_passed"), sem("o_sp_passed"), sem("o_dve_passed")
        fg_loaded, wo_hi, wo_split = sem("fg_loaded"), sem("wo_hi"), sem("wo_split")
        wo_loaded = [sem(f"wo_loaded{r}") for r in range(2)]
        gcol_ready, gbc_done, rows_ready = sem("gcol_ready"), sem("gbc_done"), sem("rows_ready")
        yr_loaded, og_loaded, x_loaded = (sig(n, 1, 16) for n in ("o_yr_loaded", "o_og_loaded", "o_x_loaded"))
        h2_stored, u2_stored = sig("h2_stored", 1, 16), sig("u2_stored", 1, 16)
        sg_ready, fq_ready, fs_ready, fr_ready = (sig(n) for n in ("o_sg_ready", "o_fq_ready", "o_fs_ready",
                                                                  "o_fr_ready"))
        yc_ready, yt_done, mm_done, h2_ready = sig("o_yc_ready"), sig("yt_done"), sig("o_mm_done", 2), sig("h2_ready")
        yth_ready, ytl_ready = sig("yth_ready"), sig("ytl_ready")
        hs_ready, hr_ready, xn_ready = sig("o_hs_ready"), sig("o_hr_ready"), sig("o_xn_ready")
        ut_done, ut_act, ut_dve = sig("o_ut_done"), sig("o_ut_act"), sig("o_ut_dve")
        h3 = lambda ap: ap.rearrange("p (h d) -> p h d", h=NH)
        bc = lambda ap: ap.unsqueeze(2).to_broadcast([P, NH, HD])

        TURN = (("turn", 1), ("second_half", 0), ("first_half", 1), ("gate", 2), ("residual", 0), ("norm", 0))

        def run(eng, front, back):
            def turn(tiles, p):
                for step, ahead in TURN:
                    if ahead < len(tiles):
                        (front if ahead else back)(step, tiles[ahead], (p + ahead) % 2)

            for step, t in (("gate", 0), ("turn", 0), ("first_half", 0), ("gate", 1)):
                front(step, t, t)
            with eng.Fori(0, NT // 2 - 1) as pair:
                t0 = eng.snap(2 * pair)
                t1, t2, t3 = (eng.snap(t0 + n) for n in (1, 2, 3))
                turn((t0, t1, t2), 0)
                turn((t1, t2, t3), 1)
            turn((NT - 2, NT - 1), 0)
            turn((NT - 1,), 1)

        def tokens(eng, t):
            return ds(t * P if isinstance(t, int) else eng.snap(t * P), P)

        with nc.Block() as block:
            @block.sync
            def _(sp):
                for s in (yr_loaded, og_loaded, x_loaded):
                    s.credit(sp)
                sp.dma_start(fg[:, :], io["fox_out_g"].partition_broadcast(P)).then_inc(fg_loaded, 16)
                for k in range(KT):
                    if k >= 2:
                        sp.wait_ge(wo_split, k - 1)
                    sp.dma_start(raw[:, k % 2, :], io["w_o"][k * P:(k + 1) * P, :]).then_inc(wo_loaded[k % 2], 16)

                def front(step, t, p):
                    if step == "gate":
                        rows = tokens(sp, t)
                        wait_apart(sp, sg_ready.sem, sg_ready.last(t, 1), sp_passed)
                        sp.dma_start(og[:, :], dr["og"][rows, :]).then_inc(og_loaded.sem, 16)
                        wait_apart(sp, yt_done.sem, yt_done.last(t, 1), sp_passed)
                        sp.dma_start(yc[:, 0:W], dr["yrw"][rows, :]).then_inc(yr_loaded.sem, 16)

                def back(step, t, p):
                    if step == "second_half":
                        rows = tokens(sp, t)
                        wait_apart(sp, h2_ready.sem, h2_ready.last(t, 1), sp_passed)
                        sp.dma_start(xt[:, :], io["x"][0, rows, :]).then_inc(x_loaded.sem, 16)

                run(sp, front, back)

            @block.gpsimd
            def _(pool):
                fr_ready.credit(pool)
                hr_ready.credit(pool)

                def front(step, t, p):
                    if step == "gate":
                        pool.wait_ge(fs_ready.sem, fs_ready.this(t, 1))
                        pool.tensor_tensor(fr[:, :], fs[:, :], per["eps"][:, :], ALU.add)
                        pool.drain()
                        pool.tensor_tensor(fr[:, :], fr[:, :], per["mhalf"][:, :], ALU.pow).then_inc(fr_ready.sem, 1)

                def back(step, t, p):
                    if step == "residual":
                        pool.wait_ge(hs_ready.sem, hs_ready.this(t, 1))
                        pool.tensor_tensor(hr[:, :], hs[:, :], per["eps"][:, 0:1], ALU.add)
                        pool.drain()
                        pool.tensor_tensor(hr[:, :], hr[:, :], per["mhalf"][:, 0:1], ALU.pow
                                           ).then_inc(hr_ready.sem, 1)

                run(pool, front, back)

            @block.tensor
            def _(pe):
                for s in (yt_done, mm_done, ut_done):
                    s.credit(pe)
                pe.wait_ge(gcol_ready, 1)
                for n in range(2):
                    for k in range(KT):
                        mm = pe.matmul(bk[2 * n + k // 4][:, (k % 4) * P:(k % 4 + 1) * P], gcol[:, n, k, :],
                                       ident[:, :], start=True, stop=True)
                mm.then_inc(gbc_done, 1)
                pe.wait_ge(rows_ready, 1)

                def product(n, p):
                    for k in range(KT):
                        cs = slice(n * 512, (n + 1) * 512)
                        out = y_banks[p][n][:, :]
                        pe.matmul(out, yth[p][:, k, :], woh[:, k, cs], start=(k == 0), stop=False)
                        pe.matmul(out, yth[p][:, k, :], wol[:, k, cs], start=False, stop=False)
                        mm = pe.matmul(out, ytl[p][:, k, :], woh[:, k, cs], start=False, stop=(k == KT - 1))
                    mm.then_inc(mm_done.sem, 1)

                def front(step, t, p):
                    if step == "turn":
                        pe.wait_ge(yc_ready.sem, yc_ready.this(t, 1))
                        pe.wait_ge(ytl_ready.sem, ytl_ready.last(t, 1))
                        for k in range(KT):
                            mm = pe.transpose(bk[k // 4][:, (k % 4) * P:(k % 4 + 1) * P], yc[:, k * P:(k + 1) * P],
                                              ident[:, :])
                        mm.then_inc(yt_done.sem, 1)
                    elif step == "first_half":
                        if isinstance(t, int) and t == 0:
                            pe.wait_ge(wo_split, KT)
                        pe.wait_ge(ytl_ready.sem, ytl_ready.this(t, 1))
                        product(0, p)

                def back(step, t, p):
                    if step == "second_half":
                        product(1, p)
                    elif step == "norm":
                        pe.wait_ge(xn_ready.sem, xn_ready.this(t, 1))
                        pe.wait_ge(ut_act.sem, ut_act.last(t, 1))
                        pe.wait_ge(ut_dve.sem, ut_dve.last(t, 1))
                        for k in range(KT):
                            mm = pe.transpose(bk[4 + k // 4][:, (k % 4) * P:(k % 4 + 1) * P], xn[:, k * P:(k + 1) * P],
                                              ident[:, :])
                        mm.then_inc(ut_done.sem, 1)

                run(pe, front, back)

            @block.scalar
            def _(act):
                for s in (sg_ready, fq_ready, yth_ready, hs_ready, ut_act, h2_stored, u2_stored):
                    s.credit(act)
                for k in range(KT):
                    act.wait_ge(wo_loaded[k % 2], 16 * (k // 2 + 1))
                    act.copy(woh[:, k, :], raw[:, k % 2, :]).then_inc(wo_hi, 1)

                def front(step, t, p):
                    if step == "gate":
                        wait_apart(act, fs_ready.sem, fs_ready.last(t, 1), act_passed)
                        act.activation(fq[:, :].unsqueeze(1), oall[:, ds(t, 1), 0:W], ACT.Square,
                                       scale=HD ** -0.5).then_inc(fq_ready.sem, 1)
                        act.wait_ge(og_loaded.sem, og_loaded.this(t, 1))
                        act.wait_ge(yc_ready.sem, yc_ready.last(t, 1))
                        act.activation(sg[:, :], og[:, :], ACT.Tanh, scale=0.5).then_inc(sg_ready.sem, 1)
                    elif step == "turn":
                        act.wait_ge(yt_done.sem, yt_done.this(t, 1))
                        act.wait_ge(mm_done.sem, mm_done.last(t, 1))
                        for m in range(2):
                            ev = act.copy(yth[p][:, 4 * m:4 * m + 4, :], bk[m][:, :].rearrange("p (k n) -> p k n", k=4))
                        ev.then_inc(yth_ready.sem, 1)

                def back(step, t, p):
                    if step == "residual":
                        rows = tokens(act, t)
                        wait_apart(act, h2_ready.sem, h2_ready.this(t, 1), act_passed)
                        act.dma_start(dr["h2"][rows, :], h2[:, :]).then_inc(h2_stored.sem, 16)
                        act.wait_ge(hr_ready.sem, hr_ready.last(t, 1))
                        act.activation(junk[:, :], h2[:, :], ACT.Square, scale=D ** -0.5,
                                       accum_out=hs[:, :]).then_inc(hs_ready.sem, 1)
                    elif step == "norm":
                        act.wait_ge(u2_stored.sem, u2_stored.last(t, 1))
                        act.wait_ge(ut_done.sem, ut_done.this(t, 1))
                        for k in range(4):
                            ev = act.activation(u2[:, k, :], bk[4][:, k * P:(k + 1) * P], ACT.Identity,
                                                bias=per["mod2"][:, 8 + k:9 + k], scale=per["nscale2"][:, k:k + 1])
                        ev.then_inc(ut_act.sem, 1)
                        rows = tokens(act, t)
                        wait_apart(act, ut_act.sem, ut_act.this(t, 1), act_passed)
                        wait_apart(act, ut_dve.sem, ut_dve.this(t, 1), act_passed)
                        act.dma_start(dr["u2t"][:, rows].rearrange("(k p) n -> p k n", p=P), u2[:, :, :]
                                      ).then_inc(u2_stored.sem, 16)

                run(act, front, back)
                act.wait_ge(h2_stored.sem, h2_stored.this(NT - 1, 1))
                act.wait_ge(u2_stored.sem, u2_stored.this(NT - 1, 1))

            @block.vector
            def _(dve):
                for s in (fs_ready, yc_ready, ytl_ready, h2_ready, xn_ready, ut_dve):
                    s.credit(dve)
                tt = dve.tensor_tensor
                dve.scalar_tensor_tensor(per["nscale2"][:, :], per["mod2"][:, 16:24], 1.0, vc[:, V_G2:V_G2 + 8],
                                         ALU.add, ALU.mult)
                for n, at in ((0, 0), (1, 24)):
                    dve.tensor_copy(gcol[:, n, :, :], per["mod2"][:, at:at + 8].unsqueeze(2).to_broadcast(
                        [P, KT, P]))
                    dve.drain()
                dve.sem_inc(gcol_ready, 1)
                dve.wait_ge(gbc_done, 1)
                for n, dst in ((0, g1[:, :]), (1, per["g2row"][:, :])):
                    for m in range(2):
                        dve.tensor_copy(dst[:, m * 512:(m + 1) * 512], bk[2 * n + m][:, :])
                dve.drain()
                dve.sem_inc(rows_ready, 1)
                for k in range(KT):
                    dve.wait_ge(wo_hi, k + 1)
                    tt(wol[:, k, :], raw[:, k % 2, :], woh[:, k, :].bitcast(F32), ALU.subtract).then_inc(wo_split, 1)
                dve.wait_ge(fg_loaded, 16)

                def front(step, t, p):
                    if step == "gate":
                        dve.wait_ge(fq_ready.sem, fq_ready.this(t, 1))
                        dve.wait_ge(fr_ready.sem, fr_ready.last(t, 1))
                        dve.tensor_reduce(fs[:, :], h3(fq[:, :]), AX.X, ALU.add).then_inc(fs_ready.sem, 1)
                        dve.wait_ge(sg_ready.sem, sg_ready.this(t, 1))
                        dve.tensor_scalar(sg[:, :], sg[:, :], 0.5, 0.5, ALU.mult, ALU.add)
                        dve.drain()
                        tt(sg[:, :], sg[:, :], fg[:, :], ALU.mult)
                        dve.wait_ge(fr_ready.sem, fr_ready.this(t, 1))
                        wait_apart(dve, yt_done.sem, yt_done.last(t, 1), dve_passed)
                        tt(h3(yc[:, W:D]), oall[:, ds(t, 1), 0:W].rearrange("p o (h d) -> p (o h) d", h=NH),
                           bc(fr[:, :]), ALU.mult)
                        dve.drain()
                        dve.wait_ge(yr_loaded.sem, yr_loaded.this(t, 1))
                        tt(yc[:, W:D], yc[:, W:D], sg[:, :], ALU.mult).then_inc(yc_ready.sem, 1)
                    elif step == "turn":
                        dve.wait_ge(yth_ready.sem, yth_ready.this(t, 1))
                        for m in range(2):
                            part = slice(4 * m, 4 * m + 4)
                            ev = tt(ytl[p][:, part, :], bk[m][:, :].rearrange("p (k n) -> p k n", k=4),
                                    yth[p][:, part, :].bitcast(F32), ALU.subtract)
                        ev.then_inc(ytl_ready.sem, 1)

                def back(step, t, p):
                    if step == "residual":
                        dve.wait_ge(h2_stored.sem, h2_stored.last(t, 1))
                        dve.wait_ge(hs_ready.sem, hs_ready.last(t, 1))
                        for n in range(2):
                            dve.wait_ge(mm_done.sem, mm_done.this(t, n + 1))
                            cs = slice(n * 512, (n + 1) * 512)
                            tt(h2[:, cs], y_banks[p][n][:, :], g1[:, cs], ALU.mult)
                        dve.drain()
                        dve.wait_ge(x_loaded.sem, x_loaded.this(t, 1))
                        tt(h2[:, :], h2[:, :], xt[:, :], ALU.add).then_inc(h2_ready.sem, 1)
                    elif step == "norm":
                        dve.drain()
                        dve.wait_ge(hr_ready.sem, hr_ready.this(t, 1))
                        dve.wait_ge(ut_done.sem, ut_done.last(t, 1))
                        dve.tensor_scalar(xn[:, :], h2[:, :], hr[:, 0:1], None, ALU.mult).then_inc(xn_ready.sem, 1)
                        dve.wait_ge(u2_stored.sem, u2_stored.last(t, 1))
                        dve.wait_ge(ut_done.sem, ut_done.this(t, 1))
                        for k in range(4, 8):
                            ev = dve.tensor_scalar(u2[:, k, :], bk[5][:, (k - 4) * P:(k - 3) * P],
                                                   per["nscale2"][:, k:k + 1], per["mod2"][:, 8 + k:9 + k],
                                                   ALU.mult, ALU.add)
                        ev.then_inc(ut_dve.sem, 1)

                run(dve, front, back)


def block_mlp(nc, io, per, dr):
    FC = 256
    CW = KT * FC
    N1, N2 = FF // FC, FF // 512
    FT, FH = FF // P, FC // P
    NW = N1 + 2 * N2
    CH, AHEAD = NW + 2, 4
    HR, PB = 3, 4
    assert CH % 2 == 0
    with ExitStack() as ctx:
        sb = lambda n, s, d=F32: ctx.enter_context(nc.sbuf_tensor(n, s, d))
        sem = ctx.enter_context(stage_semaphores(nc))
        sig = lambda n, per_turn=1, step=1: Signal(sem(n), per_turn, step)
        raw = sb("m_raw", [P, 2, CW])
        wh, wl = sb("m_wh", [P, 2, CW], F32R), sb("m_wl", [P, 2, CW], F32R)
        uh, ul = sb("m_uh", [P, KT, GT], F32R), sb("m_ul", [P, KT, GT], F32R)
        hid = sb("m_hid", [P, FT, GT])
        hh, hl = sb("m_hh", [P, HR, GT], F32R), sb("m_hl", [P, HR, GT], F32R)
        rl = sb("m_rl", [P, PB, GT])
        h3 = sb("m_h3", [P, GS, D])
        tmp = sb("m_tmp", [P, 2, 512])
        junk = sb("m_junk", [P, D])
        fgr = sb("m_fgr", [P, D])
        hs, hr = sb("m_hs", [P, GS]), sb("m_hr", [P, GS])
        bk = [ctx.enter_context(nc.psum_tensor(f"m_b{i}", [P, 512], F32)) for i in range(8)]
        down_banks = ([bk[2], bk[3], bk[0], bk[1]], bk[4:8])
        fg_loaded, sp_passed = sem("m_fg_loaded"), sem("m_sp_passed")
        raw_loaded = [sig(f"raw_loaded{r}", CH // 2, 16) for r in range(2)]
        w_hi, w_split = sig("w_hi", CH), sig("w_split", CH)
        h2_loaded, out_stored = sig("m_h2_loaded", 1, 16), sig("out_stored", GS, 16)
        up_done, rl_ready, hid_ready = sig("up_done", FT), sig("rl_ready", FT), sig("hid_ready", FT)
        hid_hi, hid_split, hid_used = sig("hid_hi", 2 * FT), sig("hid_split", 2 * FT), sig("hid_used", 2 * FT)
        down_ev = sig("down_ev", 2)
        hs_ready, hr_ready, out_ready = sig("m_hs_ready", GS), sig("m_hr_ready", GS), sig("m_out_ready", GS)

        def split_slots(L):
            if L % CH in (NW - 2, NW - 1):
                i = L % CH - (NW - 2)
                return tuple(u[:, 4 * i:4 * i + 4, :].rearrange("p k n -> p (k n)") for u in (uh, ul))
            return wh[:, L % 2, :], wl[:, L % 2, :]

        def splits_of(c):
            return (c,) if c < NW - 2 else (NW - 2, NW - 1) if c == NW - 2 else (NW,)

        def hidden_of(c):
            m = 4 * (c - N1)
            return range(m + 2 if m else 0, min(m + 6, 2 * FT))

        with nc.Block() as block:
            @block.sync
            def _(sp):
                raw_loaded[0].credit(sp, AHEAD // 2)
                raw_loaded[1].credit(sp, AHEAD // 2)
                h2_loaded.credit(sp)

                def load(g, L, group):
                    if L >= 2 - AHEAD:
                        wait_apart(sp, w_split.sem, w_split.this(g, L - 1), sp_passed)
                    slot = raw[:, L % 2, :]
                    if L % CH in (NW - 2, NW - 1):
                        i = L % CH - (NW - 2)
                        src = dr["u2t"][i * 512:(i + 1) * 512, group].rearrange("(k p) n -> p k n", p=P)
                        slot = slot.rearrange("p (k n) -> p k n", k=4)
                    else:
                        c = (L + 2) % CH
                        if c < N1:
                            src = io["w_mlp1"][:, c * FC:(c + 1) * FC].rearrange("(k p) n -> p k n", p=P)
                            slot = slot.rearrange("p (k n) -> p k n", k=KT)
                        else:
                            half, m = divmod(c - N1, N2)
                            src = io["w_mlp2"][m * 512:(m + 1) * 512, half * 512:(half + 1) * 512].rearrange(
                                "(f p) n -> p f n", p=P)
                            slot = slot.rearrange("p (f n) -> p f n", f=4)
                    sp.dma_start(slot, src).then_inc(raw_loaded[L % 2].sem, 16)

                for L in range(-AHEAD, 0):
                    load(0, L, slice(0, GT))
                with sp.Fori(0, NG) as g:
                    t0 = sp.snap(g * GT)
                    t1 = sp.snap((g + 1) % NG * GT)
                    for L in range(CH):
                        load(g, L, ds(t1, GT))
                        if L == N1:
                            wait_apart(sp, out_stored.sem, out_stored.last(g, GS), sp_passed)
                            sp.dma_start(h3[:, :, :], dr["h2"][ds(t0, GT), :].rearrange("(s p) n -> p s n", p=P)
                                         ).then_inc(h2_loaded.sem, 16)
                for r in raw_loaded:
                    sp.wait_ge(r.sem, r.this(NG - 1, CH // 2))

            @block.gpsimd
            def _(pool):
                hr_ready.credit(pool)
                with pool.Fori(0, NG) as g:
                    for s in range(GS):
                        pool.wait_ge(hs_ready.sem, hs_ready.this(g, s + 1))
                        pool.tensor_tensor(hr[:, s:s + 1], hs[:, s:s + 1], per["eps"][:, 0:1], ALU.add)
                        pool.drain()
                        pool.tensor_tensor(hr[:, s:s + 1], hr[:, s:s + 1], per["mhalf"][:, 0:1],
                                           ALU.pow).then_inc(hr_ready.sem, 1)

            @block.tensor
            def _(pe):
                up_done.credit(pe)
                hid_used.credit(pe)
                with pe.Fori(0, NG) as g:
                    for c in range(N1):
                        pe.wait_ge(w_split.sem, w_split.this(g, c - 1))
                        w1h, w1l = (w[:, c % 2, :].rearrange("p (k n) -> p k n", k=KT) for w in (wh, wl))
                        for m in range(FH):
                            f = c * FH + m
                            pe.wait_ge(rl_ready.sem, rl_ready.this(g, f + 1 - PB))
                            if f == 0:
                                pe.wait_ge(down_ev.sem, down_ev.last(g, 1))
                            cs = slice(m * P, (m + 1) * P)
                            for k in range(KT):
                                pe.matmul(bk[f % PB][:, :], w1h[:, k, cs], uh[:, k, :], start=(k == 0), stop=False)
                                pe.matmul(bk[f % PB][:, :], w1h[:, k, cs], ul[:, k, :], start=False, stop=False)
                                mm = pe.matmul(bk[f % PB][:, :], w1l[:, k, cs], uh[:, k, :], start=False,
                                               stop=(k == KT - 1))
                            mm.then_inc(up_done.sem, 1)
                    pe.wait_ge(rl_ready.sem, rl_ready.this(g, FT))
                    for half in range(2):
                        banks = down_banks[half]
                        if half:
                            pe.wait_ge(down_ev.sem, down_ev.last(g, 2))
                        for m in range(N2):
                            c = N1 + half * N2 + m
                            pe.wait_ge(w_split.sem, w_split.this(g, c - 1))
                            w2h, w2l = (w[:, c % 2, :].rearrange("p (f n) -> p f n", f=4) for w in (wh, wl))
                            for fi in range(4):
                                F = FT * half + 4 * m + fi
                                pe.wait_ge(hid_split.sem, hid_split.this(g, F + 1))
                                first, last = F % FT == 0, F % FT == FT - 1
                                for s in range(GS):
                                    cs = slice(s * P, (s + 1) * P)
                                    pe.matmul(banks[s][:, :], hh[:, F % HR, cs], w2h[:, fi, :], start=first, stop=False)
                                    pe.matmul(banks[s][:, :], hh[:, F % HR, cs], w2l[:, fi, :], start=False, stop=False)
                                    mm = pe.matmul(banks[s][:, :], hl[:, F % HR, cs], w2h[:, fi, :], start=False,
                                                   stop=last)
                                mm.then_inc(hid_used.sem, 1)

            @block.scalar
            def _(act):
                for s in (rl_ready, hid_hi, hs_ready, out_stored):
                    s.credit(act)
                w_hi.credit(act, AHEAD)
                act.dma_start(fgr[:, :], io["final_g"].partition_broadcast(P)).then_inc(fg_loaded, 16)

                def split(g, L):
                    act.wait_ge(raw_loaded[L % 2].sem, raw_loaded[L % 2].this(g, L // 2 + 1))
                    if L >= 0:
                        c = L if L < NW - 2 else N1 - 1 if L < NW else L - 2
                        if c < N1:
                            act.wait_ge(up_done.sem, up_done.this(g, FH * (c + 1)))
                        else:
                            act.wait_ge(hid_used.sem, hid_used.this(g, 4 * (c - N1 + 1)))
                    act.copy(split_slots(L)[0], raw[:, L % 2, :]).then_inc(w_hi.sem, 1)

                for L in range(-AHEAD, 0):
                    split(0, L)
                with act.Fori(0, NG) as g:
                    t0 = act.snap(g * GT)
                    ts = [act.snap(t0 + s * P) for s in range(GS)]
                    for c in range(NW):
                        for f in range(FH * c, FH * (c + 1)) if c < N1 else ():
                            act.wait_ge(up_done.sem, up_done.this(g, f + 1))
                            act.wait_ge(hid_ready.sem, hid_ready.this(g, f + 1 - PB))
                            act.activation(rl[:, f % PB, :], bk[f % PB][:, :], ACT.Relu).then_inc(rl_ready.sem, 1)
                        for F in hidden_of(c) if c >= N1 else ():
                            if F < FT:
                                act.wait_ge(hid_ready.sem, hid_ready.this(g, F + 1))
                            act.wait_ge(hid_used.sem, hid_used.this(g, F + 1 - HR))
                            act.copy(hh[:, F % HR, :], hid[:, F % FT, :]).then_inc(hid_hi.sem, 1)
                        for L in splits_of(c):
                            split(g, L)
                    split(g, NW + 1)
                    for s in range(GS):
                        act.drain()
                        if s == 0:
                            act.wait_ge(hr_ready.sem, hr_ready.last(g, GS))
                            act.wait_ge(down_ev.sem, down_ev.this(g, 2))
                        act.activation(junk[:, :], h3[:, s, :], ACT.Square, scale=D ** -0.5,
                                       accum_out=hs[:, s:s + 1]).then_inc(hs_ready.sem, 1)
                    for s in range(GS):
                        act.wait_ge(out_ready.sem, out_ready.this(g, s + 1))
                        act.dma_start(io["out"][0, ds(ts[s], P), :], h3[:, s, :]).then_inc(out_stored.sem, 16)
                act.wait_ge(out_stored.sem, out_stored.this(NG - 1, GS))

            @block.vector
            def _(dve):
                for s in (hid_ready, hid_split, down_ev, out_ready):
                    s.credit(dve)
                w_split.credit(dve, AHEAD)
                tt = dve.tensor_tensor

                def split(g, L):
                    hi, lo = split_slots(L)
                    dve.wait_ge(w_hi.sem, w_hi.this(g, L + 1))
                    tt(lo, raw[:, L % 2, :], hi.bitcast(F32), ALU.subtract).then_inc(w_split.sem, 1)

                def evict(g, half):
                    cs = slice(half * 512, (half + 1) * 512)
                    dve.wait_ge(hid_used.sem, hid_used.this(g, FT * (half + 1)))
                    for s in range(GS):
                        tt(tmp[:, s % 2, :], down_banks[half][s][:, :], per["g2row"][:, cs], ALU.mult)
                        dve.drain()
                        ev = tt(h3[:, s, cs], h3[:, s, cs], tmp[:, s % 2, :], ALU.add)
                    ev.then_inc(down_ev.sem, 1)

                for L in range(-AHEAD, 0):
                    split(0, L)
                dve.wait_ge(fg_loaded, 16)
                with dve.Fori(0, NG) as g:
                    for c in range(NW):
                        for f in range(FH * c, FH * (c + 1)) if c < N1 else ():
                            dve.wait_ge(rl_ready.sem, rl_ready.this(g, f + 1))
                            tt(hid[:, f, :], rl[:, f % PB, :], rl[:, f % PB, :], ALU.mult).then_inc(hid_ready.sem, 1)
                        for F in hidden_of(c) if c >= N1 else ():
                            if F < FT:
                                dve.wait_ge(hid_ready.sem, hid_ready.this(g, F + 1))
                            dve.wait_ge(hid_hi.sem, hid_hi.this(g, F + 1))
                            tt(hl[:, F % HR, :], hid[:, F % FT, :], hh[:, F % HR, :].bitcast(F32),
                               ALU.subtract).then_inc(hid_split.sem, 1)
                        for L in splits_of(c):
                            split(g, L)
                        if c == N1 + N2:
                            dve.wait_ge(h2_loaded.sem, h2_loaded.this(g, 1))
                            evict(g, 0)
                    split(g, NW + 1)
                    evict(g, 1)
                    for s in range(GS):
                        dve.wait_ge(hr_ready.sem, hr_ready.this(g, s + 1))
                        dve.scalar_tensor_tensor(h3[:, s, :], h3[:, s, :], hr[:, s:s + 1], fgr[:, :], ALU.mult,
                                                 ALU.mult).then_inc(out_ready.sem, 1)


KEPT = {"ident": [P, P], "ones": [P, P], "tri": [P, P], "vc": [P, V_N], "modc": [P, 16], "mod2": [P, 32],
        "nscale1": [P, 8], "nscale2": [P, 8], "silc": [P, 8], "omu": [P, RT], "fraw": [P, NT, NH], "eps": [P, 8],
        "mhalf": [P, 8]}
MASKS = {"smask": [P, 4, P], "tmask": [P, LEVELS + 1, P], "wmask": [P, LEVELS + 1, P], "headcol": [P, 2],
         "headrow": [P, W], "reset": [P, W]}
SCRATCH = {"prw": [RW, T], "og": [T, W], "yrw": [T, W], "h2": [T, D], "u2t": [D, T],
           "qh": [W, T], "ql": [W, T], "kh": [W, T], "kl": [W, T], "v": [T, 2 * W], "fneg": [2, P, P]}


_INS = ["x", "c", "w_ada", "b_ada", "norm1_g", "w_in", "mu_shift", "w0", "w_up_decay", "a0", "w_up_a", "w_up_g",
        "k_k", "k_a", "r_k", "gn_g", "gn_b", "b_f", "q_norm_g", "k_norm_g", "fox_out_g", "w_o", "norm2_g",
        "w_mlp1", "w_mlp2", "final_g"]


def build(nc, io):
    dr = {n: nc.dram_tensor(f"scratch_{n}", shape, F32, kind="Internal").ap() for n, shape in SCRATCH.items()}
    keep = lambda ctx, shapes: {n: ctx.enter_context(nc.sbuf_tensor(n, shape, F32)) for n, shape in shapes.items()}
    with ExitStack() as ctx:
        per = keep(ctx, KEPT)
        with ExitStack() as masks_ctx:
            masks = keep(masks_ctx, MASKS)
            block_constants(nc, io, {**per, **masks}, dr)
            block_project(nc, io, per, dr)
            block_rwkv(nc, io, {**per, **masks}, dr)
        per |= keep(ctx, {"g2row": [P, D]})
        with ExitStack() as tiles_ctx:
            tiles = keep(tiles_ctx, {"tiles": [P, NT, W]})
            block_fox(nc, io, {**per, **tiles}, dr)
            block_out_proj(nc, io, {**per, **tiles}, dr)
        block_mlp(nc, io, per, dr)


def kernel(**inputs):
    import numpy as np
    import concourse.bacc as bacc
    from concourse.bass_utils import run_bass_kernel_spmd

    nc = bacc.Bacc("TRN2", target_bir_lowering=False, num_devices=1)
    arrays, io = {}, {}
    for name in _INS:
        a = np.ascontiguousarray(inputs[name])
        arrays[f"in_{name}"] = a
        io[name] = nc.dram_tensor(f"in_{name}", a.shape, mybir.dt.from_np(a.dtype), kind="ExternalInput").ap()
    io["out"] = nc.dram_tensor("out", [1, T, D], F32, kind="ExternalOutput").ap()
    build(nc, io)
    r = run_bass_kernel_spmd(nc, [arrays], core_ids=[0])
    return r.results[0]["out"]
```
